# Optimizing a Trainium2 kernel written in Bass

```python
import math
import numpy as np
import jax, jax.numpy as jnp
from jax import lax

D_MODEL = 1024
BATCH = 1
SEQ = 256
DEPTH = 2

GRID_W = 64
MEM_LEN = 256
HEAD_DIM = 64
DA_HEADS = 4
DA_VDIM = 2 * HEAD_DIM
DA_QK = DA_HEADS * 2 * HEAD_DIM
DA_V = DA_HEADS * DA_VDIM
Q_BLOCK = 128
NA_HEADS = 8
NA_W = NA_HEADS * HEAD_DIM
NA_WIN_ROWS = 8
NA_WIN_COLS = 16
NA_QCOLS = 16
NA_KCOLS = 32
SC_W = 512
SC_K = 3
N_BRANCH = 3
BRANCH_W = 512
IN_SPLITS = (DA_QK, DA_QK, DA_V, NA_W, NA_W, NA_W, SC_W, SC_W, SC_W, N_BRANCH * D_MODEL)
IN_COLS = 7680
XA_HEADS = 4
XA_DIM = D_MODEL // XA_HEADS
D_FF = 2816
FFN_K = 3
ROPE_THETA = 10000.0
LN_EPS = 1e-5


def layer_norm(x, g, b):
    xf = x.astype(jnp.float32)
    mu = jnp.mean(xf, axis=-1, keepdims=True)
    var = jnp.mean(jnp.square(xf - mu), axis=-1, keepdims=True)
    y = (xf - mu) * lax.rsqrt(var + LN_EPS)
    return (y * g.astype(jnp.float32) + b.astype(jnp.float32)).astype(x.dtype)

def rms_norm(x, g):
    xf = x.astype(jnp.float32)
    y = xf * lax.rsqrt(jnp.mean(jnp.square(xf), axis=-1, keepdims=True) + LN_EPS)
    return (y * g.astype(jnp.float32)).astype(x.dtype)

def rope(x, pos):
    d = x.shape[-1]
    half = d // 2
    inv = ROPE_THETA ** (-jnp.arange(half, dtype=jnp.float32) * 2.0 / d)
    ang = pos.astype(jnp.float32)[:, None] * inv[None, :]
    cos = jnp.cos(ang).astype(x.dtype)
    sin = jnp.sin(ang).astype(x.dtype)
    x1, x2 = x[..., :half], x[..., half:]
    return jnp.concatenate([x1 * cos - x2 * sin, x2 * cos + x1 * sin], axis=-1)

def dwconv(x, w):
    k, c = w.shape
    return lax.conv_general_dilated(x, w[:, None, :], window_strides=(1,), padding=[(k // 2, k // 2)],
                                    dimension_numbers=('NWC', 'WIO', 'NWC'), feature_group_count=c)

def diff_attention(q, k, v, lam, pos):
    b, s = q.shape[0], q.shape[1]
    q = rope(q.transpose(0, 2, 3, 1, 4), pos) * (HEAD_DIM ** -0.5)
    k = rope(k.transpose(0, 2, 3, 1, 4), pos)
    vt = v.transpose(0, 2, 1, 3)
    nb = s // Q_BLOCK
    qb = q.reshape(b, DA_HEADS, 2, nb, Q_BLOCK, HEAD_DIM).transpose(3, 0, 1, 2, 4, 5)

    def block(qblk):
        sc = jnp.einsum('bhmqd,bhmkd->bhmqk', qblk, k, preferred_element_type=jnp.float32)
        p = jax.nn.softmax(sc, axis=-1)
        w = p[:, :, 0] - lam * p[:, :, 1]
        return jnp.einsum('bhqk,bhkv->bhqv', w.astype(vt.dtype), vt)

    o = lax.map(block, qb)
    return o.transpose(1, 2, 0, 3, 4).reshape(b, DA_HEADS, s, DA_VDIM)

def _na_static(rows):
    wr = min(NA_WIN_ROWS, rows)
    n_cb = GRID_W // NA_QCOLS
    c = np.arange(GRID_W).reshape(n_cb, NA_QCOLS)
    cs = np.clip(c - NA_WIN_COLS // 2, 0, GRID_W - NA_WIN_COLS)
    kstart = np.minimum(cs[:, 0], GRID_W - NA_KCOLS)
    kcol = kstart[:, None] + np.arange(NA_KCOLS)
    rel = kcol[:, None, :] - c[:, :, None]
    valid = (kcol[:, None, :] >= cs[:, :, None]) & (kcol[:, None, :] < cs[:, :, None] + NA_WIN_COLS)
    dc_idx = np.clip(rel + NA_WIN_COLS - 1, 0, 2 * NA_WIN_COLS - 2)
    return wr, n_cb, kcol.astype(np.int32), dc_idx.astype(np.int32), valid

def neighbourhood_attention(q, k, v, rpb):
    b, s = q.shape[0], q.shape[1]
    rows = s // GRID_W
    wr, n_cb, kcol, dc_idx, valid = _na_static(rows)

    def grid(t):
        return t.reshape(b, rows, GRID_W, NA_HEADS, HEAD_DIM).transpose(0, 3, 1, 2, 4)

    qg = grid(q) * (HEAD_DIM ** -0.5)
    kg = grid(k)
    vg = grid(v)
    qr = qg.reshape(b, NA_HEADS, rows, n_cb, NA_QCOLS, HEAD_DIM).transpose(2, 0, 1, 3, 4, 5)
    kcol_j = jnp.asarray(kcol)
    mask = jnp.asarray(valid)[:, :, None, :]
    bias_c = rpb[:, :, jnp.asarray(dc_idx)]

    def row_block(args):
        r, qblk = args
        rs = jnp.clip(r - wr // 2, 0, rows - wr)
        k_rows = lax.dynamic_slice_in_dim(kg, rs, wr, axis=2)
        v_rows = lax.dynamic_slice_in_dim(vg, rs, wr, axis=2)
        k_blk = jnp.take(k_rows, kcol_j, axis=3)
        v_blk = jnp.take(v_rows, kcol_j, axis=3)
        sc = jnp.einsum('bhjqd,bhrjkd->bhjqrk', qblk, k_blk, preferred_element_type=jnp.float32)
        dr_idx = rs + jnp.arange(wr) - r + (NA_WIN_ROWS - 1)
        bias = jnp.take(bias_c, dr_idx, axis=1).transpose(0, 2, 3, 1, 4)
        sc = jnp.where(mask, sc + bias[None].astype(jnp.float32), -jnp.inf)
        p = jax.nn.softmax(sc.reshape(sc.shape[:4] + (wr * NA_KCOLS,)), axis=-1).reshape(sc.shape)
        return jnp.einsum('bhjqrk,bhrjkd->bhjqd', p.astype(v_blk.dtype), v_blk)

    o = lax.map(row_block, (jnp.arange(rows, dtype=jnp.int32), qr))
    return o.transpose(1, 0, 3, 4, 2, 5).reshape(b, s, NA_W)

def hybrid_mixer(x, w_in, lam_q1, lam_k1, lam_q2, lam_k2, subln_g, rpb, sc_conv_w, w_branch, w_mix_out, lam_init, pos):
    b, s, _ = x.shape
    proj = x @ w_in
    qa, ka, va, qb, kb, vb, gb, gc, hc, gates = jnp.split(proj, np.cumsum(IN_SPLITS)[:-1].tolist(), axis=-1)
    lam = (jnp.exp(jnp.sum(lam_q1.astype(jnp.float32) * lam_k1.astype(jnp.float32)))
           - jnp.exp(jnp.sum(lam_q2.astype(jnp.float32) * lam_k2.astype(jnp.float32))) + lam_init)
    oa = diff_attention(qa.reshape(b, s, DA_HEADS, 2, HEAD_DIM), ka.reshape(b, s, DA_HEADS, 2, HEAD_DIM),
                        va.reshape(b, s, DA_HEADS, DA_VDIM), lam, pos)
    ya = (rms_norm(oa, subln_g) * (1.0 - lam_init)).transpose(0, 2, 1, 3).reshape(b, s, DA_V)
    yb = neighbourhood_attention(qb, kb, vb, rpb)
    yc = gb * dwconv(gc * hc, sc_conv_w)
    g = jax.nn.sigmoid(gates.reshape(b, s, N_BRANCH, D_MODEL))
    merged = (g[:, :, 0] * (ya @ w_branch[0]) + g[:, :, 1] * (yb @ w_branch[1])
              + g[:, :, 2] * (yc @ w_branch[2]))
    return merged @ w_mix_out

def memory_cross_attention(x, mem, xa_q, xa_kv, xa_o):
    b, s, _ = x.shape
    q = (x @ xa_q).reshape(b, s, XA_HEADS, XA_DIM) * (XA_DIM ** -0.5)
    k, v = jnp.split(mem @ xa_kv, 2, axis=-1)
    k = k.reshape(b, mem.shape[1], XA_HEADS, XA_DIM)
    v = v.reshape(b, mem.shape[1], XA_HEADS, XA_DIM)
    p = jax.nn.softmax(jnp.einsum('bqhd,bkhd->bhqk', q, k, preferred_element_type=jnp.float32), axis=-1)
    o = jnp.einsum('bhqk,bkhd->bqhd', p.astype(v.dtype), v).reshape(b, s, D_MODEL)
    return o @ xa_o

def conv_ffn(x, ffn_w_in, ffn_conv_w, ffn_conv_b, ffn_w_out):
    u, gt = jnp.split(x @ ffn_w_in, 2, axis=-1)
    a = dwconv(gt, ffn_conv_w) + ffn_conv_b
    return (jax.nn.silu(a) * u) @ ffn_w_out

def first_inputs(seed: int = 0) -> dict:
    key = jax.random.key(seed)
    ks = jax.random.split(key, 24)
    beta = (8.0 * DEPTH) ** -0.25

    def nrm(k, shape, scale):
        return jax.random.normal(k, shape, jnp.float32) * scale

    is_value = (False, False, True, False, False, True, False, False, True, False)
    col_scale = np.concatenate([np.full(n, beta if iv else 1.0, np.float32) for n, iv in zip(IN_SPLITS, is_value)])
    kv_scale = np.concatenate([np.ones(D_MODEL, np.float32), np.full(D_MODEL, beta, np.float32)])
    return {
        'x': nrm(ks[0], (BATCH, SEQ, D_MODEL), 1.0),
        'mem': nrm(ks[1], (BATCH, MEM_LEN, D_MODEL), 1.0),
        'emb_ln_g': 1.0 + nrm(ks[2], (D_MODEL,), 0.02),
        'emb_ln_b': nrm(ks[3], (D_MODEL,), 0.02),
        'w_in': nrm(ks[4], (DEPTH, D_MODEL, IN_COLS), D_MODEL ** -0.5) * jnp.asarray(col_scale),
        'lam_q1': nrm(ks[5], (DEPTH, HEAD_DIM), 0.1),
        'lam_k1': nrm(ks[6], (DEPTH, HEAD_DIM), 0.1),
        'lam_q2': nrm(ks[7], (DEPTH, HEAD_DIM), 0.1),
        'lam_k2': nrm(ks[8], (DEPTH, HEAD_DIM), 0.1),
        'subln_g': 1.0 + nrm(ks[9], (DEPTH, DA_VDIM), 0.02),
        'rpb': nrm(ks[10], (DEPTH, NA_HEADS, 2 * NA_WIN_ROWS - 1, 2 * NA_WIN_COLS - 1), 0.1),
        'sc_conv_w': nrm(ks[11], (DEPTH, SC_K, SC_W), SC_K ** -0.5),
        'w_branch': nrm(ks[12], (DEPTH, N_BRANCH, BRANCH_W, D_MODEL), BRANCH_W ** -0.5 * beta),
        'w_mix_out': nrm(ks[13], (DEPTH, D_MODEL, D_MODEL), D_MODEL ** -0.5 * beta),
        'xa_q': nrm(ks[14], (DEPTH, D_MODEL, D_MODEL), D_MODEL ** -0.5),
        'xa_kv': nrm(ks[15], (DEPTH, D_MODEL, 2 * D_MODEL), D_MODEL ** -0.5) * jnp.asarray(kv_scale),
        'xa_o': nrm(ks[16], (DEPTH, D_MODEL, D_MODEL), D_MODEL ** -0.5 * beta),
        'ffn_w_in': nrm(ks[17], (DEPTH, D_MODEL, 2 * D_FF), D_MODEL ** -0.5 * beta),
        'ffn_conv_w': nrm(ks[18], (DEPTH, FFN_K, D_FF), FFN_K ** -0.5),
        'ffn_conv_b': nrm(ks[19], (DEPTH, D_FF), 0.02),
        'ffn_w_out': nrm(ks[20], (DEPTH, D_FF, D_MODEL), D_FF ** -0.5 * beta),
        'ln_g': 1.0 + nrm(ks[21], (DEPTH, 3, D_MODEL), 0.02),
        'ln_b': nrm(ks[22], (DEPTH, 3, D_MODEL), 0.02),
    }

def first_block(x, mem, emb_ln_g, emb_ln_b, w_in, lam_q1, lam_k1, lam_q2, lam_k2, subln_g, rpb, sc_conv_w,
              w_branch, w_mix_out, xa_q, xa_kv, xa_o, ffn_w_in, ffn_conv_w, ffn_conv_b, ffn_w_out, ln_g, ln_b):
    alpha = (2.0 * DEPTH) ** 0.25
    pos = jnp.arange(x.shape[1], dtype=jnp.int32)
    x = layer_norm(x, emb_ln_g, emb_ln_b)
    for l in range(DEPTH):
        lam_init = 0.8 - 0.6 * math.exp(-0.3 * l)
        h = hybrid_mixer(x, w_in[l], lam_q1[l], lam_k1[l], lam_q2[l], lam_k2[l], subln_g[l], rpb[l],
                         sc_conv_w[l], w_branch[l], w_mix_out[l], lam_init, pos)
        x = layer_norm(alpha * x + h, ln_g[l, 0], ln_b[l, 0])
        h = memory_cross_attention(x, mem, xa_q[l], xa_kv[l], xa_o[l])
        x = layer_norm(alpha * x + h, ln_g[l, 1], ln_b[l, 1])
        h = conv_ffn(x, ffn_w_in[l], ffn_conv_w[l], ffn_conv_b[l], ffn_w_out[l])
        x = layer_norm(alpha * x + h, ln_g[l, 2], ln_b[l, 2])
    return x


DEPTH_2 = 1

N_MEM = 256
MAX_POS_OFFSET = 1024
BLOCK = 128
RMS_EPS = 1e-6
NEG_INF = -1e30

MLA_HEADS = 8
MLA_NOPE = 64
MLA_ROPE = 32
MLA_V = 64
MLA_QK_DIM = MLA_NOPE + MLA_ROPE
MLA_Q_RANK = 384
MLA_KV_RANK = 256
MLA_WIDTH = MLA_HEADS * MLA_V

DIL_PAIRS = ((128, 1), (512, 4), (2048, 16))
DIL_GROUPS = 3
DIL_HEADS_PER_GROUP = 4
DIL_HEADS = DIL_GROUPS * DIL_HEADS_PER_GROUP
DIL_HEAD_DIM = 128
DIL_WIDTH = DIL_HEADS_PER_GROUP * DIL_HEAD_DIM

MEM_HEADS = 4
MEM_HEAD_DIM = 128
MEM_WIDTH = MEM_HEADS * MEM_HEAD_DIM


CONV_WIDTH = 3

OFF_Q = MLA_Q_RANK
OFF_KV = OFF_Q + MLA_KV_RANK
OFF_KR = OFF_KV + MLA_ROPE
OFF_DIL = OFF_KR + 3 * DIL_HEADS * DIL_HEAD_DIM
OFF_MEMQ = OFF_DIL + MEM_WIDTH
D_IN = OFF_MEMQ + N_BRANCH * D_MODEL


def _rms_norm(x, g):
    xf = x.astype(jnp.float32)
    y = xf * lax.rsqrt(jnp.mean(xf * xf, axis=-1, keepdims=True) + RMS_EPS)
    return (y * g.astype(jnp.float32)).astype(x.dtype)

def _rope(t, positions):
    half = t.shape[-1] // 2
    inv_freq = ROPE_THETA ** (-jnp.arange(half, dtype=jnp.float32) / half)
    ang = positions.astype(jnp.float32)[:, :, None, None] * inv_freq
    cos, sin = jnp.cos(ang), jnp.sin(ang)
    t1 = t[..., :half].astype(jnp.float32)
    t2 = t[..., half:].astype(jnp.float32)
    return jnp.concatenate([t1 * cos - t2 * sin, t2 * cos + t1 * sin], axis=-1).astype(t.dtype)

def _alibi_slopes(n):
    return jnp.exp2(-8.0 * jnp.arange(1, n + 1, dtype=jnp.float32) / n)

def _mla(c_q, c_kv, k_rope, positions, q_norm, w_uq, kv_norm, w_ukv):
    B, S, _ = c_q.shape
    q = (_rms_norm(c_q, q_norm) @ w_uq).reshape(B, S, MLA_HEADS, MLA_QK_DIM)
    q = jnp.concatenate([q[..., :MLA_NOPE], _rope(q[..., MLA_NOPE:], positions)], axis=-1)
    kv = (_rms_norm(c_kv, kv_norm) @ w_ukv).reshape(B, S, MLA_HEADS, MLA_NOPE + MLA_V)
    k_pe = jnp.broadcast_to(_rope(k_rope[:, :, None, :], positions), (B, S, MLA_HEADS, MLA_ROPE))
    k = jnp.concatenate([kv[..., :MLA_NOPE], k_pe], axis=-1)
    v = kv[..., MLA_NOPE:]
    n_blk = S // BLOCK
    q_blocks = (q * MLA_QK_DIM ** -0.5).reshape(B, n_blk, BLOCK, MLA_HEADS, MLA_QK_DIM).transpose(1, 0, 2, 3, 4)
    key_idx = jnp.arange(S)

    def attend(args):
        q_blk, blk = args
        s = jnp.einsum('bqhd,bkhd->bhqk', q_blk, k).astype(jnp.float32)
        q_idx = blk * BLOCK + jnp.arange(BLOCK)
        s = jnp.where(key_idx[None, :] <= q_idx[:, None], s, NEG_INF)
        p = jax.nn.softmax(s, axis=-1).astype(v.dtype)
        return jnp.einsum('bhqk,bkhd->bqhd', p, v)

    o = lax.map(attend, (q_blocks, jnp.arange(n_blk)))
    return o.transpose(1, 0, 2, 3, 4).reshape(B, S, MLA_WIDTH)

def _dilated_group(q, k, v, window, dilation, slopes):
    B, S, H, dh = q.shape
    span = window // dilation
    L = S // dilation
    n_blk = -(-L // BLOCK)
    Lp = n_blk * BLOCK

    def to_blocks(t):
        t = t.reshape(B, L, dilation, H, dh).transpose(0, 2, 3, 1, 4)
        t = jnp.pad(t, ((0, 0), (0, 0), (0, 0), (0, Lp - L), (0, 0)))
        return t.reshape(B, dilation, H, n_blk, BLOCK, dh)

    def band(t):
        prev = jnp.pad(t, ((0, 0), (0, 0), (0, 0), (1, 0), (0, 0), (0, 0)))[:, :, :, :-1]
        return jnp.concatenate([prev, t], axis=4)

    qb = to_blocks(q) * dh ** -0.5
    kb = band(to_blocks(k))
    vb = band(to_blocks(v))
    s = jnp.einsum('bdhnqe,bdhnke->bdhnqk', qb, kb).astype(jnp.float32)
    dist = jnp.arange(BLOCK)[:, None] + BLOCK - jnp.arange(2 * BLOCK)[None, :]
    key_sub = jnp.arange(n_blk)[:, None, None] * BLOCK - BLOCK + jnp.arange(2 * BLOCK)[None, None, :]
    valid = (dist >= 0) & (dist <= span) & (key_sub >= 0)
    alibi = -slopes.astype(jnp.float32)[:, None, None, None] * (dist * dilation).astype(jnp.float32)
    s = jnp.where(valid, s + alibi, NEG_INF)
    m = jnp.max(s, axis=-1, keepdims=True)
    e = jnp.exp(s - m)
    den = jnp.sum(e, axis=-1, keepdims=True)
    o = jnp.einsum('bdhnqk,bdhnke->bdhnqe', (e / den).astype(v.dtype), vb)
    lse = (m + jnp.log(den))[..., 0]
    o = o.reshape(B, dilation, H, Lp, dh)[:, :, :, :L].transpose(0, 3, 1, 2, 4).reshape(B, S, H, dh)
    lse = lse.reshape(B, dilation, H, Lp)[..., :L].transpose(0, 3, 1, 2).reshape(B, S, H)
    return o, lse

def _dilated_mixture(dil_qkv):
    B, S, _ = dil_qkv.shape
    qkv = dil_qkv.reshape(B, S, 3, DIL_GROUPS, DIL_HEADS_PER_GROUP, DIL_HEAD_DIM)
    slopes = _alibi_slopes(DIL_HEADS).reshape(DIL_HEADS_PER_GROUP, DIL_GROUPS).T
    outs, lses = [], []
    for g, (window, dilation) in enumerate(DIL_PAIRS):
        o, lse = _dilated_group(qkv[:, :, 0, g], qkv[:, :, 1, g], qkv[:, :, 2, g], window, dilation, slopes[g])
        outs.append(o)
        lses.append(lse)
    w = jax.nn.softmax(jnp.stack(lses, axis=0), axis=0)
    o_stack = jnp.stack(outs, axis=0)
    o = jnp.sum(w[..., None].astype(o_stack.dtype) * o_stack, axis=0)
    return o.reshape(B, S, DIL_WIDTH)

def _mem_attention(q, mem, g_mem, w_mem_kv):
    B, S, _ = q.shape
    M = mem.shape[1]
    kv = (_rms_norm(mem, g_mem) @ w_mem_kv).reshape(B, M, 2, MEM_HEADS, MEM_HEAD_DIM)
    qh = q.reshape(B, S, MEM_HEADS, MEM_HEAD_DIM) * MEM_HEAD_DIM ** -0.5
    s = jnp.einsum('bshd,bmhd->bhsm', qh, kv[:, :, 0]).astype(jnp.float32)
    p = jax.nn.softmax(s, axis=-1).astype(q.dtype)
    return jnp.einsum('bhsm,bmhd->bshd', p, kv[:, :, 1]).reshape(B, S, MEM_WIDTH)

def _conv_ffn(h, w_up, conv_w, conv_b, w_down):
    S = h.shape[1]
    u = h @ w_up
    u_pad = jnp.pad(u, ((0, 0), (CONV_WIDTH - 1, 0), (0, 0)))
    z = conv_b + conv_w[0] * u_pad[:, 0:S]
    for j in range(1, CONV_WIDTH):
        z = z + conv_w[j] * u_pad[:, j:j + S]
    gate, val = z[..., :D_FF], z[..., D_FF:]
    return (jax.nn.silu(gate) * val) @ w_down

def _layer(x, mem, positions, g_pre_mix, w_in, b_gate, mla_q_norm, w_uq, mla_kv_norm, w_ukv, g_mem, w_mem_kv,
           w_br_mla, w_br_dil, w_br_mem, w_o, g_post_mix, g_pre_ffn, w_ffn_up, conv_w, conv_b, w_ffn_down, g_post_ffn):
    B, S, _ = x.shape
    h = _rms_norm(x, g_pre_mix)
    proj = h @ w_in
    y_mla = _mla(proj[..., :OFF_Q], proj[..., OFF_Q:OFF_KV], proj[..., OFF_KV:OFF_KR], positions,
                 mla_q_norm, w_uq, mla_kv_norm, w_ukv)
    y_dil = _dilated_mixture(proj[..., OFF_KR:OFF_DIL])
    y_mem = _mem_attention(proj[..., OFF_DIL:OFF_MEMQ], mem, g_mem, w_mem_kv)
    gates = jax.nn.sigmoid((proj[..., OFF_MEMQ:] + b_gate).astype(jnp.float32)).astype(x.dtype)
    gates = gates.reshape(B, S, N_BRANCH, D_MODEL)
    merged = (gates[:, :, 0] * (y_mla @ w_br_mla)
              + gates[:, :, 1] * (y_dil @ w_br_dil)
              + gates[:, :, 2] * (y_mem @ w_br_mem))
    x = x + _rms_norm(merged @ w_o, g_post_mix)
    h2 = _rms_norm(x, g_pre_ffn)
    x = x + _rms_norm(_conv_ffn(h2, w_ffn_up, conv_w, conv_b, w_ffn_down), g_post_ffn)
    return x

def second_inputs(seed: int = 0) -> dict:
    key = jax.random.key(seed)
    ks = jax.random.split(key, 24)
    f32 = jnp.float32

    def dense(k, fan_in, fan_out):
        return jax.random.normal(k, (DEPTH_2, fan_in, fan_out), f32) * fan_in ** -0.5

    def gain(k, n):
        return 1.0 + 0.05 * jax.random.normal(k, (DEPTH_2, n), f32)

    x = jax.random.normal(ks[0], (BATCH, SEQ, D_MODEL), f32)
    mem = jax.random.normal(ks[1], (BATCH, N_MEM, D_MODEL), f32)
    offset = jax.random.randint(ks[2], (BATCH, 1), 0, MAX_POS_OFFSET, dtype=jnp.int32)
    positions = (offset + jnp.arange(SEQ, dtype=jnp.int32)[None, :]).astype(jnp.int32)
    return {
        "x": x,
        "mem": mem,
        "positions": positions,
        "g_pre_mix": gain(ks[3], D_MODEL),
        "w_in": dense(ks[4], D_MODEL, D_IN),
        "b_gate": 0.1 * jax.random.normal(ks[5], (DEPTH_2, N_BRANCH * D_MODEL), f32),
        "mla_q_norm": gain(ks[6], MLA_Q_RANK),
        "w_uq": dense(ks[7], MLA_Q_RANK, MLA_HEADS * MLA_QK_DIM),
        "mla_kv_norm": gain(ks[8], MLA_KV_RANK),
        "w_ukv": dense(ks[9], MLA_KV_RANK, MLA_HEADS * (MLA_NOPE + MLA_V)),
        "g_mem": gain(ks[10], D_MODEL),
        "w_mem_kv": dense(ks[11], D_MODEL, 2 * MEM_WIDTH),
        "w_br_mla": dense(ks[12], MLA_WIDTH, D_MODEL),
        "w_br_dil": dense(ks[13], DIL_WIDTH, D_MODEL),
        "w_br_mem": dense(ks[14], MEM_WIDTH, D_MODEL),
        "w_o": dense(ks[15], D_MODEL, D_MODEL),
        "g_post_mix": gain(ks[16], D_MODEL),
        "g_pre_ffn": gain(ks[17], D_MODEL),
        "w_ffn_up": dense(ks[18], D_MODEL, 2 * D_FF),
        "conv_w": jax.random.normal(ks[19], (DEPTH_2, CONV_WIDTH, 2 * D_FF), f32) * CONV_WIDTH ** -0.5,
        "conv_b": 0.01 * jax.random.normal(ks[20], (DEPTH_2, 2 * D_FF), f32),
        "w_ffn_down": dense(ks[21], D_FF, D_MODEL),
        "g_post_ffn": gain(ks[22], D_MODEL),
    }

def second_block(x, mem, positions, g_pre_mix, w_in, b_gate, mla_q_norm, w_uq, mla_kv_norm, w_ukv, g_mem, w_mem_kv,
              w_br_mla, w_br_dil, w_br_mem, w_o, g_post_mix, g_pre_ffn, w_ffn_up, conv_w, conv_b, w_ffn_down,
              g_post_ffn):
    for l in range(DEPTH_2):
        x = _layer(x, mem, positions, g_pre_mix[l], w_in[l], b_gate[l], mla_q_norm[l], w_uq[l], mla_kv_norm[l],
                   w_ukv[l], g_mem[l], w_mem_kv[l], w_br_mla[l], w_br_dil[l], w_br_mem[l], w_o[l], g_post_mix[l],
                   g_pre_ffn[l], w_ffn_up[l], conv_w[l], conv_b[l], w_ffn_down[l], g_post_ffn[l])
    return x


def setup_inputs(seed=0):
    out = dict(first_inputs(seed))
    for name, value in second_inputs(seed + 1).items():
        if name != "x":
            out[name + "_2"] = value
    return out


def reference(
    x, mem, emb_ln_g, emb_ln_b, w_in, lam_q1, lam_k1, lam_q2, lam_k2, subln_g, rpb, sc_conv_w,
    w_branch, w_mix_out, xa_q, xa_kv, xa_o, ffn_w_in, ffn_conv_w, ffn_conv_b, ffn_w_out, ln_g,
    ln_b, mem_2, positions_2, g_pre_mix_2, w_in_2, b_gate_2, mla_q_norm_2, w_uq_2,
    mla_kv_norm_2, w_ukv_2, g_mem_2, w_mem_kv_2, w_br_mla_2, w_br_dil_2, w_br_mem_2, w_o_2,
    g_post_mix_2, g_pre_ffn_2, w_ffn_up_2, conv_w_2, conv_b_2, w_ffn_down_2, g_post_ffn_2,
):
    x = first_block(
        x, mem, emb_ln_g, emb_ln_b, w_in, lam_q1, lam_k1, lam_q2, lam_k2, subln_g, rpb,
        sc_conv_w, w_branch, w_mix_out, xa_q, xa_kv, xa_o, ffn_w_in, ffn_conv_w, ffn_conv_b,
        ffn_w_out, ln_g, ln_b,
    )
    return second_block(
        x, mem_2, positions_2, g_pre_mix_2, w_in_2, b_gate_2, mla_q_norm_2, w_uq_2,
        mla_kv_norm_2, w_ukv_2, g_mem_2, w_mem_kv_2, w_br_mla_2, w_br_dil_2, w_br_mem_2, w_o_2,
        g_post_mix_2, g_pre_ffn_2, w_ffn_up_2, conv_w_2, conv_b_2, w_ffn_down_2, g_post_ffn_2,
    )


_drawn_inputs = setup_inputs


def setup_inputs(seed=0):
    import zlib

    import numpy as np

    out = dict(_drawn_inputs(seed))
    spreads = {}
    factors = {'lam_q1': 4.107,
     'lam_q2': 3.223,
     'lam_k2': 4.772,
     'subln_g': 8.0,
     'rpb': 23.43,
     'ffn_conv_b': 8.0,
     'mla_q_norm_2': 9.408,
     'g_mem_2': 3.516,
     'conv_b_2': 6.963,
     'mla_kv_norm_2': 2.877}
    for name, (base, spread) in spreads.items():
        noise = np.random.default_rng([zlib.crc32(name.encode()), seed]).standard_normal(out[name].shape)
        drawn = base * np.exp(spread * noise) if base else spread * noise
        out[name] = __import__('jax').numpy.asarray(drawn.astype(out[name].dtype))
    for name, factor in factors.items():
        out[name] = (out[name] * factor).astype(out[name].dtype)
    return out
```

```python
from contextlib import ExitStack

import numpy as np
import concourse.bass as bass
from concourse import mybir

F32 = mybir.dt.float32
I32 = mybir.dt.int32
ACT = mybir.ActivationFunctionType
ALU = mybir.AluOpType
AX = mybir.AxisListType

P = 128
T = 256
D = 1024
DC = D // P
DEPTH = 2
FF = 2816
FC = FF // P
FPAIR = FC // 2
TILE_N = 256
UNIT_TILES = 8
RING = 6
MEM_UNITS_1 = 89
UNITS_1 = 90
UNITS_2 = 85
ALPHA = (2.0 * DEPTH) ** 0.25
EPS_LN = 1e-5
EPS_RMS = 1e-6
NEG = -1e30

ROUND = 1.5 * 2.0 ** 23
TWO_PI = (6.28125, 0.0019350051879882812, 2 * 3.141592653589793 - 6.28125 - 0.0019350051879882812)
PI_BELOW = 3.1415925

RPB_H, RPB_R, RPB_C = 8, 15, 31
NJ = 6


def columns(*parts):
    at, n = {}, 0
    for name, width in parts:
        at[name] = n
        n += width
    return at, n


CONST, CONST_N = columns(("ident", P), ("rot1", P), ("cos", 2 * T), ("sin", 2 * T), ("ones", P), ("na_mask", 64),
                         ("causal", 384), ("rot2", 96), ("inv", 1), ("eps_ln", 1), ("eps_rms", 1),
                         ("emb_g", DC), ("emb_b", DC))
COL1, COL1_N = columns(("ln_g", 3 * DC), ("ln_b", 3 * DC), ("subln", 1), ("one_minus", 1), ("lam_init", 1),
                       ("sc_w", 12), ("ffn_w", 3 * FC), ("ffn_b", FC), ("lam", 256))
COL2, COL2_N = columns(("g_mem", DC), ("g_pre_mix", DC), ("q_norm", 3), ("kv_norm", 2), ("b_gate", 24),
                       ("g_pre_ffn", DC), ("conv_w", 6 * FC), ("conv_b", 2 * FC))
COL_N = max(COL1_N, COL2_N)

SLOPES = np.exp2(-8.0 * np.arange(1, 13, dtype=np.float64) / 12).astype(np.float32).reshape(4, 3).T

COUNTS = {
    "general_full0": (2, 27, 28),
    "general_full1": (2, 27, 27),
    "general_full2": (2, 26, 27),
    "general_full3": (2, 26, 27),
    "scores_full": (0, 20, 24),
    "probsT_full": (0, 16, 24),
    "attn_out_full": (0, 12, 12),
    "general_free0": (2, 27, 28),
    "general_free2": (2, 26, 27),
    "std_ready": (1, 3, 7),
    "general_free1": (2, 27, 27),
    "general_free3": (2, 26, 27),
    "lam_exp": (0, 1, 0),
    "exp_done": (0, 20, 16),
    "probsT_ready": (0, 16, 24),
    "attn_out_read": (0, 12, 12),
    "ya_sq": (0, 1, 0),
    "conv_init": (0, 11, 22),
    "silu_done": (0, 11, 11),
    "squares_done": (0, 0, 7),
    "sin_ready": (0, 0, 1),
    "dve_step": (2, 72, 84),
    "var_ready": (1, 3, 0),
    "xhat_ready": (2, 6, 7),
    "lam_sums": (0, 1, 0),
    "rope_ready": (0, 4, 5),
    "neg_max_ready": (0, 20, 16),
    "probs_ready": (0, 16, 16),
    "yc_ready": (0, 1, 0),
    "scores_read": (0, 8, 20),
    "ya_ready": (0, 1, 0),
    "merge_step": (0, 4, 4),
    "merged_ready": (0, 4, 4),
    "angle_ready": (0, 0, 1),
    "z_ready": (0, 0, 1),
    "ffn_act_ready": (0, 0, 11),
    "out_ready": (0, 0, 1),
    "rows_in": (1, 3, 2),
    "bias_in": (32, 1, 0),
    "pool_step": (1, 3, 0),
    "x_ready": (1, 3, 0),
    "cols_in": (0, 1, 1),
    "bias_ready": (0, 1, 0),
    "mem2_in": (0, 0, 1),
    "pos_in": (0, 0, 1),
    "dil_in": (0, 0, 1),
    "const_in": (1, 0, 0),
    "x_in": (2, 0, 0),
    "weights_landed0": (1, 15, 14),
    "weights_landed1": (1, 15, 13),
    "weights_landed2": (1, 15, 13),
    "weights_landed3": (1, 15, 13),
    "weights_landed4": (1, 15, 13),
    "weights_landed5": (1, 14, 13),
    "out_done": (0, 0, 1),
}


class Signal:

    def __init__(self, name, sem, unit, stage):
        self.name, self.sem, self.unit, self.stage = name, sem, unit, stage
        self.pro, self.per, self.post = COUNTS.get(name, (0, 0, 0))

    def at(self, n):
        return self.sem, self.unit * (self.stage.base(self) + n + 1)

    def last(self):
        return self.at(self.stage.said[self.name] - 1)

    def more(self):
        self.stage.count(self)
        return self.sem, self.unit


class Stage:

    def __init__(self):
        self.kind, self.layer, self.said, self.seen = "pro", 0, {}, {}

    def enter(self, kind, layer=0):
        self.kind, self.layer, self.said = kind, layer, {}

    def base(self, s):
        if self.kind == "pro":
            return 0
        if self.kind == "layer":
            return s.pro + self.layer * s.per
        return s.pro + DEPTH * s.per

    def count(self, s, k=1):
        self.said[s.name] = self.said.get(s.name, 0) + k
        which = ("pro", "layer", "post").index(self.kind)
        self.seen.setdefault(s.name, [0, 0, 0])[which] += k


def jobs_of(kind):
    sets = {"layer": (("da", 8), ("na", 8), ("xa", 4)), "post": (("mla", 8), ("dil", 4), ("mem", 4))}[kind]
    return [(name, i) for name, n in sets for i in range(n)]


def parts_of(name):
    return 3 if name == "dil" else 1


def build(nc, a, out):
    stage = Stage()
    ctx = ExitStack()
    with ctx:
        def sb(name, cols, dt=F32):
            return ctx.enter_context(nc.sbuf_tensor(name, [P, cols], dt))

        def signal(name, unit=1):
            return Signal(name, ctx.enter_context(nc.semaphore(name)), unit, stage)



        ring = sb("weight_ring", RING * UNIT_TILES * TILE_N)
        x_tok = sb("x_tok", 2 * D)
        z_tok = sb("z_tok", 2 * D)
        xT = sb("xT", DC * T)
        memT = sb("memT", DC * T)
        big = sb("gates_or_ffn", 24 * T)
        yT = sb("branch_inputs", 12 * T)
        e_ring = sb("exp_ring", 3 * 1152)
        pT = sb("probsT_ring", 4 * 512)
        rows = sb("ln_rows", 2 * D)
        const = sb("const", CONST_N)
        col = sb("param_cols", COL_N)
        area = sb("attention_area", 48 * T)
        stat = sb("softmax_stats", 24)
        nst = sb("norm_stats", 64)

        def mat(tile, c0, n, w=T):
            return tile[:, c0:c0 + n * w].rearrange("p (c w) -> p c w", w=w)

        x3, z3 = mat(x_tok, 0, 2, D), mat(z_tok, 0, 2, D)
        xT3, memT3, big3, yT3 = mat(xT, 0, DC), mat(memT, 0, DC), mat(big, 0, 24), mat(yT, 0, 12)
        ident = const[:, CONST["ident"]:CONST["ident"] + P]
        ones = const[:, CONST["ones"]:CONST["ones"] + P]
        cos2 = const[:, CONST["cos"]:CONST["cos"] + 2 * T]
        sin2 = const[:, CONST["sin"]:CONST["sin"] + 2 * T]
        qa, ka = mat(area, 0, 4), mat(area, 4 * T, 4)
        va = mat(area, 8 * T, 2, 512)
        qn, kn = mat(area, 12 * T, 4), mat(area, 16 * T, 4)
        vn = mat(area, 20 * T, 2, 512)
        gb, cin = mat(area, 24 * T, 4), mat(area, 28 * T, 4)
        gc = mat(area, 32 * T, 4)
        bias_tab = area[:, 36 * T:48 * T].rearrange("p (h j k) -> p h j k", h=8, j=NJ)
        conv_tmp = mat(z_tok, 0, 4)
        ya_rstd = mat(z_tok, 4 * T, 4)
        raw = mat(big, 0, 8)
        scratch = mat(e_ring, 2048, 2, 512)
        xq, xk = mat(area, 0, 8), mat(area, 8 * T, 8)
        xv = mat(area, 16 * T, 2, D)
        qm = mat(z_tok, 0, 8)
        km = mat(area, 0, 8)
        vm = mat(area, 8 * T, 2, 512)
        mk, mq = mat(area, 0, 4), mat(area, 4 * T, 4)
        mv = mat(area, 8 * T, 2, 512)
        dq, dk = mat(area, 12 * T, 12), mat(area, 24 * T, 12)
        dv = mat(area, 36 * T, 2, 1536)
        mem2 = mat(area, 12 * T, 2, D)
        cz = mat(e_ring, 0, 2, 768)
        cT = mat(pT, 0, 5)
        kraw = big[:, 0:T]
        angle, half_sine = big[:, 2 * T:3 * T], big[:, 3 * T:4 * T]
        turns, pos_int = big[:, 4 * T:5 * T], big[:, 5 * T:6 * T].bitcast(I32)
        junk = mat(yT, 0, 2, D)
        distm = rows[:, 0:3 * 384].rearrange("p (g w) -> p g w", g=3)
        dbias = rows[:, 3 * 384:5 * 384].rearrange("p (b w) -> p b w", b=2)
        merged = mat(e_ring, 0, 8)
        merge_tmp = mat(z_tok, 0, 2, 512)
        mem_tok = mat(area, 0, 2, D)

        def colp(name, i=0, packed=COL1):
            return col[:, packed[name] + i:packed[name] + i + 1]

        def cconst(name, i=0):
            return const[:, CONST[name] + i:CONST[name] + i + 1]

        ps = [ctx.enter_context(nc.psum_tensor(f"general{b}", [P, 512], F32)) for b in range(4)]
        sc = [ctx.enter_context(nc.psum_tensor(f"scores{b}", [P, 512], F32)) for b in range(2)]
        tp = ctx.enter_context(nc.psum_tensor("probs_transposed", [P, 512], F32))
        po = ctx.enter_context(nc.psum_tensor("attention_out", [P, 512], F32))

        const_in = signal("const_in", 16)
        xin = signal("x_in", 16)
        landed = [signal(f"weights_landed{s}", 16) for s in range(RING)]
        cols_in = signal("cols_in", 16)
        rows_in = signal("rows_in", 16)
        bias_in = signal("bias_in", 16)
        bias_ready = signal("bias_ready")
        full = [signal(f"general_full{b}") for b in range(4)]
        free = [signal(f"general_free{b}") for b in range(4)]
        sc_full = signal("scores_full")
        sc_read = signal("scores_read")
        tp_full = signal("probsT_full")
        pT_ready = signal("probsT_ready")
        po_full = signal("attn_out_full")
        po_read = signal("attn_out_read")
        nmax = signal("neg_max_ready")
        exp_done = signal("exp_done")
        p_ready = signal("probs_ready")
        dve_step = signal("dve_step")
        pool_step = signal("pool_step")
        squares_done = signal("squares_done")
        var_ready = signal("var_ready")
        std_ready = signal("std_ready")
        xhat_ready = signal("xhat_ready")
        x_ready = signal("x_ready")
        rope_ready = signal("rope_ready")
        ya_sq = signal("ya_sq")
        ya_std = signal("ya_std")
        ya_ready = signal("ya_ready")
        yc_ready = signal("yc_ready")
        merged_ready = signal("merged_ready")
        merge_step = signal("merge_step")
        conv_init = signal("conv_init")
        silu_done = signal("silu_done")
        act_ready = signal("ffn_act_ready")
        z_ready = signal("z_ready")
        lam_sum = signal("lam_sums")
        lam_exp = signal("lam_exp")
        angle_ready = signal("angle_ready")
        sin_ready = signal("sin_ready")
        dil_in = signal("dil_in", 16)
        pos_in = signal("pos_in", 16)
        mem2_in = signal("mem2_in", 16)
        out_ready = signal("out_ready")
        out_done = signal("out_done", 16)

        FILLS, LAST_USE = {}, {}
        ORDER = {"layer": jobs_of("layer"), "post": jobs_of("post")}

        def fill_of(key):
            return FILLS[(stage.kind, key)]




        def need_last_phase(eng):
            for b in range(4):
                eng.wait_ge(*free[b].at(-1))

        def need_act(eng, i):
            if stage.kind == "layer":
                eng.wait_ge(*when_read(("up", i)))
            else:
                eng.wait_ge(*act_ready.at(i))

        def cbuf(i, k):
            return e_ring[:, (2 * i + k) * 512:(2 * i + k) * 512 + 512]

        def sbuf(i):
            return e_ring[:, 2048 + (i % 2) * 512:2048 + (i % 2) * 512 + 512]

        def need_exp_buffer(eng, j):
            k = j - 3
            if k < 0:
                return
            name, i = ORDER[stage.kind][k]
            if k not in NUM[stage.kind][3]:
                eng.wait_ge(*p_ready.at(NUM[stage.kind][3][k + 1]))
            else:
                eng.wait_ge(*tp_full.at(NUM[stage.kind][1][(k, parts_of(name) - 1)]))

        def bank_of(key):
            return ps[fill_of(key)[0]]

        def when_full(key):
            b, n = fill_of(key)
            return full[b].at(n)

        def when_read(key):
            b, n = fill_of(key)
            return free[b].at(n)

        def read(key):
            return free[fill_of(key)[0]].more()

        def numbering(kind):
            scores, transposes, outs, probs, owner = {}, {}, {}, {}, []
            for j, (name, i) in enumerate(ORDER[kind]):
                for g in range(parts_of(name)):
                    scores[(j, g)] = len(scores)
                    owner.append(j)
                if name != "da" or i % 2 == 1:
                    probs[j] = len(probs)
                    for g in range(parts_of(name)):
                        transposes[(j, g)] = len(transposes)
                if name not in ("da", "na", "mla") or i % 2 == 1:
                    outs[j] = len(outs)
            return scores, transposes, outs, probs, owner

        NUM = {k: numbering(k) for k in ORDER}
        READS = {}
        for kind in ORDER:
            n = 0
            for j, (name, i) in enumerate(ORDER[kind]):
                for g in range(parts_of(name)):
                    if name in ("na", "mla", "dil"):
                        READS[(kind, j, g)] = n
                        n += 1

        def spans(name):
            return ((0, 128), (128, 384)) if name in ("mla", "dil") else ((0, 256), (256, 512))

        def exp_views(j, t):
            name, _ = ORDER[stage.kind][j]
            lo, hi = spans(name)[t]
            e = e_ring[:, (j % 3) * 1152:(j % 3) * 1152 + 1152]
            if name == "dil":
                return e.rearrange("p (g w) -> p g w", g=3)[:, :, lo:hi]
            return e[:, lo:hi]

        def st(kind, j, t0=0, t1=2):
            o = {"mx": 0, "nm": 6, "sum": 12, "rec": 18}[kind] + 2 * (j % 3)
            return stat[:, o + t0:o + t1]

        def set_jobs(name):
            return [j for j, (s, _) in enumerate(ORDER[stage.kind]) if s == name]

        def step_slots(fillers, n):
            slots = [[] for _ in range(n)]
            extra = max(0, len(fillers) - n)
            k = 0
            for i in range(n):
                take = 1 + (1 if i < extra else 0)
                slots[i] = fillers[k:k + take]
                k += take
            return slots

        SC_FILL = [("gc", 0), ("gc", 1), ("hc", 0), ("hc", 1), ("gb", 0), ("gb", 1)]
        GATES = [("gate", i) for i in range(12)]
        da_fillers, na_fillers = step_slots((SC_FILL + GATES)[:10], 10), step_slots(GATES[4:], 10)
        xa_fillers = step_slots([("xv", i) for i in range(4)], 6)
        mla_fillers = step_slots(GATES, 10)
        dil_fillers = step_slots([("mk", 0), ("mk", 1), ("mv", 0), ("mv", 1), ("mq", 0), ("mq", 1)], 6)
        mem_fillers = step_slots([], 6)

        SCALE = {"da": 0.125, "na": 0.125, "xa": 1.0 / 16, "mla": 96.0 ** -0.5, "dil": 128.0 ** -0.5,
                 "mem": 128.0 ** -0.5}

        block = ctx.enter_context(nc.Block())

        @block.tensor
        def _(pe):
            state = {"tile": 0, "bank": 0, "uses": [0] * 4}

            def start_phase(kind, l=0):
                stage.enter(kind, l)
                state["tile"], state["bank"], state["uses"] = 0, 0, [0] * 4

            def open_bank(key):
                b = state["bank"] % 4
                state["bank"] += 1
                n = state["uses"][b]
                state["uses"][b] += 1
                FILLS[(stage.kind, key)] = (b, n)
                if n > 0 or stage.kind != "pro":
                    pe.wait_ge(*free[b].at(n - 1))
                return b

            def weight_tile(g):
                slot = (g // UNIT_TILES) % RING
                at = (slot * UNIT_TILES + g % UNIT_TILES) * TILE_N
                return ring[:, at:at + TILE_N]

            def linear(key, act, kcs, feature_major, m=P):
                b = open_bank(key)
                g0 = state["tile"]
                state["tile"] += kcs
                for half in range(2):
                    for kc in range(kcs):
                        g = g0 + kc
                        u = g // UNIT_TILES
                        if half == 0 and g % UNIT_TILES == 0:
                            pe.wait_ge(*landed[u % RING].at(u // RING - 1))
                        w = weight_tile(g)
                        if feature_major:
                            ins = nc.tensor.matmul(ps[b][0:m, half * T:half * T + T], w[:, half * m:half * m + m],
                                                   act(kc), start=(kc == 0), stop=(kc == kcs - 1))
                        else:
                            ins = nc.tensor.matmul(ps[b][:, half * T:half * T + T], act(kc)[:, half * P:half * P + P],
                                                   w, start=(kc == 0), stop=(kc == kcs - 1))
                ins.then_inc(*full[b].more())
                for u in range(g0 // UNIT_TILES, (g0 + kcs - 1) // UNIT_TILES + 1):
                    LAST_USE[(stage.kind, u)] = (b, FILLS[(stage.kind, key)][1])

            def transposes(key, src, n0):
                b = open_bank(key)
                for c in range(2):
                    for t in range(2):
                        ins = nc.tensor.transpose(ps[b][:, c * T + t * P:c * T + t * P + P],
                                                  src[:, t, (n0 + c) * P:(n0 + c) * P + P], ident)
                ins.then_inc(*full[b].more())

            def to_feature(name, src):
                for i in range(DC // 2):
                    transposes((name, i), src, 2 * i)

            def job(j):
                return ORDER[stage.kind][j]

            def scores(j):
                name, i = job(j)
                number = NUM[stage.kind][0]
                for g in range(parts_of(name)):
                    n = number[(j, g)]
                    if n >= 2:
                        jj = NUM[stage.kind][4][n - 2]
                        gg = n - 2 - number[(jj, 0)]
                        if job(jj)[0] in ("na", "mla", "dil"):
                            pe.wait_ge(*sc_read.at(READS[(stage.kind, jj, gg)]))
                        else:
                            pe.wait_ge(*exp_done.at(jj))
                    dst = sc[n % 2]
                    for t in range(2):
                        lo, hi = spans(name)[t]
                        q0 = t * P
                        if name in ("da", "na"):
                            r0 = 64 * (i % 2)
                            q, k = (qa, ka) if name == "da" else (qn, kn)
                            pairs = [(q[r0:r0 + 64, i // 2, q0:q0 + P], k[r0:r0 + 64, i // 2, :])]
                        elif name == "xa":
                            pairs = [(xq[:, 2 * i + c, q0:q0 + P], xk[:, 2 * i + c, :]) for c in range(2)]
                        elif name == "mla":
                            pairs = [(qm[0:96, i, q0:q0 + P], km[0:96, i, 0:hi - lo])]
                        elif name == "dil":
                            pairs = [(dq[:, 4 * g + i, q0:q0 + P], dk[:, 4 * g + i, 0:hi - lo])]
                        else:
                            pairs = [(mq[:, i, q0:q0 + P], mk[:, i, :])]
                        for c, (q, k) in enumerate(pairs):
                            ins = nc.tensor.matmul(dst[:, lo:hi], q, k, start=(c == 0), stop=(c == len(pairs) - 1))
                    ins.then_inc(*sc_full.more())

            def turn(j):
                name, i = job(j)
                if j not in NUM[stage.kind][3]:
                    return
                pe.wait_ge(*p_ready.at(NUM[stage.kind][3][j]))
                for g in range(parts_of(name)):
                    n = NUM[stage.kind][1][(j, g)]
                    if n > 0:
                        pe.wait_ge(*pT_ready.at(n - 1))
                    for t in range(2):
                        e = exp_views(j, t)
                        if name == "dil":
                            e = e[:, g, :]
                        for kt in range(2 if spans(name)[t][1] - spans(name)[t][0] == 256 else 1):
                            ins = nc.tensor.transpose(tp[:, kt * T + t * P:kt * T + t * P + P],
                                                      e[:, kt * P:kt * P + P], ident)
                    ins.then_inc(*tp_full.more())

            def values(j):
                name, i = job(j)
                if j not in NUM[stage.kind][3]:
                    return
                parts = parts_of(name)
                pe.wait_ge(*pT_ready.at(NUM[stage.kind][1][(j, parts - 1)]))
                pair = name in ("na", "mla")
                if not (pair and i % 2 == 1):
                    n = NUM[stage.kind][2][j + 1 if pair else j]
                    if n > 0:
                        pe.wait_ge(*po_read.at(n - 1))
                for c in range(2 if name == "xa" else 1):
                    first = True
                    for g in range(parts):
                        slot = NUM[stage.kind][1][(j, g)] % 4
                        for kt in range(2):
                            p = pT[:, slot * 512 + kt * T:slot * 512 + kt * T + T]
                            lo = P if kt == 1 and name in ("mla", "dil") else 0
                            if name == "da":
                                v, r0, m = va[:, kt, (i // 2) * P:(i // 2) * P + P], 0, P
                            elif name == "na":
                                v, r0, m = vn[:, kt, i * 64:i * 64 + 64], 64 * (i % 2), 64
                            elif name == "mla":
                                v, r0, m = vm[:, kt, i * 64:i * 64 + 64], 64 * (i % 2), 64
                            elif name == "xa":
                                v, r0, m = xv[:, kt, (2 * i + c) * P:(2 * i + c) * P + P], 0, P
                            elif name == "dil":
                                v, r0, m = dv[:, kt, (4 * g + i) * P:(4 * g + i) * P + P], 0, P
                            else:
                                v, r0, m = mv[:, kt, i * P:i * P + P], 0, P
                            ins = nc.tensor.matmul(po[r0:r0 + m, c * T + lo:c * T + T], v, p[:, lo:T],
                                                   start=first, stop=(g == parts - 1 and kt == 1))
                            first = False
                if j in NUM[stage.kind][2]:
                    ins.then_inc(*po_full.more())

            def filler(key):
                kind = key[0]
                if kind in ("gc", "hc", "gb", "gate"):
                    linear(key, lambda kc: xT3[:, kc, :], DC, True)
                elif kind == "xv" or kind == "mv":
                    linear(key, lambda kc: memT3[:, kc, :], DC, False)
                elif kind == "mk":
                    linear(key, lambda kc: memT3[:, kc, :], DC, True)
                elif kind == "mq":
                    linear(key, lambda kc: xT3[:, kc, :], DC, True)

            def attention(name, fillers):
                js = set_jobs(name)
                for step in range(len(js) + 2):
                    if step < len(js):
                        scores(js[step])
                    for key in fillers[step]:
                        filler(key)
                    if step >= 2:
                        values(js[step - 2])
                    if 1 <= step <= len(js):
                        turn(js[step - 1])

            def need_xT(name):
                for i in range(DC // 2):
                    pe.wait_ge(*when_read((name, i)))

            def branches():
                for cb in range(4):
                    for br in range(3):
                        linear(("branch", cb, br), lambda kc: yT3[:, 4 * br + kc, :], 4, True)

            def project(name, n):
                pe.wait_ge(*merged_ready.at(3))
                for cb in range(4):
                    linear((name, cb), lambda kc: merged[:, kc, :], DC, False)

            def ffn(order):
                for i in range(FPAIR):
                    for which in order:
                        linear((which, i), lambda kc: xT3[:, kc, :], DC, True)
                need_act(pe, FPAIR - 1)
                for cb in range(4):
                    linear(("down", cb), lambda kc: big3[:, kc, :], FC, False)

            start_phase("pro")
            pe.wait_ge(*const_in.at(0))
            pe.wait_ge(*xin.at(1))
            to_feature("memT", mem_tok)
            pe.wait_ge(*xhat_ready.at(1))
            to_feature("xT0", z3)

            with pe.Fori(0, DEPTH) as l:
                start_phase("layer", l)
                need_last_phase(pe)
                for name in ("qa", "ka"):
                    for i in range(2):
                        linear((name, i), lambda kc: xT3[:, kc, :], DC, True)
                for i in range(2):
                    linear(("va", i), lambda kc: xT3[:, kc, :], DC, False)
                for n, (name, i) in enumerate((("qa", 0), ("qa", 1), ("ka", 0), ("ka", 1))):
                    pe.wait_ge(*when_read((name, i)))
                    b = open_bank(("rot", n))
                    nc.tensor.matmul(ps[b][:, :], const[:, CONST["rot1"]:CONST["rot1"] + P],
                                         raw[:, 2 * n:2 * n + 2, :], start=True, stop=True).then_inc(*full[b].more())
                for name in ("qn", "kn"):
                    for i in range(2):
                        linear((name, i), lambda kc: xT3[:, kc, :], DC, True)
                for i in range(2):
                    linear(("vn", i), lambda kc: xT3[:, kc, :], DC, False)
                pe.wait_ge(*rope_ready.at(3))
                pe.wait_ge(*when_read(("va", 1)))
                attention("da", da_fillers)
                pe.wait_ge(*when_read(("vn", 1)))
                pe.wait_ge(*when_read(("vn", 0)))
                attention("na", na_fillers)
                pe.wait_ge(*ya_sq.at(0))
                for i in range(2):
                    b = open_bank(("ss", i))
                    nc.tensor.matmul(ps[b][:, :], ones, conv_tmp[:, 2 * i:2 * i + 2, :], start=True, stop=True).then_inc(*full[b].more())
                pe.wait_ge(*ya_ready.at(0))
                pe.wait_ge(*yc_ready.at(0))
                pe.wait_ge(*po_read.at(NUM["layer"][2][15]))
                branches()
                project("mix", 0)
                for i in range(4):
                    linear(("xk", i), lambda kc: memT3[:, kc, :], DC, True)
                pe.wait_ge(*xhat_ready.at(1))
                to_feature("ln0", z3)
                need_xT("ln0")
                for i in range(4):
                    linear(("xq", i), lambda kc: xT3[:, kc, :], DC, True)
                pe.wait_ge(*when_read(("xk", 3)))
                for i in range(4):
                    pe.wait_ge(*when_read(("xq", i)))
                attention("xa", xa_fillers)
                pe.wait_ge(*po_read.at(NUM["layer"][2][19]))
                for cb in range(4):
                    linear(("xo", cb), lambda kc: yT3[:, kc, :], DC, False)
                pe.wait_ge(*xhat_ready.at(3))
                to_feature("ln1", z3)
                need_xT("ln1")
                ffn(("gt", "up"))
                pe.wait_ge(*xhat_ready.at(5))
                to_feature("ln2", z3)

            start_phase("post")
            pe.wait_ge(*xhat_ready.at(1))
            to_feature("premix", z3)
            need_xT("premix")
            for i in range(3):
                linear(("c", i), lambda kc: xT3[:, kc, :], DC, False)
            pe.wait_ge(*xhat_ready.at(3))
            to_feature("mem2T", mem2)
            pe.wait_ge(*xhat_ready.at(4))
            for i in range(3):
                b = open_bank(("cT", i))
                for c in range(2):
                    lo, w = ((2 * i + c) * P, P) if 2 * i + c < 5 else (576, 96)
                    for t in range(2):
                        ins = nc.tensor.transpose(ps[b][0:w, c * T + t * P:c * T + t * P + P], cz[:, t, lo:lo + w],
                                                  ident)
                ins.then_inc(*full[b].more())
            for i in range(3):
                pe.wait_ge(*when_read(("cT", i)))
            for i in range(4):
                linear(("uq", i), lambda kc: cT[:, kc, :], 3, True, m=96)
            for i in range(2):
                linear(("uk", i), lambda kc: cT[:, 3 + kc, :], 2, True)
            for i in range(2):
                linear(("uv", i), lambda kc: cT[:, 3 + kc, :], 2, False)
            for i in range(5):
                b = open_bank(("rot2", i))
                if i < 4:
                    pe.wait_ge(*when_read(("uq", i)))
                    src = qm[64:96, 2 * i:2 * i + 2, :]
                else:
                    src = kraw[64:96, :]
                nc.tensor.matmul(ps[b][0:96, 0:512 if i < 4 else T], const[64:96, CONST["rot2"]:CONST["rot2"] + 96],
                                     src, start=True, stop=True).then_inc(*full[b].more())
            pe.wait_ge(*rope_ready.at(4))
            for key in (("uk", 0), ("uk", 1), ("uv", 0), ("uv", 1)):
                pe.wait_ge(*when_read(key))
            attention("mla", mla_fillers)
            for name in ("dq", "dk"):
                for i in range(6):
                    linear((name, i), lambda kc: xT3[:, kc, :], DC, True)
            for i in range(6):
                linear(("dv", i), lambda kc: xT3[:, kc, :], DC, False)
            for name in ("dq", "dk", "dv"):
                for i in range(2, 6):
                    pe.wait_ge(*when_read((name, i)))
            attention("dil", dil_fillers)
            for key in (("mk", 0), ("mk", 1), ("mv", 0), ("mv", 1), ("mq", 0), ("mq", 1)):
                pe.wait_ge(*when_read(key))
            attention("mem", mem_fillers)
            pe.wait_ge(*po_read.at(NUM["post"][2][15]))
            branches()
            project("wo", 0)
            pe.wait_ge(*xhat_ready.at(6))
            to_feature("preffn", z3)
            need_xT("preffn")
            ffn(("gt", "up"))

        @block.scalar
        def _(act):
            def evacuate(key, dst, func=ACT.Copy, **kw):
                act.wait_ge(*when_full(key))
                src = bank_of(key)
                nc.scalar.activation(dst, src[:, :].rearrange("p (c w) -> p c w", w=T), func, **kw).then_inc(*read(key))

            def gains(name, k0, dst, gain, bias):
                for i in (0, 2):
                    act.wait_ge(*when_full((name, i)))
                    src = bank_of((name, i))
                    for c in range(2):
                        part, o = src[:, c * T:c * T + T], dst[:, 2 * i + c, :]
                        if gain is None:
                            ins = nc.scalar.activation(o, part, ACT.Copy)
                        elif bias is None:
                            ins = nc.scalar.activation(o, part, ACT.Copy, scale=gain(2 * i + c))
                        else:
                            ins = nc.scalar.activation(o, part, ACT.Identity, bias=bias(2 * i + c),
                                                       scale=gain(2 * i + c))
                    ins.then_inc(*read((name, i)))

            def exps(j):
                name, i = ORDER[stage.kind][j]
                act.wait_ge(*nmax.at(j))
                scale = SCALE[name]
                from_psum = name in ("da", "xa", "mem")
                if from_psum:
                    need_exp_buffer(act, j)
                for t in range(2):
                    e = exp_views(j, t)
                    lo, hi = spans(name)[t]
                    src = sc[NUM[stage.kind][0][(j, 0)] % 2][:, lo:hi] if from_psum else e
                    ins = nc.scalar.activation(e, src, ACT.Exp, bias=st("nm", j, t, t + 1),
                                               scale=scale if from_psum else 1.0, accum_out=st("sum", j, t, t + 1))
                ins.then_inc(*exp_done.more())

            def probs_out(j):
                name, i = ORDER[stage.kind][j]
                if j not in NUM[stage.kind][3]:
                    return
                for g in range(parts_of(name)):
                    n = NUM[stage.kind][1][(j, g)]
                    act.wait_ge(*tp_full.at(n))
                    if n >= 4:
                        jj = [k for k, v in NUM[stage.kind][1].items() if v == n - 4][0][0]
                        outs = NUM[stage.kind][2]
                        if jj in outs:
                            act.wait_ge(*po_full.at(outs[jj]))
                        else:
                            act.wait_ge(*po_full.at(outs[jj + 1]))
                    slot = n % 4
                    if name in ("mla", "dil"):
                        nc.scalar.activation(pT[:, slot * 512:slot * 512 + T], tp[:, 0:T], ACT.Copy)
                        ins = nc.scalar.activation(pT[:, slot * 512 + 384:slot * 512 + 512], tp[:, 384:512], ACT.Copy)
                    else:
                        ins = nc.scalar.activation(pT[:, slot * 512:slot * 512 + 512], tp[:, :], ACT.Copy)
                    ins.then_inc(*pT_ready.more())

            def attn_out(j):
                name, i = ORDER[stage.kind][j]
                if j not in NUM[stage.kind][2]:
                    return
                act.wait_ge(*po_full.at(NUM[stage.kind][2][j]))
                if name == "xa":
                    dst, src = yT3[:, 2 * i:2 * i + 2, :], po[:, :].rearrange("p (c w) -> p c w", w=T)
                else:
                    c = {"da": i // 2, "na": 4 + i // 2, "mla": i // 2, "dil": 4 + i, "mem": 8 + i}[name]
                    dst, src = yT3[:, c, :], po[:, 0:T]
                nc.scalar.activation(dst, src, ACT.Copy).then_inc(*po_read.more())

            def filler(key):
                kind, i = key
                if kind == "gate":
                    act.wait_ge(*when_full(key))
                    src = bank_of(key)
                    if stage.kind == "layer":
                        nc.scalar.activation(big3[:, 2 * i:2 * i + 2, :],
                                                     src[:, :].rearrange("p (c w) -> p c w", w=T), ACT.Sigmoid).then_inc(*read(key))
                    else:
                        for c in range(2):
                            ins = nc.scalar.activation(big3[:, 2 * i + c, :], src[:, c * T:c * T + T], ACT.Sigmoid,
                                                       bias=colp("b_gate", 2 * i + c, COL2), scale=1.0)
                        ins.then_inc(*read(key))
                elif kind in ("gc", "gb", "mk", "mq"):
                    evacuate(key, {"gc": gc, "gb": gb, "mk": mk, "mq": mq}[kind][:, 2 * i:2 * i + 2, :])
                elif kind == "mv":
                    evacuate(key, mv[:, :, i * T:i * T + T])
                elif kind == "xv":
                    evacuate(key, xv[:, :, i * T:i * T + T])

            def attention(name, fillers):
                js = set_jobs(name)
                for step in range(len(js) + 2):
                    if step < len(js):
                        exps(js[step])
                    for key in fillers[step]:
                        filler(key)
                    if step >= 2:
                        attn_out(js[step - 2])
                    if 1 <= step <= len(js):
                        probs_out(js[step - 1])

            def std(n, src, dst, scale, eps):
                act.wait_ge(*var_ready.at(n))
                nc.scalar.activation(dst, src, ACT.Sqrt, bias=cconst(eps), scale=scale).then_inc(*std_ready.more())

            def ffn(gates_too, packed, w, b):
                for i in range(FPAIR + 1):
                    if i < FPAIR:
                        for k, which in enumerate(("gt", "up") if gates_too else ("gt",)):
                            act.wait_ge(*when_full((which, i)))
                            src = bank_of((which, i))
                            if i >= 2:
                                need_act(act, i - 2)
                            for c in range(2):
                                ch = (k * FC if gates_too else 0) + 2 * i + c
                                tap = 2 if gates_too else 1
                                dst = cbuf(i % 2, k)[:, c * T:c * T + T]
                                ins = nc.scalar.activation(dst, src[:, c * T:c * T + T], ACT.Identity,
                                                           bias=colp(b, ch, packed),
                                                           scale=colp(w, 3 * ch + tap, packed))
                            ins.then_inc(*conv_init.more())
                    if i >= 1:
                        act.wait_ge(*when_read(("gt", i - 1)))
                        nc.scalar.activation(sbuf(i - 1), cbuf((i - 1) % 2, 0), ACT.Silu).then_inc(*silu_done.more())

            stage.enter("pro")
            act.wait_ge(*const_in.at(0))
            gains("memT", 0, memT3, None, None)
            std(0, nst[:, 49:52:2], nst[:, 52:54], 1.0, "eps_ln")
            gains("xT0", 0, xT3, lambda c: cconst("emb_g", c), lambda c: cconst("emb_b", c))

            with act.Fori(0, DEPTH) as l:
                stage.enter("layer", l)
                need_last_phase(act)
                for n, (name, i) in enumerate((("qa", 0), ("qa", 1), ("ka", 0), ("ka", 1))):
                    evacuate((name, i), raw[:, 2 * n:2 * n + 2, :])
                for i in range(2):
                    evacuate(("va", i), va[:, :, i * T:i * T + T])
                for name, dst in (("qn", qn), ("kn", kn)):
                    for i in range(2):
                        evacuate((name, i), dst[:, 2 * i:2 * i + 2, :])
                for i in range(2):
                    evacuate(("vn", i), vn[:, :, i * T:i * T + T])
                act.wait_ge(*lam_sum.at(0))
                nc.scalar.activation(nst[:, 58:60], nst[:, 56:58], ACT.Exp).then_inc(*lam_exp.more())
                attention("da", da_fillers)
                attention("na", na_fillers)
                act.wait_ge(*yc_ready.at(0))
                nc.scalar.activation(conv_tmp, yT3[:, 0:4, :], ACT.Square).then_inc(*ya_sq.more())
                for i in range(2):
                    act.wait_ge(*when_full(("ss", i)))
                    src = bank_of(("ss", i))
                    ins = nc.scalar.activation(ya_rstd[:, 2 * i:2 * i + 2, :],
                                               src[:, :].rearrange("p (c w) -> p c w", w=T), ACT.Sqrt, bias=cconst("eps_ln"), scale=1.0 / P)
                    ins.then_inc(*read(("ss", i)))
                for i in range(4):
                    evacuate(("xk", i), xk[:, 2 * i:2 * i + 2, :])
                std(0, nst[:, 49:52:2], nst[:, 52:54], 1.0, "eps_ln")
                gains("ln0", 0, xT3, lambda c: colp("ln_g", c), lambda c: colp("ln_b", c))
                for i in range(4):
                    evacuate(("xq", i), xq[:, 2 * i:2 * i + 2, :])
                attention("xa", xa_fillers)
                std(1, nst[:, 49:52:2], nst[:, 52:54], 1.0, "eps_ln")
                gains("ln1", 0, xT3, lambda c: colp("ln_g", DC + c), lambda c: colp("ln_b", DC + c))
                ffn(False, COL1, "ffn_w", "ffn_b")
                std(2, nst[:, 49:52:2], nst[:, 52:54], 1.0, "eps_ln")
                gains("ln2", 0, xT3, lambda c: colp("ln_g", 2 * DC + c), lambda c: colp("ln_b", 2 * DC + c))

            stage.enter("post")
            act.wait_ge(*cols_in.at(0))
            act.wait_ge(*mem2_in.at(0))

            def mean_square(src, width, n0):
                for t in range(2):
                    ins = nc.scalar.activation(junk[:, t, 0:width], src[:, t, 0:width], ACT.Square,
                                               accum_out=nst[:, n0 + t:n0 + t + 1])
                ins.then_inc(*squares_done.more())
                act.wait_ge(*squares_done.last())
                nc.scalar.activation(nst[:, n0 + 8:n0 + 10], nst[:, n0:n0 + 2], ACT.Sqrt,
                                         bias=cconst("eps_rms"), scale=1.0 / width).then_inc(*std_ready.more())

            act.wait_ge(*x_ready.at(-1))
            mean_square(x3, D, 0)
            mean_square(mem2, D, 2)
            gains("premix", 0, xT3, lambda c: colp("g_pre_mix", c, COL2), None)
            for i in range(3):
                evacuate(("c", i), cz[:, :, i * T:i * T + T])
            act.wait_ge(*when_read(("c", 2)))
            for lo, w, n0 in ((0, 384, 4), (384, 256, 6)):
                mean_square(cz[:, :, lo:lo + w], w, n0)
            gains("mem2T", 0, memT3, lambda c: colp("g_mem", c, COL2), None)
            for i in range(3):
                act.wait_ge(*when_full(("cT", i)))
                src = bank_of(("cT", i))
                for c in range(2):
                    k = 2 * i + c
                    if k < 5:
                        g = colp("q_norm", k, COL2) if k < 3 else colp("kv_norm", k - 3, COL2)
                        ins = nc.scalar.activation(cT[:, k, :], src[:, c * T:c * T + T], ACT.Copy, scale=g)
                    else:
                        ins = nc.scalar.activation(kraw[64:96, :], src[64:96, c * T:c * T + T], ACT.Copy)
                ins.then_inc(*read(("cT", i)))
            act.wait_ge(*angle_ready.at(0))
            nc.scalar.activation(sin2[64:96, 0:T], angle[64:96, :], ACT.Sin)
            nc.scalar.activation(sin2[64:96, T:2 * T], angle[64:96, :], ACT.Sin)
            nc.scalar.activation(half_sine[64:96, :], angle[64:96, :], ACT.Sin, scale=0.5).then_inc(*sin_ready.more())
            for i in range(4):
                act.wait_ge(*when_full(("uq", i)))
                src = bank_of(("uq", i))
                nc.scalar.activation(qm[0:96, 2 * i:2 * i + 2, :],
                                             src[0:96, :].rearrange("p (c w) -> p c w", w=T), ACT.Copy).then_inc(*read(("uq", i)))
            for i in range(2):
                act.wait_ge(*when_full(("uk", i)))
                src = bank_of(("uk", i))
                for par in range(2):
                    ins = nc.scalar.activation(km[0:64, 4 * i + par:4 * i + par + 3:2, :],
                                               src[64 * par:64 * par + 64, :].rearrange("p (c w) -> p c w", w=T),
                                               ACT.Copy)
                ins.then_inc(*read(("uk", i)))
            for i in range(2):
                evacuate(("uv", i), vm[:, :, i * T:i * T + T])
            attention("mla", mla_fillers)
            for name, dst in (("dq", dq), ("dk", dk)):
                for i in range(6):
                    evacuate((name, i), dst[:, 2 * i:2 * i + 2, :])
            for i in range(6):
                evacuate(("dv", i), dv[:, :, i * T:i * T + T])
            attention("dil", dil_fillers)
            attention("mem", mem_fillers)
            for cb in range(4):
                evacuate(("wo", cb), z3[:, :, cb * T:cb * T + T])
            act.wait_ge(*when_read(("wo", 3)))
            mean_square(z3, D, 0)
            act.wait_ge(*z_ready.at(0))
            mean_square(x3, D, 2)
            gains("preffn", 0, xT3, lambda c: colp("g_pre_ffn", c, COL2), None)
            ffn(True, COL2, "conv_w", "conv_b")
            for cb in range(4):
                evacuate(("down", cb), z3[:, :, cb * T:cb * T + T])
            act.wait_ge(*when_read(("down", 3)))
            mean_square(z3, D, 4)


        @block.vector
        def _(dve):
            def halves(src):
                return src[:, :].rearrange("p (c w) -> p c w", w=T)

            def gains(name, dst, gain, bias):
                for i in (1, 3):
                    dve.wait_ge(*when_full((name, i)))
                    src = bank_of((name, i))
                    for c in range(2):
                        part, o = src[:, c * T:c * T + T], dst[:, 2 * i + c, :]
                        if gain is None:
                            ins = nc.vector.tensor_copy(o, part)
                        elif bias is None:
                            ins = nc.vector.tensor_scalar(o, part, gain(2 * i + c), None, ALU.mult)
                        else:
                            ins = nc.vector.tensor_scalar(o, part, gain(2 * i + c), bias(2 * i + c), ALU.mult, ALU.add)
                    ins.then_inc(*read((name, i)))

            bn = nst[:, 24:48].rearrange("p (t h s) -> p t h s", t=2, h=2)

            def statistics(half):
                for t in range(2):
                    ins = nc.vector.bn_stats(bn[:, t, half, :], z3[:, t, half * 512:half * 512 + 512])
                return ins

            def normalise(n):
                statistics(1).then_inc(*dve_step.more())
                dve.wait_ge(*dve_step.last())
                nc.vector.memset(nst[:, 63:64], 0.0)
                for t in range(2):
                    ins = nc.vector.bn_aggr(nst[:, 48 + 2 * t:50 + 2 * t], bn[:, t, :, :])
                ins.then_inc(*var_ready.more())
                dve.wait_ge(*std_ready.at(n))
                nc.vector.reciprocal(nst[:, 54:56], nst[:, 52:54]).then_inc(*dve_step.more())
                dve.wait_ge(*dve_step.last())
                for t in range(2):
                    nc.vector.tensor_scalar(z3[:, t, :], z3[:, t, :], nst[:, 48 + 2 * t:49 + 2 * t],
                                                nst[:, 54 + t:55 + t], ALU.subtract, ALU.mult).then_inc(*xhat_ready.more())

            def residual_norm(name, k, n):
                dve.wait_ge(*x_ready.at(k))
                for cb in range(4):
                    dve.wait_ge(*when_full((name, cb)))
                    src = bank_of((name, cb))
                    at = slice(cb * T, cb * T + T)
                    nc.vector.scalar_tensor_tensor(z3[:, :, at], x3[:, :, at], ALPHA, halves(src),
                                                           ALU.mult, ALU.add).then_inc(*read((name, cb)))
                    if cb == 1:
                        dve.wait_ge(*when_read((name, cb)))
                        statistics(0)
                dve.wait_ge(*when_read((name, 3)))
                normalise(n)

            def rope(n, rot, x_raw, cosine, sine, dst, sc_a, sc_b):
                dve.wait_ge(*when_full(rot))
                src = bank_of(rot)
                if n > 0:
                    dve.wait_ge(*rope_ready.at(n - 1))
                nc.vector.tensor_tensor(sc_a, x_raw, cosine, ALU.mult)
                nc.vector.tensor_tensor(sc_b, src[:, :], sine, ALU.mult).then_inc(*read(rot))
                dve.wait_ge(*when_read(rot))
                nc.vector.tensor_tensor(dst, sc_a, sc_b, ALU.add).then_inc(*rope_ready.more())

            def maxima(j):
                name, i = ORDER[stage.kind][j]
                number = NUM[stage.kind][0]
                if name in ("na", "mla", "dil"):
                    need_exp_buffer(dve, j)
                for g in range(parts_of(name)):
                    n = number[(j, g)]
                    need_score = n
                    src = sc[n % 2]
                    e = e_ring[:, (j % 3) * 1152:(j % 3) * 1152 + 1152]
                    if name == "dil":
                        nc.vector.tensor_scalar(dbias[:, g % 2, :], distm[:, g, :], -float(SLOPES[g, i]), None,
                                                       ALU.mult).then_inc(*dve_step.more())
                        dve.wait_ge(*dve_step.last())
                    dve.wait_ge(*sc_full.at(need_score))
                    if name == "na":
                        for t in range(2):
                            j0 = 2 * (1 - t)
                            ins = nc.vector.scalar_tensor_tensor(
                                e[:, t * T:t * T + T], src[:, t * T:t * T + T], SCALE[name],
                                bias_tab[:, i, j0:j0 + 4, :].rearrange("p j k -> p (j k)"), ALU.mult, ALU.add)
                    elif name == "mla":
                        ins = nc.vector.scalar_tensor_tensor(e[:, 0:384], src[:, 0:384], SCALE[name],
                                                             const[:, CONST["causal"]:CONST["causal"] + 384],
                                                             ALU.mult, ALU.add)
                    elif name == "dil":
                        ins = nc.vector.scalar_tensor_tensor(e[:, g * 384:g * 384 + 384], src[:, 0:384], SCALE[name],
                                                             dbias[:, g % 2, :], ALU.mult, ALU.add)
                    if name in ("na", "mla", "dil"):
                        ins.then_inc(*sc_read.more())
                if name in ("na", "mla", "dil"):
                    dve.wait_ge(*sc_read.last())
                for t in range(2):
                    lo, hi = spans(name)[t]
                    view = exp_views(j, t) if name in ("na", "mla", "dil") else src[:, lo:hi]
                    ins = nc.vector.tensor_reduce(st("mx", j, t, t + 1), view, AX.XY if name == "dil" else AX.X,
                                                  ALU.max)
                ins.then_inc(*dve_step.more())
                dve.wait_ge(*dve_step.last())
                k = -1.0 if name in ("na", "mla", "dil") else -SCALE[name]
                nc.vector.tensor_scalar(st("nm", j), st("mx", j), k, None, ALU.mult).then_inc(*nmax.more())

            def normed(j):
                name, i = ORDER[stage.kind][j]
                dve.wait_ge(*exp_done.at(j))
                nc.vector.reciprocal(st("rec", j), st("sum", j)).then_inc(*dve_step.more())
                dve.wait_ge(*dve_step.last())
                if name == "da" and i % 2 == 0:
                    return
                if name == "da":
                    nc.vector.tensor_scalar(st("rec", j), st("rec", j), nst[:, 60:61], None, ALU.mult).then_inc(*dve_step.more())
                    dve.wait_ge(*dve_step.last())
                    for t in range(2):
                        ins = nc.vector.tensor_scalar(exp_views(j, t), exp_views(j, t), st("rec", j, t, t + 1), None,
                                                      ALU.mult)
                    ins.then_inc(*dve_step.more())
                    dve.wait_ge(*dve_step.last())
                    for t in range(2):
                        ins = nc.vector.scalar_tensor_tensor(exp_views(j, t), exp_views(j - 1, t),
                                                             st("rec", j - 1, t, t + 1), exp_views(j, t),
                                                             ALU.mult, ALU.add)
                else:
                    for t in range(2):
                        ins = nc.vector.tensor_scalar(exp_views(j, t), exp_views(j, t), st("rec", j, t, t + 1), None,
                                                      ALU.mult)
                ins.then_inc(*p_ready.more())

            def filler(key):
                kind, i = key
                if kind == "hc":
                    dve.wait_ge(*when_read(("gc", i)))
                    dve.wait_ge(*when_full(key))
                    src = bank_of(key)
                    nc.vector.tensor_tensor(cin[:, 2 * i:2 * i + 2, :], gc[:, 2 * i:2 * i + 2, :], halves(src),
                                                    ALU.mult).then_inc(*read(key))

            def attention(name, fillers, at_step=None, extra=None):
                js = set_jobs(name)
                for step in range(len(js) + 2):
                    if step < len(js):
                        maxima(js[step])
                    for key in fillers[step]:
                        filler(key)
                    if 1 <= step <= len(js):
                        normed(js[step - 1])
                    if step == at_step:
                        extra()

            def gated_conv():
                dve.wait_ge(*x_ready.at(-1))
                dve.wait_ge(*when_read(("hc", 1)))
                dve.wait_ge(*when_read(("gb", 0)))
                dve.wait_ge(*when_read(("gb", 1)))
                w = lambda c, k: colp("sc_w", 3 * c + k)
                for c in range(4):
                    ins = nc.vector.tensor_scalar(conv_tmp[:, c, :], cin[:, c, :], w(c, 1), None, ALU.mult)
                ins.then_inc(*dve_step.more())
                dve.wait_ge(*dve_step.last())
                for c in range(4):
                    ins = nc.vector.scalar_tensor_tensor(conv_tmp[:, c, 1:T], cin[:, c, 0:T - 1], w(c, 0),
                                                         conv_tmp[:, c, 1:T], ALU.mult, ALU.add)
                ins.then_inc(*dve_step.more())
                dve.wait_ge(*dve_step.last())
                for c in range(4):
                    ins = nc.vector.scalar_tensor_tensor(conv_tmp[:, c, 0:T - 1], cin[:, c, 1:T], w(c, 2),
                                                         conv_tmp[:, c, 0:T - 1], ALU.mult, ALU.add)
                ins.then_inc(*dve_step.more())
                dve.wait_ge(*dve_step.last())
                nc.vector.tensor_tensor(yT3[:, 8:12, :], conv_tmp, gb, ALU.mult).then_inc(*yc_ready.more())

            def merge():
                for cb in range(4):
                    for br in range(3):
                        dve.wait_ge(*when_full(("branch", cb, br)))
                        src = bank_of(("branch", cb, br))
                        gate = big3[:, 8 * br + 2 * cb:8 * br + 2 * cb + 2, :]
                        acc = merged[:, 2 * cb:2 * cb + 2, :]
                        if br == 0:
                            nc.vector.tensor_tensor(acc, gate, halves(src), ALU.mult).then_inc(*read(("branch", cb, br)))
                            continue
                        tmp = merge_tmp[:, br - 1, :].rearrange("p (c w) -> p c w", w=T)
                        nc.vector.tensor_tensor(tmp, gate, halves(src), ALU.mult).then_inc(*read(("branch", cb, br)))
                        dve.wait_ge(*when_read(("branch", cb, br)))
                        nc.vector.tensor_tensor(acc, acc, tmp, ALU.add).then_inc(*(merge_step if br == 1 else merged_ready).more())
                        if br == 1:
                            dve.wait_ge(*merge_step.at(cb))

            def ffn(gates_too, packed, w):
                for i in range(FPAIR + 1):
                    if i < FPAIR:
                        for k, which in enumerate(("gt", "up") if gates_too else ("gt",)):
                            dve.wait_ge(*conv_init.at(2 * i + k if gates_too else i))
                            src = ps[fill_of((which, i))[0]]
                            for turn in range(2):
                                for c in range(2):
                                    ch = (k * FC if gates_too else 0) + 2 * i + c
                                    s, d = src[:, c * T:c * T + T], cbuf(i % 2, k)[:, c * T:c * T + T]
                                    if gates_too:
                                        shift, tap = turn + 1, 1 - turn
                                        s, d = s[:, 0:T - shift], d[:, shift:T]
                                    else:
                                        s, d, tap = ((s[:, 0:T - 1], d[:, 1:T], 0), (s[:, 1:T], d[:, 0:T - 1], 2))[turn]
                                    ins = nc.vector.scalar_tensor_tensor(d, s, colp(w, 3 * ch + tap, packed), d,
                                                                         ALU.mult, ALU.add)
                                if turn == 0:
                                    ins.then_inc(*dve_step.more())
                                    dve.wait_ge(*dve_step.last())
                            ins.then_inc(*read((which, i)))
                    if i >= 1:
                        dve.wait_ge(*silu_done.at(i - 1))
                        dst = big[:, 2 * (i - 1) * T:2 * i * T]
                        if gates_too:
                            dve.wait_ge(*when_read(("up", i - 1)))
                            nc.vector.tensor_tensor(dst, sbuf(i - 1), cbuf((i - 1) % 2, 1), ALU.mult).then_inc(*act_ready.more())
                        else:
                            dve.wait_ge(*when_full(("up", i - 1)))
                            src = bank_of(("up", i - 1))
                            nc.vector.tensor_tensor(dst, sbuf(i - 1), src[:, :], ALU.mult).then_inc(*read(("up", i - 1)))

            def inverse_std(n, n0):
                dve.wait_ge(*std_ready.at(n))
                nc.vector.reciprocal(nst[:, n0 + 16:n0 + 18], nst[:, n0 + 8:n0 + 10]).then_inc(*dve_step.more())
                dve.wait_ge(*dve_step.last())

            def add_normed(n, n0, gain_rows, done):
                inverse_std(n, n0)
                dve.wait_ge(*rows_in.at(gain_rows))
                for t in range(2):
                    ins = nc.vector.scalar_tensor_tensor(z3[:, t, :], z3[:, t, :], nst[:, n0 + 16 + t:n0 + 17 + t],
                                                         rows[:, 0:D], ALU.mult, ALU.mult)
                ins.then_inc(*dve_step.more())
                dve.wait_ge(*dve_step.last())
                nc.vector.tensor_tensor(x_tok[:, :], x_tok[:, :], z_tok[:, :], ALU.add).then_inc(*done.more())

            stage.enter("pro")
            dve.wait_ge(*const_in.at(0))
            dve.wait_ge(*xin.at(1))
            statistics(0)
            normalise(0)
            gains("memT", memT3, None, None)
            gains("xT0", xT3, lambda c: cconst("emb_g", c), lambda c: cconst("emb_b", c))

            with dve.Fori(0, DEPTH) as l:
                stage.enter("layer", l)
                dve.wait_ge(*cols_in.at(0))
                lam = col[:, COL1["lam"]:COL1["lam"] + 256].rearrange("p (a b w) -> p a b w", a=2, b=2)
                prod = e_ring[:, 0:128].rearrange("p (a w) -> p a w", a=2)
                nc.vector.tensor_tensor(prod, lam[:, :, 0, :], lam[:, :, 1, :], ALU.mult).then_inc(*dve_step.more())
                dve.wait_ge(*dve_step.last())
                nc.vector.tensor_reduce(nst[:, 56:58], prod, AX.X, ALU.add).then_inc(*lam_sum.more())
                nc.vector.tensor_tensor(nst[:, 61:62], colp("subln"), colp("one_minus"), ALU.mult)
                for n in range(4):
                    dst = (qa, ka)[n // 2][:, 2 * (n % 2):2 * (n % 2) + 2, :].rearrange("p c w -> p (c w)")
                    x_raw = raw[:, 2 * n:2 * n + 2, :].rearrange("p c w -> p (c w)")
                    rope(n, ("rot", n), x_raw, cos2, sin2, dst, scratch[:, 0, :], scratch[:, 1, :])
                dve.wait_ge(*lam_exp.at(0))
                nc.vector.tensor_tensor(nst[:, 62:63], nst[:, 59:60], nst[:, 58:59], ALU.subtract).then_inc(*dve_step.more())
                dve.wait_ge(*dve_step.last())
                nc.vector.tensor_tensor(nst[:, 60:61], nst[:, 62:63], colp("lam_init"), ALU.subtract).then_inc(*dve_step.more())
                dve.wait_ge(*dve_step.last())
                attention("da", da_fillers, 8, gated_conv)
                dve.wait_ge(*bias_ready.at(0))
                attention("na", na_fillers)
                dve.wait_ge(*when_read(("ss", 0)))
                dve.wait_ge(*when_read(("ss", 1)))
                nc.vector.reciprocal(ya_rstd, ya_rstd).then_inc(*dve_step.more())
                dve.wait_ge(*dve_step.last())
                nc.vector.scalar_tensor_tensor(yT[:, 0:4 * T], yT[:, 0:4 * T], nst[:, 61:62],
                                                   z_tok[:, 4 * T:8 * T], ALU.mult, ALU.mult).then_inc(*ya_ready.more())
                merge()
                residual_norm("mix", -1, 0)
                gains("ln0", xT3, lambda c: colp("ln_g", c), lambda c: colp("ln_b", c))
                attention("xa", xa_fillers)
                residual_norm("xo", 0, 1)
                gains("ln1", xT3, lambda c: colp("ln_g", DC + c), lambda c: colp("ln_b", DC + c))
                ffn(False, COL1, "ffn_w")
                residual_norm("down", 1, 2)
                gains("ln2", xT3, lambda c: colp("ln_g", 2 * DC + c), lambda c: colp("ln_b", 2 * DC + c))

            stage.enter("post")
            dve.wait_ge(*x_ready.at(-1))
            inverse_std(0, 0)
            for t in range(2):
                nc.vector.tensor_scalar(z3[:, t, :], x3[:, t, :], nst[:, 16 + t:17 + t], None, ALU.mult).then_inc(*xhat_ready.more())
            inverse_std(1, 2)
            for t in range(2):
                nc.vector.tensor_scalar(mem2[:, t, :], mem2[:, t, :], nst[:, 18 + t:19 + t], None, ALU.mult).then_inc(*xhat_ready.more())
            dve.wait_ge(*cols_in.at(0))
            gains("premix", xT3, lambda c: colp("g_pre_mix", c, COL2), None)
            dve.wait_ge(*pos_in.at(0))
            ang, trn, red = turns[64:96, :], half_sine[64:96, :], angle[64:96, :]
            nc.vector.tensor_copy(ang, pos_int[64:96, :]).then_inc(*dve_step.more())
            dve.wait_ge(*dve_step.last())
            nc.vector.tensor_scalar(ang, ang, const[64:96, CONST["inv"]:CONST["inv"] + 1], None, ALU.mult).then_inc(*dve_step.more())
            dve.wait_ge(*dve_step.last())
            nc.vector.tensor_scalar(trn, ang, 1.0 / (2 * np.pi), ROUND, ALU.mult, ALU.add).then_inc(*dve_step.more())
            dve.wait_ge(*dve_step.last())
            nc.vector.tensor_scalar(trn, trn, ROUND, None, ALU.subtract).then_inc(*dve_step.more())
            dve.wait_ge(*dve_step.last())
            nc.vector.scalar_tensor_tensor(red, trn, -TWO_PI[0], ang, ALU.mult, ALU.add).then_inc(*dve_step.more())
            dve.wait_ge(*dve_step.last())
            nc.vector.scalar_tensor_tensor(red, trn, -TWO_PI[1], red, ALU.mult, ALU.add).then_inc(*dve_step.more())
            dve.wait_ge(*dve_step.last())
            nc.vector.scalar_tensor_tensor(red, trn, -TWO_PI[2], red, ALU.mult, ALU.add).then_inc(*dve_step.more())
            dve.wait_ge(*dve_step.last())
            nc.vector.tensor_scalar(red, red, PI_BELOW, -PI_BELOW, ALU.min, ALU.max).then_inc(*angle_ready.more())
            for n, (lo, w) in enumerate(((0, 384), (384, 256))):
                inverse_std(2 + n, 4 + 2 * n)
                for t in range(2):
                    ins = nc.vector.tensor_scalar(cz[:, t, lo:lo + w], cz[:, t, lo:lo + w],
                                                  nst[:, 20 + 2 * n + t:21 + 2 * n + t], None, ALU.mult)
            ins.then_inc(*xhat_ready.more())
            gains("mem2T", memT3, lambda c: colp("g_mem", c, COL2), None)
            dve.wait_ge(*sin_ready.at(0))
            nc.vector.tensor_tensor(turns[64:96, :], half_sine[64:96, :], half_sine[64:96, :], ALU.mult).then_inc(*dve_step.more())
            dve.wait_ge(*dve_step.last())
            for c in range(2):
                ins = nc.vector.tensor_scalar(cos2[64:96, c * T:c * T + T], turns[64:96, :], -2.0, 1.0, ALU.mult, ALU.add)
            ins.then_inc(*dve_step.more())
            dve.wait_ge(*dve_step.last())
            for n in range(4):
                part = qm[64:96, 2 * n:2 * n + 2, :].rearrange("p c w -> p (c w)")
                src_key = ("rot2", n)
                dve.wait_ge(*when_full(src_key))
                src = bank_of(src_key)
                if n > 0:
                    dve.wait_ge(*rope_ready.at(n - 1))
                nc.vector.tensor_tensor(scratch[64:96, 0, :], part, cos2[64:96, :], ALU.mult)
                nc.vector.tensor_tensor(scratch[64:96, 1, :], src[64:96, :], sin2[64:96, :], ALU.mult).then_inc(*read(src_key))
                dve.wait_ge(*when_read(src_key))
                nc.vector.tensor_tensor(part, scratch[64:96, 0, :], scratch[64:96, 1, :], ALU.add).then_inc(*rope_ready.more())
            dve.wait_ge(*when_full(("rot2", 4)))
            src = bank_of(("rot2", 4))
            dve.wait_ge(*rope_ready.at(3))
            nc.vector.tensor_tensor(scratch[64:96, 0, 0:T], kraw[64:96, :], cos2[64:96, 0:T], ALU.mult)
            nc.vector.tensor_tensor(scratch[64:96, 1, 0:T], src[64:96, 0:T], sin2[64:96, 0:T], ALU.mult).then_inc(*read(("rot2", 4)))
            dve.wait_ge(*when_read(("rot2", 4)))
            nc.vector.tensor_tensor(km[64:96, :, :], scratch[64:96, 0:1, 0:T].to_broadcast([32, 8, T]),
                                        scratch[64:96, 1:2, 0:T].to_broadcast([32, 8, T]), ALU.add).then_inc(*rope_ready.more())
            attention("mla", mla_fillers)
            dve.wait_ge(*dil_in.at(0))
            attention("dil", dil_fillers)
            attention("mem", mem_fillers)
            merge()
            for cb in range(4):
                dve.wait_ge(*when_read(("wo", cb)))
            add_normed(4, 0, 0, z_ready)
            inverse_std(5, 2)
            for t in range(2):
                nc.vector.tensor_scalar(z3[:, t, :], x3[:, t, :], nst[:, 18 + t:19 + t], None, ALU.mult).then_inc(*xhat_ready.more())
            gains("preffn", xT3, lambda c: colp("g_pre_ffn", c, COL2), None)
            ffn(True, COL2, "conv_w")
            for cb in range(4):
                dve.wait_ge(*when_read(("down", cb)))
            add_normed(6, 4, 1, out_ready)

        @block.gpsimd
        def _(pool):
            def load_rows(k, first=True):
                src = bass.AP(a["ln_rows"].tensor, k * (2 * D), [[0, P], [1, 2 * D]])
                pool.dma_start(rows[:, :], src).then_inc(*rows_in.more())

            def next_x(xhat, rows_n, n):
                pool.wait_ge(*rows_in.at(rows_n))
                pool.wait_ge(*xhat_ready.at(xhat))
                for t in range(2):
                    ins = nc.gpsimd.tensor_tensor(x3[:, t, :], z3[:, t, :], rows[:, 0:D], ALU.mult)
                ins.then_inc(*pool_step.more())
                pool.wait_ge(*pool_step.last())
                for t in range(2):
                    ins = nc.gpsimd.tensor_tensor(x3[:, t, :], x3[:, t, :], rows[:, D:2 * D], ALU.add)
                ins.then_inc(*x_ready.more())
                pool.wait_ge(*x_ready.at(n))

            stage.enter("pro")
            load_rows(0)
            for l in range(DEPTH):
                for h in range(RPB_H):
                    for s in range(2):
                        src = bass.AP(a["rpb"].tensor,
                                      ((l * RPB_H + h) * RPB_R + NJ - 1 - s) * RPB_C + RPB_C // 2,
                                      [[RPB_C, NJ], [-1, 64], [1, 64]])
                        dst = a["bias_scratch"][l, 64 * s:64 * s + 64, h * NJ * 64:(h + 1) * NJ * 64]
                        pool.dma_start(dst.rearrange("p (j k) -> j p k", j=NJ), src).then_inc(*bias_in.more())
            pool.wait_ge(*const_in.at(0))
            next_x(1, 0, 0)
            pool.wait_ge(*bias_in.at(2 * DEPTH * RPB_H - 1))

            with pool.Fori(0, DEPTH) as l:
                stage.enter("layer", l)
                need_last_phase(pool)
                pool.dma_start(col[:, :], a["cols"][l]).then_inc(*cols_in.more())
                load_rows(1 + 3 * l)
                pool.dma_start(area[:, 36 * T:48 * T], a["bias_scratch"][l]).then_inc(*bias_in.more())
                pool.wait_ge(*bias_in.at(0))
                table = area[:, 36 * T:48 * T].rearrange("p (a k) -> p a k", k=64)
                mask = const[:, CONST["na_mask"]:CONST["na_mask"] + 64].unsqueeze(1).to_broadcast([P, 8 * NJ, 64])
                nc.gpsimd.tensor_tensor(table, table, mask, ALU.add).then_inc(*bias_ready.more())
                for k in range(3):
                    if k:
                        load_rows(1 + k + 3 * l)
                    next_x(2 * k + 1, k, k)

            stage.enter("post")
            need_last_phase(pool)
            pool.dma_start(mem2, a["mem_2"].rearrange("b (t p) d -> p (b t) d", p=P)).then_inc(*mem2_in.more())
            pool.dma_start(col[:, :], a["cols"][DEPTH]).then_inc(*cols_in.more())
            pos = bass.AP(a["positions_2"].tensor, 0, [[0, 32], [1, T]])
            pool.dma_start(pos_int[64:96, :], pos).then_inc(*pos_in.more())
            pool.dma_start(rows[:, 0:3 * 384], a["distm"]).then_inc(*dil_in.more())
            pool.wait_ge(*nmax.at(11))
            load_rows(7)
            pool.wait_ge(*z_ready.at(0))
            load_rows(8)

        @block.sync
        def _(sp):
            def load_unit(g, slot):
                dst = ring[:, slot * UNIT_TILES * TILE_N:(slot + 1) * UNIT_TILES * TILE_N]
                sp.dma_start(dst, a["stream"][g]).then_inc(*landed[slot].more())

            stage.enter("pro")
            sp.dma_start(const[:, :], a["const"]).then_inc(*const_in.more())
            sp.dma_start(z3, a["x"].rearrange("b (t p) d -> p (b t) d", p=P)).then_inc(*xin.more())
            sp.dma_start(mem_tok, a["mem"].rearrange("b (t p) d -> p (b t) d", p=P)).then_inc(*xin.more())
            for u in range(RING):
                load_unit(u, u)

            def stream(units, total, first):
                for u in range(RING, total):
                    if (stage.kind, u - RING) not in LAST_USE:
                        assert stage.kind == "layer" and u - RING == MEM_UNITS_1
                    else:
                        b, n = LAST_USE[(stage.kind, u - RING)]
                        sp.wait_ge(*full[b].at(n))
                    if stage.kind == "post" or u != MEM_UNITS_1:
                        load_unit(first + u, u % RING)

            with sp.Fori(0, DEPTH) as l:
                stage.enter("layer", l)
                stream(MEM_UNITS_1, UNITS_1 + RING, l * UNITS_1)
            stage.enter("post")
            stream(UNITS_2, UNITS_2, DEPTH * UNITS_1)
            sp.wait_ge(*out_ready.at(0))
            sp.dma_start(out.rearrange("b (t p) d -> p (b t) d", p=P), x3).then_inc(*out_done.more())
            sp.wait_ge(*out_done.at(0))

    counted = {k: tuple(v) for k, v in stage.seen.items()}
    assert counted == COUNTS, counted
    return stage


def tiles_of(w):
    k, n = w.shape
    if n % TILE_N:
        w = np.concatenate([w, np.zeros((k, TILE_N - n % TILE_N), w.dtype)], 1)
    return w.reshape(k // P, P, -1, TILE_N).transpose(2, 0, 1, 3).reshape(-1, P, TILE_N)


def units_of(tiles, units):
    t = np.concatenate(tiles)
    t = np.concatenate([t, np.zeros((units * UNIT_TILES - len(t), P, TILE_N), t.dtype)])
    return t.reshape(units, UNIT_TILES, P, TILE_N).transpose(0, 2, 1, 3).reshape(units, P, UNIT_TILES * TILE_N)


def stream_of(i):
    out = []
    for l in range(DEPTH):
        w = i["w_in"][l]
        cuts = {n: w[:, 512 * k:512 * k + 512] for k, n in enumerate(("qa", "ka", "va", "qn", "kn", "vn", "gb", "gc", "hc"))}
        t = [tiles_of(cuts[n]) for n in ("qa", "ka", "va", "qn", "kn", "vn", "gc", "hc", "gb")]
        t.append(tiles_of(w[:, 4608:]))
        t += branch_tiles(i["w_branch"][l])
        kv = i["xa_kv"][l]
        t += [tiles_of(i["w_mix_out"][l]), tiles_of(kv[:, :D]), tiles_of(i["xa_q"][l]), tiles_of(kv[:, D:]),
              tiles_of(i["xa_o"][l])]
        t += pair_tiles(i["ffn_w_in"][l], True)
        t.append(tiles_of(i["ffn_w_out"][l]))
        out.append(units_of(t, UNITS_1))
    w = i["w_in_2"][0]
    t = [tiles_of(w[:, 0:672])]
    uq = i["w_uq_2"][0].reshape(384, 4, 192)
    uq = np.concatenate([uq, np.zeros((384, 4, 64), uq.dtype)], 2).reshape(384, 1024)
    ukv = i["w_ukv_2"][0].reshape(256, 8, 128)
    t += [tiles_of(uq), tiles_of(ukv[:, :, :64].reshape(256, 512)), tiles_of(ukv[:, :, 64:].reshape(256, 512))]
    t.append(tiles_of(w[:, 5792:]))
    t += [tiles_of(w[:, 672 + 1536 * k:672 + 1536 * (k + 1)]) for k in range(3)]
    t.append(tiles_of(i["w_mem_kv_2"][0]))
    t.append(tiles_of(w[:, 5280:5792]))
    t += branch_tiles(np.stack([i["w_br_mla_2"][0], i["w_br_dil_2"][0], i["w_br_mem_2"][0]]))
    t.append(tiles_of(i["w_o_2"][0]))
    t += pair_tiles(i["w_ffn_up_2"][0], False)
    t.append(tiles_of(i["w_ffn_down_2"][0]))
    out.append(units_of(t, UNITS_2))
    return np.concatenate(out)


def branch_tiles(w):
    parts = [tiles_of(x).reshape(4, 4, P, TILE_N) for x in w]
    return [parts[br][cb] for cb in range(4) for br in range(3)]


def pair_tiles(w, gate_last):
    a, b = tiles_of(w[:, :FF]), tiles_of(w[:, FF:])
    gate, value = (b, a) if gate_last else (a, b)
    gate, value = gate.reshape(FPAIR, DC, P, TILE_N), value.reshape(FPAIR, DC, P, TILE_N)
    return [x for k in range(FPAIR) for x in (gate[k], value[k])]


def chunked(v):
    return v.reshape(-1, P).T


def cols_of(i):
    pages = np.zeros((DEPTH + 1, P, COL_N), np.float32)

    def put(page, at, name, value):
        pages[page, :, at[name]:at[name] + value.shape[1]] = value

    def taps(w):
        return w.reshape(3, -1, P).transpose(2, 1, 0).reshape(P, -1)

    for l in range(DEPTH):
        lam_init = 0.8 - 0.6 * float(np.exp(-0.3 * l))
        put(l, COL1, "ln_g", chunked(i["ln_g"][l].reshape(-1)))
        put(l, COL1, "ln_b", chunked(i["ln_b"][l].reshape(-1)))
        put(l, COL1, "subln", chunked(i["subln_g"][l]))
        put(l, COL1, "one_minus", np.full((P, 1), 1.0 - lam_init, np.float32))
        put(l, COL1, "lam_init", np.full((P, 1), lam_init, np.float32))
        put(l, COL1, "sc_w", taps(i["sc_conv_w"][l]))
        put(l, COL1, "ffn_w", taps(i["ffn_conv_w"][l]))
        put(l, COL1, "ffn_b", chunked(i["ffn_conv_b"][l]))
        lam = np.concatenate([i["lam_q1"][l], i["lam_k1"][l], i["lam_q2"][l], i["lam_k2"][l]])
        put(l, COL1, "lam", np.broadcast_to(lam, (P, 256)))
    for name, key in (("g_mem", "g_mem_2"), ("g_pre_mix", "g_pre_mix_2"), ("q_norm", "mla_q_norm_2"),
                      ("kv_norm", "mla_kv_norm_2"), ("b_gate", "b_gate_2"), ("g_pre_ffn", "g_pre_ffn_2"),
                      ("conv_b", "conv_b_2")):
        put(DEPTH, COL2, name, chunked(i[key][0]))
    put(DEPTH, COL2, "conv_w", taps(i["conv_w_2"][0]))
    return pages


def const_of(i):
    c = np.zeros((P, CONST_N), np.float32)

    def put(name, value):
        c[:value.shape[0], CONST[name]:CONST[name] + value.shape[1]] = value

    put("ident", np.eye(P))
    half = 32
    rot = np.zeros((P, P))
    for m in range(0, P, 64):
        for d in range(half):
            rot[m + d + half, m + d] = -1
            rot[m + d, m + d + half] = 1
    put("rot1", rot)
    inv = np.float32(10000.0) ** (-np.arange(half, dtype=np.float32) * np.float32(2.0) / np.float32(64))
    ang = (np.arange(T, dtype=np.float32)[None, :] * inv.astype(np.float32)[:, None]).astype(np.float32)
    put("cos", np.tile(np.cos(ang.astype(np.float64)), (4, 2)))
    put("sin", np.tile(np.sin(ang.astype(np.float64)), (4, 2)))
    put("ones", np.ones((P, P)))
    q, k = np.arange(P)[:, None] % 64, np.arange(64)[None, :]
    start = np.clip(q - 8, 0, 48)
    put("na_mask", np.where((k >= start) & (k < start + 16), 0.0, NEG))
    qi, ki = np.arange(P)[:, None], np.arange(P)[None, :]
    diag = np.where(ki <= qi, 0.0, NEG)
    put("causal", np.concatenate([diag, np.zeros((P, P)), diag], 1))
    rot = np.zeros((P, 96))
    for d in range(16):
        rot[64 + d + 16, 64 + d] = -1
        rot[64 + d, 64 + d + 16] = 1
    put("rot2", rot)
    inv2 = np.float32(10000.0) ** (-np.arange(16, dtype=np.float32) / np.float32(16))
    put("inv", np.tile(inv2, 8)[:, None])
    put("eps_ln", np.full((P, 1), EPS_LN))
    put("eps_rms", np.full((P, 1), EPS_RMS))
    put("emb_g", chunked(i["emb_ln_g"]))
    put("emb_b", chunked(i["emb_ln_b"]))
    return c


def distances():
    out = []
    for window, d in ((128, 1), (512, 4), (2048, 16)):
        for q0, n in ((0, P), (P, T)):
            dist = (q0 + np.arange(P))[:, None] - np.arange(n)[None, :]
            ok = (dist >= 0) & (dist % d == 0) & (dist <= window)
            out.append(np.where(ok, dist, 1e33))
    return np.concatenate(out, 1).astype(np.float32)


def kernel(**inputs):
    import concourse.bacc as _bacc
    from concourse.bass_utils import run_bass_kernel_spmd as _run

    i = {k: np.ascontiguousarray(v) for k, v in inputs.items()}
    zero = np.zeros(D, np.float32)
    rows = np.concatenate([i["emb_ln_g"], i["emb_ln_b"]]
                          + [x for l in range(DEPTH) for k in range(3) for x in (i["ln_g"][l, k], i["ln_b"][l, k])]
                          + [i["g_post_mix_2"][0], zero, i["g_post_ffn_2"][0], zero])
    arrays = {"x": i["x"], "mem": i["mem"], "mem_2": i["mem_2"], "positions_2": i["positions_2"],
              "rpb": i["rpb"].reshape(-1), "stream": stream_of(i), "cols": cols_of(i), "const": const_of(i),
              "distm": distances(), "ln_rows": rows}
    nc = _bacc.Bacc("TRN2", target_bir_lowering=False, num_devices=1)
    aps = {n: nc.dram_tensor(f"in_{n}", v.shape, mybir.dt.from_np(v.dtype), kind="ExternalInput").ap()
           for n, v in arrays.items()}
    aps["bias_scratch"] = nc.dram_tensor("bias_scratch", (DEPTH, P, RPB_H * NJ * 64), F32, kind="Internal").ap()
    out = nc.dram_tensor("out_x", (1, T, D), F32, kind="ExternalOutput").ap()
    build(nc, aps, out)
    r = _run(nc, [{f"in_{n}": v for n, v in arrays.items()}], core_ids=[0])
    return r.results[0]["out_x"]
```

```python
from contextlib import ExitStack

import numpy as np
import concourse.bass as bass
from concourse import mybir

F32 = mybir.dt.float32
F32R = mybir.dt.float32r
I32 = mybir.dt.int32
ACT = mybir.ActivationFunctionType
ALU = mybir.AluOpType
AX = mybir.AxisListType

P = 128
T = 256
D = 1024
DC = D // P
DEPTH = 2
FF = 2816
FC = FF // P
FPAIR = FC // 2
TILE_N = 256
HALF_TILES = 4
HALF_N = HALF_TILES * TILE_N
RAW = 5
SPLIT = 4
HALVES_1 = 178
PERIOD = 180
HALVES_2 = 169
ALPHA = (2.0 * DEPTH) ** 0.25
EPS_LN = 1e-5
EPS_RMS = 1e-6
NEG = -1e30

ROUND = 1.5 * 2.0 ** 23
TWO_PI = (6.28125, 0.0019350051879882812, 2 * 3.141592653589793 - 6.28125 - 0.0019350051879882812)
PI_BELOW = 3.1415925

RPB_H, RPB_R, RPB_C = 8, 15, 31
NJ = 6


def columns(*parts):
    at, n = {}, 0
    for name, width in parts:
        at[name] = n
        n += width
    return at, n


CONST, CONST_N = columns(("ident", P), ("rot1", P), ("cos", 2 * T), ("sin", 2 * T), ("ones", P), ("na_mask", 64),
                         ("causal", 384), ("rot2", 96), ("inv", 1), ("eps_ln", 1), ("eps_rms", 1),
                         ("emb_g", DC), ("emb_b", DC))
COL1, COL1_N = columns(("ln_g", 3 * DC), ("ln_b", 3 * DC), ("subln", 1), ("one_minus", 1), ("lam_init", 1),
                       ("sc_w", 12), ("ffn_w", 3 * FC), ("ffn_b", FC), ("lam", 256))
COL2, COL2_N = columns(("g_mem", DC), ("g_pre_mix", DC), ("q_norm", 3), ("kv_norm", 2), ("b_gate", 24),
                       ("g_pre_ffn", DC), ("conv_w", 6 * FC), ("conv_b", 2 * FC))
COL_N = max(COL1_N, COL2_N)

SLOPES = np.exp2(-8.0 * np.arange(1, 13, dtype=np.float64) / 12).astype(np.float32).reshape(4, 3).T

COUNTS = {
    "general_full0": (2, 26, 27),
    "general_full1": (2, 26, 26),
    "general_full2": (2, 25, 26),
    "general_full3": (2, 25, 26),
    "weights_half_used": (0, 93, 88),
    "scores_full": (0, 20, 24),
    "probsT_full": (0, 16, 24),
    "attn_out_full": (0, 12, 12),
    "down_full": (0, 4, 4),
    "general_free0": (2, 26, 27),
    "general_free2": (2, 25, 26),
    "std_ready": (1, 3, 7),
    "weights_hi_done": (4, 178, 165),
    "xT_gained": (4, 12, 12),
    "general_free1": (2, 26, 26),
    "general_free3": (2, 25, 26),
    "lam_exp": (0, 1, 0),
    "exp_done": (0, 20, 16),
    "probsT_ready": (0, 16, 24),
    "attn_out_read": (0, 12, 12),
    "yc_hi_ready": (0, 1, 0),
    "ya_sq": (0, 1, 0),
    "attn_out_hi": (0, 8, 8),
    "ya_hi_ready": (0, 1, 1),
    "memT_hi_ready": (0, 2, 0),
    "conv_init": (0, 11, 22),
    "silu_done": (0, 11, 11),
    "squares_done": (0, 0, 7),
    "cT_hi_ready": (0, 0, 3),
    "sin_ready": (0, 0, 1),
    "down_product_in": (0, 0, 4),
    "dve_step": (6, 106, 118),
    "var_ready": (1, 3, 0),
    "xhat_ready": (2, 6, 7),
    "weights_lo_done": (4, 178, 165),
    "lam_sums": (0, 1, 0),
    "rope_ready": (0, 4, 5),
    "neg_max_ready": (0, 20, 16),
    "probs_ready": (0, 16, 16),
    "yc_ready": (0, 4, 0),
    "yc_lo_ready": (0, 1, 0),
    "scores_read": (0, 8, 20),
    "ya_ready": (0, 1, 0),
    "ya_lo_ready": (0, 1, 1),
    "merge_step": (0, 12, 12),
    "merged_ready": (0, 4, 4),
    "memT_lo_ready": (0, 2, 0),
    "ffn_act_ready": (0, 11, 11),
    "angle_ready": (0, 0, 1),
    "z_ready": (0, 0, 1),
    "out_ready": (0, 0, 1),
    "rows_in": (1, 3, 2),
    "bias_in": (32, 1, 0),
    "pool_step": (1, 3, 0),
    "x_ready": (1, 3, 0),
    "cols_in": (0, 1, 1),
    "bias_ready": (0, 1, 0),
    "mem2_in": (0, 0, 1),
    "pos_in": (0, 0, 1),
    "dil_in": (0, 0, 1),
    "const_in": (1, 0, 0),
    "x_in": (2, 0, 0),
    "weights_landed0": (1, 36, 33),
    "weights_landed1": (1, 36, 33),
    "weights_landed2": (1, 36, 33),
    "weights_landed3": (1, 35, 33),
    "weights_landed4": (1, 35, 32),
    "out_done": (0, 0, 1),
}


class Signal:

    def __init__(self, name, sem, unit, stage):
        self.name, self.sem, self.unit, self.stage = name, sem, unit, stage
        self.pro, self.per, self.post = COUNTS.get(name, (0, 0, 0))

    def at(self, n):
        return self.sem, self.unit * (self.stage.base(self) + n + 1)

    def last(self):
        return self.at(self.stage.said[self.name] - 1)

    def more(self):
        self.stage.count(self)
        return self.sem, self.unit


class Stage:

    def __init__(self):
        self.kind, self.layer, self.said, self.seen = "pro", 0, {}, {}

    def enter(self, kind, layer=0):
        self.kind, self.layer, self.said = kind, layer, {}

    def base(self, s):
        if self.kind == "pro":
            return 0
        if self.kind == "layer":
            return s.pro + self.layer * s.per
        return s.pro + DEPTH * s.per

    def count(self, s, k=1):
        self.said[s.name] = self.said.get(s.name, 0) + k
        which = ("pro", "layer", "post").index(self.kind)
        self.seen.setdefault(s.name, [0, 0, 0])[which] += k


def jobs_of(kind):
    sets = {"layer": (("da", 8), ("na", 8), ("xa", 4)), "post": (("mla", 8), ("dil", 4), ("mem", 4))}[kind]
    return [(name, i) for name, n in sets for i in range(n)]


def parts_of(name):
    return 3 if name == "dil" else 1


def build(nc, a, out):
    stage = Stage()
    ctx = ExitStack()
    with ctx:
        def signal(name, unit=1):
            return Signal(name, ctx.enter_context(nc.semaphore(name)), unit, stage)

        sizes = (("raw", RAW * HALF_N), ("w_hi", SPLIT * HALF_N), ("w_lo", SPLIT * HALF_N), ("x", 2 * D), ("z", 2 * D),
                 ("xT_hi", 2 * D), ("xT_lo", 2 * D), ("memT", 2 * D), ("big", 24 * T), ("y", 12 * T),
                 ("exp", 3 * 1152), ("pT", 4 * 512), ("const", CONST_N), ("col", COL_N), ("area", 48 * T),
                 ("stat", 24), ("nst", 64))
        base = -(-nc.sbuf_base // 32) * 32
        top = base
        place = {}
        for name, width in sizes:
            place[name] = top
            top += -(-width // 8) * 32
        arena = ctx.enter_context(nc.sbuf_tensor("arena", [P, (top - nc.sbuf_base) // 4], F32))

        def sb(name, cols, where=None, col0=0, dt=F32):
            return nc.alloc_sbuf_tensor_at(name, [P, cols], dt, offset=place[where or name] + 4 * col0)

        raw_ring = sb("raw_weights", RAW * HALF_N, "raw")
        w_hi = sb("weights_hi", SPLIT * HALF_N, "w_hi", dt=F32R)
        w_lo = sb("weights_lo", SPLIT * HALF_N, "w_lo", dt=F32R)
        x_tok = sb("x_tok", 2 * D, "x")
        z_tok = sb("z_tok", 2 * D, "z")
        xT_hi, xT_lo = (sb(f"xT_{k}_part", 2 * D, f"xT_{k}", dt=F32R) for k in ("hi", "lo"))
        memT = sb("memory_T", 2 * D, "memT")
        big = sb("gates", 24 * T, "big")
        mT_hi, mT_lo = (sb(f"memT_{k}", 8 * T, "big", c, F32R) for k, c in (("hi", 8 * T), ("lo", 16 * T)))
        yT = sb("attn_outputs", 12 * T, "y")
        yb_hi, yb_lo = (sb(f"second_branch_{k}", 4 * T, "y", c, F32R) for k, c in (("hi", 0), ("lo", 4 * T)))
        e_ring = sb("exp_ring", 3 * 1152, "exp")
        pT = sb("probsT_ring", 4 * 512, "pT")
        const = sb("constants", CONST_N, "const")
        col = sb("param_cols", COL_N, "col")
        area = sb("attention_area", 48 * T, "area")
        ya_hi, ya_lo = (sb(f"first_branch_{k}", 4 * T, "area", c, F32R) for k, c in (("hi", 0), ("lo", 4 * T)))
        yc_hi, yc_lo = (sb(f"third_branch_{k}", 4 * T, "area", c, F32R) for k, c in (("hi", 28 * T), ("lo", 32 * T)))
        mg_hi, mg_lo = (sb(f"merged_{k}", 8 * T, "area", c, F32R) for k, c in (("hi", 8 * T), ("lo", 16 * T)))
        xo_hi, xo_lo = (sb(f"memory_out_{k}", 8 * T, "area", c, F32R) for k, c in (("hi", 24 * T), ("lo", 32 * T)))
        rows = area[:, 40 * T:48 * T]
        stat = sb("softmax_stats", 24, "stat")
        nst = sb("norm_stats", 64, "nst")

        def mat(tile, c0, n, w=T):
            return tile[:, c0:c0 + n * w].rearrange("p (c w) -> p c w", w=w)

        x3, z3 = mat(x_tok, 0, 2, D), mat(z_tok, 0, 2, D)
        memT3, big3, yT3 = mat(memT, 0, DC), mat(big, 0, 24), mat(yT, 0, 12)
        XT = mat(xT_hi, 0, DC), mat(xT_lo, 0, DC)
        MT = mat(mT_hi, 0, DC), mat(mT_lo, 0, DC)
        YB = mat(yb_hi, 0, 4), mat(yb_lo, 0, 4)
        YA = mat(ya_hi, 0, 4), mat(ya_lo, 0, 4)
        YC = mat(yc_hi, 0, 4), mat(yc_lo, 0, 4)
        MG = mat(mg_hi, 0, 8), mat(mg_lo, 0, 8)
        XO = mat(xo_hi, 0, 8), mat(xo_lo, 0, 8)
        ident = const[:, CONST["ident"]:CONST["ident"] + P]
        ones = const[:, CONST["ones"]:CONST["ones"] + P]
        cos2 = const[:, CONST["cos"]:CONST["cos"] + 2 * T]
        sin2 = const[:, CONST["sin"]:CONST["sin"] + 2 * T]
        qa, ka = mat(area, 0, 4), mat(area, 4 * T, 4)
        va = mat(area, 8 * T, 2, 512)
        qn, kn = mat(area, 12 * T, 4), mat(area, 16 * T, 4)
        vn = mat(area, 20 * T, 2, 512)
        gb, cin = mat(area, 24 * T, 4), mat(area, 28 * T, 4)
        gc = mat(area, 32 * T, 4)
        bias_tab = area[:, 36 * T:48 * T].rearrange("p (h j k) -> p h j k", h=8, j=NJ)
        conv_tmp = mat(z_tok, 0, 4)
        ya_rstd = mat(z_tok, 4 * T, 4)
        raw = mat(big, 0, 8)
        scratch = mat(e_ring, 2048, 2, 512)
        xq, xk = mat(area, 0, 8), mat(area, 8 * T, 8)
        xv = mat(area, 16 * T, 2, D)
        qm = mat(z_tok, 0, 8)
        km = mat(area, 0, 8)
        vm = mat(area, 8 * T, 2, 512)
        mk, mq = mat(area, 12 * T, 4), mat(area, 16 * T, 4)
        mv = mat(area, 20 * T, 2, 512)
        dq, dk = mat(area, 24 * T, 12), mat(area, 36 * T, 12)
        dv = mat(area, 0, 2, 1536)
        mem2 = mat(area, 12 * T, 2, D)
        cz = mat(e_ring, 0, 2, 768)
        kraw = big[:, 0:T]
        angle, half_sine = big[:, 2 * T:3 * T], big[:, 3 * T:4 * T]
        turns, pos_int = big[:, 4 * T:5 * T], big[:, 5 * T:6 * T].bitcast(I32)
        junk = mat(yT, 0, 2, D)
        distm = z_tok[:, 0:3 * 384].rearrange("p (g w) -> p g w", g=3)
        dbias = z_tok[:, 3 * 384:5 * 384].rearrange("p (b w) -> p b w", b=2)
        merge_tmp = mat(z_tok, 0, 4, 512)
        gain_tmp = mat(pT, 0, 4, 512)
        mem_tok = mat(area, 0, 2, D)

        def colp(name, i=0, packed=COL1):
            return col[:, packed[name] + i:packed[name] + i + 1]

        def cconst(name, i=0):
            return const[:, CONST[name] + i:CONST[name] + i + 1]

        ps = [ctx.enter_context(nc.psum_tensor(f"general{b}", [P, 512], F32)) for b in range(4)]
        sc = [ctx.enter_context(nc.psum_tensor(f"scores{b}", [P, 512], F32)) for b in range(2)]
        tp = ctx.enter_context(nc.psum_tensor("probs_transposed", [P, 512], F32))
        po = ctx.enter_context(nc.psum_tensor("attention_out", [P, 512], F32))
        down = [sc[0], sc[1], tp, po]

        const_in = signal("const_in", 16)
        xin = signal("x_in", 16)
        landed = [signal(f"weights_landed{s}", 16) for s in range(RAW)]
        hi_done = signal("weights_hi_done")
        lo_done = signal("weights_lo_done")
        half_used = signal("weights_half_used")
        x_gained = signal("xT_gained")
        cT_hi = signal("cT_hi_ready")
        out_hi = signal("attn_out_hi")
        mem_hi = signal("memT_hi_ready")
        mem_lo = signal("memT_lo_ready")
        yc_hi_ready = signal("yc_hi_ready")
        yc_lo_ready = signal("yc_lo_ready")
        ya_hi_ready = signal("ya_hi_ready")
        ya_lo_ready = signal("ya_lo_ready")
        down_full = signal("down_full")
        z_in = signal("down_product_in")
        cols_in = signal("cols_in", 16)
        rows_in = signal("rows_in", 16)
        bias_in = signal("bias_in", 16)
        bias_ready = signal("bias_ready")
        full = [signal(f"general_full{b}") for b in range(4)]
        free = [signal(f"general_free{b}") for b in range(4)]
        sc_full = signal("scores_full")
        sc_read = signal("scores_read")
        tp_full = signal("probsT_full")
        pT_ready = signal("probsT_ready")
        po_full = signal("attn_out_full")
        po_read = signal("attn_out_read")
        nmax = signal("neg_max_ready")
        exp_done = signal("exp_done")
        p_ready = signal("probs_ready")
        dve_step = signal("dve_step")
        pool_step = signal("pool_step")
        squares_done = signal("squares_done")
        var_ready = signal("var_ready")
        std_ready = signal("std_ready")
        xhat_ready = signal("xhat_ready")
        x_ready = signal("x_ready")
        rope_ready = signal("rope_ready")
        ya_sq = signal("ya_sq")
        ya_ready = signal("ya_ready")
        yc_ready = signal("yc_ready")
        merged_ready = signal("merged_ready")
        merge_step = signal("merge_step")
        conv_init = signal("conv_init")
        silu_done = signal("silu_done")
        act_ready = signal("ffn_act_ready")
        z_ready = signal("z_ready")
        lam_sum = signal("lam_sums")
        lam_exp = signal("lam_exp")
        angle_ready = signal("angle_ready")
        sin_ready = signal("sin_ready")
        dil_in = signal("dil_in", 16)
        pos_in = signal("pos_in", 16)
        mem2_in = signal("mem2_in", 16)
        out_ready = signal("out_ready")
        out_done = signal("out_done", 16)

        FILLS, LAST_USE, AT, DOWN_HALF = {}, {}, {}, {}
        ORDER = {"layer": jobs_of("layer"), "post": jobs_of("post")}

        def fill_of(key):
            return FILLS[(stage.kind, key)]

        def need_last_phase(eng):
            for b in range(4):
                eng.wait_ge(*free[b].at(-1))


        def in_phase():
            return {"layer": HALVES_1, "post": HALVES_2}[stage.kind]

        def is_half(h):
            return stage.kind == "post" or not HALVES_1 <= h < PERIOD

        def split_index(h):
            return h - SPLIT - (PERIOD - HALVES_1 if stage.kind == "layer" and h >= PERIOD else 0)

        def when_landed(h):
            skipped = stage.kind == "layer" and h >= PERIOD and h % RAW in [k % RAW for k in range(HALVES_1, PERIOD)]
            return landed[h % RAW].at(h // RAW - 1 - skipped)

        def raw_half(h):
            return raw_ring[:, (h % RAW) * HALF_N:(h % RAW + 1) * HALF_N]

        def hi_half(h):
            return w_hi[:, (h % SPLIT) * HALF_N:(h % SPLIT + 1) * HALF_N]

        def lo_half(h):
            return w_lo[:, (h % SPLIT) * HALF_N:(h % SPLIT + 1) * HALF_N]

        def split_limit(at):
            if stage.kind == "pro":
                return 0
            last = in_phase()
            if at < last:
                return min(at + SPLIT, last)
            return last if stage.kind == "post" else PERIOD + SPLIT

        def cbuf(i, k):
            return e_ring[:, (2 * i + k) * 512:(2 * i + k) * 512 + 512]

        def sbuf(i):
            return e_ring[:, 2048 + (i % 2) * 512:2048 + (i % 2) * 512 + 512]

        def need_exp_buffer(eng, j):
            k = j - 3
            if k < 0:
                return
            name, i = ORDER[stage.kind][k]
            if k not in NUM[stage.kind][3]:
                eng.wait_ge(*p_ready.at(NUM[stage.kind][3][k + 1]))
            else:
                eng.wait_ge(*tp_full.at(NUM[stage.kind][1][(k, parts_of(name) - 1)]))

        def bank_of(key):
            return ps[fill_of(key)[0]]

        def when_full(key):
            b, n = fill_of(key)
            return full[b].at(n)

        def when_read(key):
            b, n = fill_of(key)
            return free[b].at(n)

        def read(key):
            return free[fill_of(key)[0]].more()

        def numbering(kind):
            scores, transposes, outs, probs, owner = {}, {}, {}, {}, []
            for j, (name, i) in enumerate(ORDER[kind]):
                for g in range(parts_of(name)):
                    scores[(j, g)] = len(scores)
                    owner.append(j)
                if name != "da" or i % 2 == 1:
                    probs[j] = len(probs)
                    for g in range(parts_of(name)):
                        transposes[(j, g)] = len(transposes)
                if name not in ("da", "na", "mla") or i % 2 == 1:
                    outs[j] = len(outs)
            return scores, transposes, outs, probs, owner

        NUM = {k: numbering(k) for k in ORDER}
        READS = {}
        for kind in ORDER:
            n = 0
            for j, (name, i) in enumerate(ORDER[kind]):
                for g in range(parts_of(name)):
                    if name in ("na", "mla", "dil"):
                        READS[(kind, j, g)] = n
                        n += 1

        def spans(name):
            return ((0, 128), (128, 384)) if name in ("mla", "dil") else ((0, 256), (256, 512))

        def exp_views(j, t):
            name, _ = ORDER[stage.kind][j]
            lo, hi = spans(name)[t]
            e = e_ring[:, (j % 3) * 1152:(j % 3) * 1152 + 1152]
            if name == "dil":
                return e.rearrange("p (g w) -> p g w", g=3)[:, :, lo:hi]
            return e[:, lo:hi]

        def st(kind, j, t0=0, t1=2):
            o = {"mx": 0, "nm": 6, "sum": 12, "rec": 18}[kind] + 2 * (j % 3)
            return stat[:, o + t0:o + t1]

        def set_jobs(name):
            return [j for j, (s, _) in enumerate(ORDER[stage.kind]) if s == name]

        def step_slots(fillers, n):
            slots = [[] for _ in range(n)]
            each, extra = divmod(len(fillers), n - 2)
            k = 0
            for i in range(n - 2):
                take = each + (i < extra)
                slots[1 + i] = fillers[k:k + take]
                k += take
            return slots

        def blocks(name, n0, n1):
            return [(name, i) for i in range(n0, n1)]

        da_fillers = step_slots(blocks("gc", 0, 2) + blocks("hc", 0, 2) + blocks("gb", 0, 2) + blocks("kn", 0, 2)
                                + blocks("vn", 0, 2), 10)
        na_fillers = step_slots(blocks("gate", 0, 12), 10)
        xa_fillers = step_slots(blocks("xv", 0, 4), 6)
        mla_fillers = step_slots(blocks("mv", 0, 2) + blocks("gate", 0, 4) + blocks("dq", 0, 2), 10)
        dil_fillers = [[("dv", 0)], [("dv", 2), ("dv", 4)], [("dv", 1), ("dv", 3)], [("dv", 5), ("gate", 4)],
                       blocks("gate", 5, 7), [("gate", 7)]]
        mem_fillers = step_slots(blocks("gate", 8, 12), 6)

        SCALE = {"da": 0.125, "na": 0.125, "xa": 1.0 / 16, "mla": 96.0 ** -0.5, "dil": 128.0 ** -0.5,
                 "mem": 128.0 ** -0.5}

        def out_place(name, i):
            if name == "xa":
                at, parts, src = slice(2 * i, 2 * i + 2), XO, po[:, :].rearrange("p (c w) -> p c w", w=T)
            elif name == "mem":
                at, parts, src = i, YC, po[:, 0:T]
            else:
                at, parts, src = i // 2, YB, po[:, 0:T]
            return [part[:, at, :] for part in parts], src

        block = ctx.enter_context(nc.Block())

        @block.tensor
        def _(pe):
            state = {"tile": 0, "bank": 0, "uses": [0] * 4}

            def start_phase(kind, l=0):
                stage.enter(kind, l)
                state["tile"], state["bank"], state["uses"] = 0, 0, [0] * 4

            def open_bank(key):
                b = state["bank"] % 4
                state["bank"] += 1
                n = state["uses"][b]
                state["uses"][b] += 1
                FILLS[(stage.kind, key)] = (b, n)
                if n > 0 or stage.kind != "pro":
                    pe.wait_ge(*free[b].at(n - 1))
                return b

            def half_at(g):
                h = g // HALF_TILES
                if g % HALF_TILES == 0:
                    pe.wait_ge(*lo_done.at(split_index(h)))
                c = (h % SPLIT) * HALF_N + g % HALF_TILES * TILE_N
                return w_hi[:, c:c + TILE_N], w_lo[:, c:c + TILE_N]

            def linear(key, act, kcs, feature_major, m=P, before=None):
                b = open_bank(key)
                g0 = state["tile"]
                state["tile"] += kcs
                AT[(stage.kind, key)] = (g0 + kcs - 1) // HALF_TILES
                for kc in range(kcs):
                    if before:
                        before(kc)
                    g = g0 + kc
                    w = half_at(g)
                    x = [part[:, kc, :] for part in act]
                    for half in range(2):
                        for n, (wk, xk_) in enumerate(((0, 0), (0, 1), (1, 0))):
                            first = kc == 0 and half == 0 and n == 0
                            last = kc == kcs - 1 and half == 1 and n == 2
                            if feature_major:
                                ins = nc.tensor.matmul(ps[b][0:m, half * T:half * T + T],
                                                       w[wk][:, half * m:half * m + m], x[xk_], start=first, stop=last,
                                                       skip_group_check=True)
                            else:
                                ins = nc.tensor.matmul(ps[b][:, half * T:half * T + T],
                                                       x[wk][:, half * P:half * P + P], w[xk_], start=first, stop=last,
                                                       skip_group_check=True)
                    if kc == kcs - 1:
                        ins.then_inc(*full[b].more())
                        if g % HALF_TILES == HALF_TILES - 1:
                            LAST_USE[(stage.kind, g // HALF_TILES)] = (full[b], FILLS[(stage.kind, key)][1])
                    elif g % HALF_TILES == HALF_TILES - 1:
                        LAST_USE[(stage.kind, g // HALF_TILES)] = (half_used, stage.said.get(half_used.name, 0))
                        ins.then_inc(*half_used.more())

            def down_product(i):
                pe.wait_ge(*act_ready.at(i))
                act = [part[:, 2 * (i % 2):2 * (i % 2) + 2, :] for part in YA]
                for kc in range(2):
                    g = state["tile"]
                    state["tile"] += HALF_TILES
                    h = g // HALF_TILES
                    DOWN_HALF[(stage.kind, i)] = h
                    half_at(g)
                    w = hi_half(h), lo_half(h)
                    final = i == FPAIR - 1 and kc == 1
                    for t in range(2):
                        for c in range(2):
                            for n, (xk_, wk) in enumerate(((0, 0), (0, 1), (1, 0))):
                                ins = nc.tensor.matmul(down[2 * t + c][:, :], act[xk_][:, kc, t * P:t * P + P],
                                                       w[wk][:, c * 512:c * 512 + 512], start=(i + kc + n == 0),
                                                       stop=(final and n == 2), skip_group_check=True)
                            if final:
                                ins.then_inc(*down_full.more())
                    if final:
                        LAST_USE[(stage.kind, h)] = (down_full, 3)
                    else:
                        LAST_USE[(stage.kind, h)] = (half_used, stage.said.get(half_used.name, 0))
                        ins.then_inc(*half_used.more())

            def transposes(key, src, n0):
                b = open_bank(key)
                for c in range(2):
                    for t in range(2):
                        ins = nc.tensor.transpose(ps[b][:, c * T + t * P:c * T + t * P + P],
                                                  src[:, t, (n0 + c) * P:(n0 + c) * P + P], ident)
                ins.then_inc(*full[b].more())
                AT[(stage.kind, key)] = state["tile"] // HALF_TILES

            def to_feature(name, src):
                for i in range(DC // 2):
                    transposes((name, i), src, 2 * i)

            def job(j):
                return ORDER[stage.kind][j]

            def mark(event, j):
                AT[(stage.kind, (event, j))] = state["tile"] // HALF_TILES

            def scores(j):
                name, i = job(j)
                mark("scores", j)
                number = NUM[stage.kind][0]
                for g in range(parts_of(name)):
                    n = number[(j, g)]
                    if n >= 2:
                        jj = NUM[stage.kind][4][n - 2]
                        gg = n - 2 - number[(jj, 0)]
                        if job(jj)[0] in ("na", "mla", "dil"):
                            pe.wait_ge(*sc_read.at(READS[(stage.kind, jj, gg)]))
                        else:
                            pe.wait_ge(*exp_done.at(jj))
                    dst = sc[n % 2]
                    for t in range(2):
                        lo, hi = spans(name)[t]
                        q0 = t * P
                        if name in ("da", "na"):
                            r0 = 64 * (i % 2)
                            q, k = (qa, ka) if name == "da" else (qn, kn)
                            pairs = [(q[r0:r0 + 64, i // 2, q0:q0 + P], k[r0:r0 + 64, i // 2, :])]
                        elif name == "xa":
                            pairs = [(xq[:, 2 * i + c, q0:q0 + P], xk[:, 2 * i + c, :]) for c in range(2)]
                        elif name == "mla":
                            pairs = [(qm[0:96, i, q0:q0 + P], km[0:96, i, 0:hi - lo])]
                        elif name == "dil":
                            pairs = [(dq[:, 4 * g + i, q0:q0 + P], dk[:, 4 * g + i, 0:hi - lo])]
                        else:
                            pairs = [(mq[:, i, q0:q0 + P], mk[:, i, :])]
                        for c, (q, k) in enumerate(pairs):
                            ins = nc.tensor.matmul(dst[:, lo:hi], q, k, start=(c == 0), stop=(c == len(pairs) - 1))
                    ins.then_inc(*sc_full.more())

            def turn(j):
                name, i = job(j)
                if j not in NUM[stage.kind][3]:
                    return
                mark("turn", j)
                pe.wait_ge(*p_ready.at(NUM[stage.kind][3][j]))
                for g in range(parts_of(name)):
                    n = NUM[stage.kind][1][(j, g)]
                    if n > 0:
                        pe.wait_ge(*pT_ready.at(n - 1))
                    for t in range(2):
                        e = exp_views(j, t)
                        if name == "dil":
                            e = e[:, g, :]
                        for kt in range(2 if spans(name)[t][1] - spans(name)[t][0] == 256 else 1):
                            ins = nc.tensor.transpose(tp[:, kt * T + t * P:kt * T + t * P + P],
                                                      e[:, kt * P:kt * P + P], ident)
                    ins.then_inc(*tp_full.more())

            def values(j):
                name, i = job(j)
                if j not in NUM[stage.kind][3]:
                    return
                parts = parts_of(name)
                mark("values", j)
                pe.wait_ge(*pT_ready.at(NUM[stage.kind][1][(j, parts - 1)]))
                if name == "dil" and i % 2 == 0:
                    for g in range(parts):
                        pe.wait_ge(*when_read(("dv", 2 * g + i // 2)))
                pair = name in ("na", "mla")
                if not (pair and i % 2 == 1):
                    n = NUM[stage.kind][2][j + 1 if pair else j]
                    if n > 0:
                        pe.wait_ge(*po_read.at(n - 1))
                for c in range(2 if name == "xa" else 1):
                    first = True
                    for g in range(parts):
                        slot = NUM[stage.kind][1][(j, g)] % 4
                        for kt in range(2):
                            p = pT[:, slot * 512 + kt * T:slot * 512 + kt * T + T]
                            lo = P if kt == 1 and name in ("mla", "dil") else 0
                            if name == "da":
                                v, r0, m = va[:, kt, (i // 2) * P:(i // 2) * P + P], 0, P
                            elif name == "na":
                                v, r0, m = vn[:, kt, i * 64:i * 64 + 64], 64 * (i % 2), 64
                            elif name == "mla":
                                v, r0, m = vm[:, kt, i * 64:i * 64 + 64], 64 * (i % 2), 64
                            elif name == "xa":
                                v, r0, m = xv[:, kt, (2 * i + c) * P:(2 * i + c) * P + P], 0, P
                            elif name == "dil":
                                v, r0, m = dv[:, kt, (4 * g + i) * P:(4 * g + i) * P + P], 0, P
                            else:
                                v, r0, m = mv[:, kt, i * P:i * P + P], 0, P
                            ins = nc.tensor.matmul(po[r0:r0 + m, c * T + lo:c * T + T], v, p[:, lo:T],
                                                   start=first, stop=(g == parts - 1 and kt == 1))
                            first = False
                if j in NUM[stage.kind][2]:
                    ins.then_inc(*po_full.more())

            def filler(key):
                kind = key[0]
                if kind in ("xv", "mv"):
                    linear(key, MT, DC, False)
                elif kind == "mk":
                    linear(key, MT, DC, True)
                else:
                    linear(key, XT, DC, kind not in ("vn", "dv"))

            def ya_squares():
                pe.wait_ge(*ya_sq.at(0))
                for i in range(2):
                    b = open_bank(("ss", i))
                    AT[(stage.kind, ("ss", i))] = state["tile"] // HALF_TILES
                    nc.tensor.matmul(ps[b][:, :], ones, conv_tmp[:, 2 * i:2 * i + 2, :], start=True,
                                     stop=True).then_inc(*full[b].more())

            def attention(name, fillers, extra={}):
                js = set_jobs(name)
                for step in range(len(js) + 2):
                    if step < len(js):
                        scores(js[step])
                    for key in fillers[step]:
                        filler(key)
                    if step >= 2:
                        values(js[step - 2])
                    if 1 <= step <= len(js):
                        turn(js[step - 1])
                    if step in extra:
                        extra[step]()

            def as_ready(name):
                return lambda kc: pe.wait_ge(*when_read((name, kc // 2))) if kc % 2 == 0 else None

            def branches(parts):
                for cb in range(4):
                    for br, y in enumerate(parts):
                        linear(("branch", cb, br), y, 4, True)

            def project(name, n):
                for cb in range(4):
                    linear((name, cb), MG, DC, False,
                           before=lambda kc: pe.wait_ge(*merged_ready.at(kc // 2)) if cb == 0 and kc % 2 == 0 else None)

            def ffn(source):
                for i in range(FPAIR):
                    linear(("gt", i), XT, DC, True, before=as_ready(source) if i == 0 else None)
                    linear(("up", i), XT, DC, True)
                    if i:
                        down_product(i - 1)
                down_product(FPAIR - 1)

            start_phase("pro")
            pe.wait_ge(*const_in.at(0))
            pe.wait_ge(*xin.at(1))
            to_feature("memT", mem_tok)
            pe.wait_ge(*xhat_ready.at(1))
            to_feature("xT0", z3)

            with pe.Fori(0, DEPTH) as l:
                start_phase("layer", l)
                for name in ("qa", "ka"):
                    for i in range(2):
                        linear((name, i), XT, DC, True,
                               before=lambda kc: pe.wait_ge(*free[kc // 2].at(-1)) if (name, i) == ("qa", 0) else None)
                for i in range(2):
                    linear(("va", i), XT, DC, False)
                for n, (name, i) in enumerate((("qa", 0), ("qa", 1), ("ka", 0), ("ka", 1))):
                    pe.wait_ge(*when_read((name, i)))
                    b = open_bank(("rot", n))
                    AT[(stage.kind, ("rot", n))] = state["tile"] // HALF_TILES
                    nc.tensor.matmul(ps[b][:, :], const[:, CONST["rot1"]:CONST["rot1"] + P],
                                         raw[:, 2 * n:2 * n + 2, :], start=True, stop=True).then_inc(*full[b].more())
                for i in range(2):
                    linear(("qn", i), XT, DC, True)
                pe.wait_ge(*rope_ready.at(3))
                pe.wait_ge(*when_read(("va", 1)))
                attention("da", da_fillers)
                for key in (("qn", 0), ("qn", 1), ("kn", 0), ("kn", 1), ("vn", 0), ("vn", 1)):
                    pe.wait_ge(*when_read(key))
                attention("na", na_fillers, {4: ya_squares})
                for signal_, n in ((yc_lo_ready, 0), (po_read, NUM["layer"][2][15]), (ya_lo_ready, 0)):
                    pe.wait_ge(*signal_.at(n))
                branches((YA, YB, YC))
                project("mix", 0)
                pe.wait_ge(*mem_lo.at(1))
                for i in range(4):
                    linear(("xk", i), MT, DC, True)
                pe.wait_ge(*xhat_ready.at(1))
                to_feature("ln0", z3)
                for i in range(4):
                    linear(("xq", i), XT, DC, True, before=as_ready("ln0") if i == 0 else None)
                pe.wait_ge(*when_read(("xk", 3)))
                for i in range(4):
                    pe.wait_ge(*when_read(("xq", i)))
                attention("xa", xa_fillers)
                pe.wait_ge(*po_read.at(NUM["layer"][2][19]))
                for cb in range(4):
                    linear(("xo", cb), XO, DC, False)
                pe.wait_ge(*xhat_ready.at(3))
                to_feature("ln1", z3)
                ffn("ln1")
                pe.wait_ge(*xhat_ready.at(5))
                state["bank"] = 0
                to_feature("ln2", z3)

            start_phase("post")
            pe.wait_ge(*xhat_ready.at(1))
            to_feature("premix", z3)
            for i in range(3):
                linear(("c", i), XT, DC, False, before=as_ready("premix") if i == 0 else None)
            pe.wait_ge(*xhat_ready.at(3))
            to_feature("mem2T", mem2)
            for i in range(2):
                linear(("mq", i), XT, DC, True)
            pe.wait_ge(*xhat_ready.at(4))
            for i in range(3):
                b = open_bank(("cT", i))
                for c in range(2):
                    lo, w = ((2 * i + c) * P, P) if 2 * i + c < 5 else (576, 96)
                    for t in range(2):
                        ins = nc.tensor.transpose(ps[b][0:w, c * T + t * P:c * T + t * P + P], cz[:, t, lo:lo + w],
                                                  ident)
                ins.then_inc(*full[b].more())
                AT[(stage.kind, ("cT", i))] = state["tile"] // HALF_TILES
            for i in range(3):
                pe.wait_ge(*when_read(("cT", i)))
            for i in range(4):
                linear(("uq", i), XO, 3, True, m=96)
            for i in range(2):
                linear(("uk", i), [part[:, 3:5, :] for part in XO], 2, True)
            for i in range(2):
                linear(("uv", i), [part[:, 3:5, :] for part in XO], 2, False)
            for i in range(5):
                b = open_bank(("rot2", i))
                AT[(stage.kind, ("rot2", i))] = state["tile"] // HALF_TILES
                if i < 4:
                    pe.wait_ge(*when_read(("uq", i)))
                    src = qm[64:96, 2 * i:2 * i + 2, :]
                else:
                    src = kraw[64:96, :]
                nc.tensor.matmul(ps[b][0:96, 0:512 if i < 4 else T], const[64:96, CONST["rot2"]:CONST["rot2"] + 96],
                                     src, start=True, stop=True).then_inc(*full[b].more())
            for i in range(4):
                pe.wait_ge(*when_read(("mem2T", i)))
            for i in range(2):
                linear(("mk", i), MT, DC, True)
            pe.wait_ge(*rope_ready.at(4))
            for key in (("uk", 0), ("uk", 1), ("uv", 0), ("uv", 1)):
                pe.wait_ge(*when_read(key))
            attention("mla", mla_fillers)
            for name, i in blocks("dq", 2, 6) + blocks("dk", 0, 6):
                linear((name, i), XT, DC, True)
            for key in blocks("dq", 0, 6) + blocks("dk", 0, 6):
                pe.wait_ge(*when_read(key))
            attention("dil", dil_fillers)
            for key in (("mk", 0), ("mk", 1), ("mv", 0), ("mv", 1), ("mq", 0), ("mq", 1)):
                pe.wait_ge(*when_read(key))
            attention("mem", mem_fillers)
            for signal_, n in ((po_read, NUM["post"][2][15]), (ya_lo_ready, 0)):
                pe.wait_ge(*signal_.at(n))
            branches((YB, YA, YC))
            project("wo", 0)
            pe.wait_ge(*xhat_ready.at(6))
            to_feature("preffn", z3)
            ffn("preffn")

        @block.scalar
        def _(act):
            cursor = {"half": 0}

            def split_ahead(at):
                for h in range(cursor["half"], split_limit(at)):
                    if is_half(h):
                        act.wait_ge(*when_landed(h))
                        if is_half(h - SPLIT):
                            user, n = LAST_USE[(stage.kind, h - SPLIT)]
                            act.wait_ge(*user.at(n))
                        nc.scalar.activation(hi_half(h), raw_half(h), ACT.Copy).then_inc(*hi_done.more())
                cursor["half"] = max(cursor["half"], split_limit(at))

            def reach(key):
                split_ahead(AT[(stage.kind, key)])

            def evacuate(key, dst, func=ACT.Copy, **kw):
                reach(key)
                act.wait_ge(*when_full(key))
                src = bank_of(key)
                nc.scalar.activation(dst, src[:, :].rearrange("p (c w) -> p c w", w=T), func, **kw).then_inc(*read(key))

            def gains(name, gain, bias):
                for i in range(DC // 2):
                    reach((name, i))
                    act.wait_ge(*when_full((name, i)))
                    src = bank_of((name, i))
                    for c in range(2):
                        part, o = src[:, c * T:c * T + T], gain_tmp[:, i, c * T:c * T + T]
                        if bias is None:
                            ins = nc.scalar.activation(o, part, ACT.Copy, scale=gain(2 * i + c))
                        else:
                            ins = nc.scalar.activation(o, part, ACT.Identity, bias=bias(2 * i + c),
                                                       scale=gain(2 * i + c))
                    ins.then_inc(*x_gained.more())

            def exps(j):
                name, i = ORDER[stage.kind][j]
                reach(("scores", j))
                act.wait_ge(*nmax.at(j))
                scale = SCALE[name]
                from_psum = name in ("da", "xa", "mem")
                if from_psum:
                    need_exp_buffer(act, j)
                for t in range(2):
                    e = exp_views(j, t)
                    lo, hi = spans(name)[t]
                    src = sc[NUM[stage.kind][0][(j, 0)] % 2][:, lo:hi] if from_psum else e
                    ins = nc.scalar.activation(e, src, ACT.Exp, bias=st("nm", j, t, t + 1),
                                               scale=scale if from_psum else 1.0, accum_out=st("sum", j, t, t + 1))
                ins.then_inc(*exp_done.more())

            def probs_out(j):
                name, i = ORDER[stage.kind][j]
                if j not in NUM[stage.kind][3]:
                    return
                reach(("turn", j))
                for g in range(parts_of(name)):
                    n = NUM[stage.kind][1][(j, g)]
                    act.wait_ge(*tp_full.at(n))
                    if n >= 4:
                        jj = [k for k, v in NUM[stage.kind][1].items() if v == n - 4][0][0]
                        outs = NUM[stage.kind][2]
                        if jj in outs:
                            act.wait_ge(*po_full.at(outs[jj]))
                        else:
                            act.wait_ge(*po_full.at(outs[jj + 1]))
                    slot = n % 4
                    if name in ("mla", "dil"):
                        nc.scalar.activation(pT[:, slot * 512:slot * 512 + T], tp[:, 0:T], ACT.Copy)
                        ins = nc.scalar.activation(pT[:, slot * 512 + 384:slot * 512 + 512], tp[:, 384:512], ACT.Copy)
                    else:
                        ins = nc.scalar.activation(pT[:, slot * 512:slot * 512 + 512], tp[:, :], ACT.Copy)
                    ins.then_inc(*pT_ready.more())

            def attn_out(j):
                name, i = ORDER[stage.kind][j]
                if j not in NUM[stage.kind][2]:
                    return
                reach(("values", j))
                act.wait_ge(*po_full.at(NUM[stage.kind][2][j]))
                if name in ("da", "dil"):
                    c = 8 + (i // 2 if name == "da" else i)
                    nc.scalar.activation(yT3[:, c, :], po[:, 0:T], ACT.Copy).then_inc(*po_read.more())
                else:
                    dst, src = out_place(name, i)
                    nc.scalar.activation(dst[0], src, ACT.Copy).then_inc(*out_hi.more())

            def filler(key):
                kind, i = key
                if kind == "gate":
                    reach(key)
                    act.wait_ge(*when_full(key))
                    src = bank_of(key)
                    if stage.kind == "layer":
                        nc.scalar.activation(big3[:, 2 * i:2 * i + 2, :],
                                             src[:, :].rearrange("p (c w) -> p c w", w=T),
                                             ACT.Sigmoid).then_inc(*read(key))
                    else:
                        for c in range(2):
                            ins = nc.scalar.activation(big3[:, 2 * i + c, :], src[:, c * T:c * T + T], ACT.Sigmoid,
                                                       bias=colp("b_gate", 2 * i + c, COL2), scale=1.0)
                        ins.then_inc(*read(key))
                elif kind in ("gc", "gb", "kn", "mk", "mq", "dq"):
                    dst = {"gc": gc, "gb": gb, "kn": kn, "mk": mk, "mq": mq, "dq": dq}[kind]
                    evacuate(key, dst[:, 2 * i:2 * i + 2, :])
                elif kind in ("vn", "xv", "mv", "dv"):
                    dst = {"vn": vn, "xv": xv, "mv": mv, "dv": dv}[kind]
                    evacuate(key, dst[:, :, i * T:i * T + T])

            def attention(name, fillers, extra={}):
                js = set_jobs(name)
                for step in range(len(js) + 2):
                    if step < len(js):
                        exps(js[step])
                    for key in fillers[step]:
                        filler(key)
                    if step >= 2:
                        attn_out(js[step - 2])
                    if 1 <= step <= len(js):
                        probs_out(js[step - 1])
                    if step in extra:
                        extra[step]()

            def yc_split():
                act.wait_ge(*yc_ready.at(3))
                nc.scalar.activation(YC[0], conv_tmp, ACT.Copy).then_inc(*yc_hi_ready.more())

            def ya_squares():
                act.wait_ge(*po_read.at(NUM["layer"][2][7]))
                act.wait_ge(*yc_lo_ready.at(0))
                nc.scalar.activation(conv_tmp, yT3[:, 8:12, :], ACT.Square).then_inc(*ya_sq.more())

            def ya_roots():
                for i in range(2):
                    reach(("ss", i))
                    act.wait_ge(*when_full(("ss", i)))
                    src = bank_of(("ss", i))
                    nc.scalar.activation(ya_rstd[:, 2 * i:2 * i + 2, :],
                                         src[:, :].rearrange("p (c w) -> p c w", w=T), ACT.Sqrt,
                                         bias=cconst("eps_ln"), scale=1.0 / P).then_inc(*read(("ss", i)))

            def ya_split():
                if stage.kind == "layer":
                    act.wait_ge(*ya_ready.at(0))
                else:
                    act.wait_ge(*po_read.at(NUM["post"][2][11]))
                nc.scalar.activation(YA[0], yT3[:, 8:12, :], ACT.Copy).then_inc(*ya_hi_ready.more())

            def std(n, src, dst, scale, eps):
                act.wait_ge(*var_ready.at(n))
                nc.scalar.activation(dst, src, ACT.Sqrt, bias=cconst(eps), scale=scale).then_inc(*std_ready.more())

            def ffn(gates_too, packed, w, b):
                def first_tap(i, k, which):
                    reach((which, i))
                    act.wait_ge(*when_full((which, i)))
                    src = bank_of((which, i))
                    if i >= 2:
                        act.wait_ge(*act_ready.at(i - 2))
                    for c in range(2):
                        ch = (k * FC if gates_too else 0) + 2 * i + c
                        tap = 2 if gates_too else 1
                        ins = nc.scalar.activation(cbuf(i % 2, k)[:, c * T:c * T + T], src[:, c * T:c * T + T],
                                                   ACT.Identity, bias=colp(b, ch, packed),
                                                   scale=colp(w, 3 * ch + tap, packed))
                    ins.then_inc(*conv_init.more())

                for i in range(FPAIR + 1):
                    if i < FPAIR:
                        first_tap(i, 0, "gt")
                    if i >= 1:
                        act.wait_ge(*when_read(("gt", i - 1)))
                        nc.scalar.activation(sbuf(i - 1), cbuf((i - 1) % 2, 0), ACT.Silu).then_inc(*silu_done.more())
                    if i < FPAIR and gates_too:
                        first_tap(i, 1, "up")

            stage.enter("pro")
            act.wait_ge(*const_in.at(0))
            for i in (0, 2):
                act.wait_ge(*when_full(("memT", i)))
                src = bank_of(("memT", i))
                nc.scalar.activation(memT3[:, 2 * i:2 * i + 2, :], src[:, :].rearrange("p (c w) -> p c w", w=T),
                                     ACT.Copy).then_inc(*read(("memT", i)))
            std(0, nst[:, 49:52:2], nst[:, 52:54], 1.0, "eps_ln")
            for h in range(SPLIT):
                act.wait_ge(*landed[h].at(0))
                nc.scalar.activation(hi_half(h), raw_half(h), ACT.Copy).then_inc(*hi_done.more())
            gains("xT0", lambda c: cconst("emb_g", c), lambda c: cconst("emb_b", c))

            with act.Fori(0, DEPTH) as l:
                stage.enter("layer", l)
                cursor["half"] = SPLIT
                need_last_phase(act)
                for n, (name, i) in enumerate((("qa", 0), ("qa", 1), ("ka", 0), ("ka", 1))):
                    evacuate((name, i), raw[:, 2 * n:2 * n + 2, :])
                for i in range(2):
                    evacuate(("va", i), va[:, :, i * T:i * T + T])
                act.wait_ge(*lam_sum.at(0))
                nc.scalar.activation(nst[:, 58:60], nst[:, 56:58], ACT.Exp).then_inc(*lam_exp.more())
                for i in range(2):
                    evacuate(("qn", i), qn[:, 2 * i:2 * i + 2, :])
                attention("da", da_fillers, {9: yc_split})
                attention("na", na_fillers, {1: ya_squares, 5: ya_roots, 6: ya_split})
                reach(("branch", 3, 2))
                act.wait_ge(*when_read(("branch", 3, 2)))
                for k in range(2):
                    nc.scalar.activation(MT[0][:, 4 * k:4 * k + 4, :], memT3[:, 4 * k:4 * k + 4, :],
                                         ACT.Copy).then_inc(*mem_hi.more())
                reach(("mix", 3))
                std(0, nst[:, 49:52:2], nst[:, 52:54], 1.0, "eps_ln")
                for i in range(4):
                    evacuate(("xk", i), xk[:, 2 * i:2 * i + 2, :])
                gains("ln0", lambda c: colp("ln_g", c), lambda c: colp("ln_b", c))
                for i in range(4):
                    evacuate(("xq", i), xq[:, 2 * i:2 * i + 2, :])
                attention("xa", xa_fillers)
                reach(("xo", 3))
                std(1, nst[:, 49:52:2], nst[:, 52:54], 1.0, "eps_ln")
                gains("ln1", lambda c: colp("ln_g", DC + c), lambda c: colp("ln_b", DC + c))
                ffn(False, COL1, "ffn_w", "ffn_b")
                split_ahead(in_phase() - 1)
                std(2, nst[:, 49:52:2], nst[:, 52:54], 1.0, "eps_ln")
                gains("ln2", lambda c: colp("ln_g", 2 * DC + c), lambda c: colp("ln_b", 2 * DC + c))
                split_ahead(in_phase())

            stage.enter("post")
            cursor["half"] = SPLIT
            act.wait_ge(*cols_in.at(0))
            act.wait_ge(*mem2_in.at(0))

            def mean_square(src, width, n0):
                for t in range(2):
                    ins = nc.scalar.activation(junk[:, t, 0:width], src[:, t, 0:width], ACT.Square,
                                               accum_out=nst[:, n0 + t:n0 + t + 1])
                ins.then_inc(*squares_done.more())
                act.wait_ge(*squares_done.last())
                nc.scalar.activation(nst[:, n0 + 8:n0 + 10], nst[:, n0:n0 + 2], ACT.Sqrt,
                                         bias=cconst("eps_rms"), scale=1.0 / width).then_inc(*std_ready.more())

            act.wait_ge(*x_ready.at(-1))
            mean_square(x3, D, 0)
            mean_square(mem2, D, 2)
            gains("premix", lambda c: colp("g_pre_mix", c, COL2), None)
            for i in range(3):
                evacuate(("c", i), cz[:, :, i * T:i * T + T])
            act.wait_ge(*when_read(("c", 2)))
            for lo, w, n0 in ((0, 384, 4), (384, 256, 6)):
                mean_square(cz[:, :, lo:lo + w], w, n0)
            gains("mem2T", lambda c: colp("g_mem", c, COL2), None)
            for i in range(2):
                evacuate(("mq", i), mq[:, 2 * i:2 * i + 2, :])
            for i in range(3):
                reach(("cT", i))
                act.wait_ge(*when_full(("cT", i)))
                src = bank_of(("cT", i))
                for c in range(2):
                    k = 2 * i + c
                    if k < 5:
                        g = colp("q_norm", k, COL2) if k < 3 else colp("kv_norm", k - 3, COL2)
                        ins = nc.scalar.activation(XO[0][:, k, :], src[:, c * T:c * T + T], ACT.Copy, scale=g)
                    else:
                        ins = nc.scalar.activation(kraw[64:96, :], src[64:96, c * T:c * T + T], ACT.Copy)
                ins.then_inc(*cT_hi.more())
            act.wait_ge(*angle_ready.at(0))
            nc.scalar.activation(sin2[64:96, 0:T], angle[64:96, :], ACT.Sin)
            nc.scalar.activation(sin2[64:96, T:2 * T], angle[64:96, :], ACT.Sin)
            nc.scalar.activation(half_sine[64:96, :], angle[64:96, :], ACT.Sin, scale=0.5).then_inc(*sin_ready.more())
            for i in range(4):
                reach(("uq", i))
                act.wait_ge(*when_full(("uq", i)))
                src = bank_of(("uq", i))
                nc.scalar.activation(qm[0:96, 2 * i:2 * i + 2, :], src[0:96, :].rearrange("p (c w) -> p c w", w=T),
                                     ACT.Copy).then_inc(*read(("uq", i)))
            for i in range(2):
                reach(("uk", i))
                act.wait_ge(*when_full(("uk", i)))
                src = bank_of(("uk", i))
                for par in range(2):
                    ins = nc.scalar.activation(km[0:64, 4 * i + par:4 * i + par + 3:2, :],
                                               src[64 * par:64 * par + 64, :].rearrange("p (c w) -> p c w", w=T),
                                               ACT.Copy)
                ins.then_inc(*read(("uk", i)))
            for i in range(2):
                evacuate(("uv", i), vm[:, :, i * T:i * T + T])
            for i in range(2):
                evacuate(("mk", i), mk[:, 2 * i:2 * i + 2, :])
            attention("mla", mla_fillers)
            for name, i in blocks("dq", 2, 6) + blocks("dk", 0, 6):
                evacuate((name, i), (dq if name == "dq" else dk)[:, 2 * i:2 * i + 2, :])
            attention("dil", dil_fillers)
            attention("mem", mem_fillers, {0: ya_split})
            for cb in range(4):
                evacuate(("wo", cb), z3[:, :, cb * T:cb * T + T])
            act.wait_ge(*when_read(("wo", 3)))
            mean_square(z3, D, 0)
            reach(("preffn", 0))
            act.wait_ge(*z_ready.at(0))
            mean_square(x3, D, 2)
            gains("preffn", lambda c: colp("g_pre_ffn", c, COL2), None)
            ffn(True, COL2, "conv_w", "conv_b")
            split_ahead(in_phase())
            for t in range(2):
                for c in range(2):
                    act.wait_ge(*down_full.at(2 * t + c))
                    nc.scalar.activation(z3[:, t, c * 512:c * 512 + 512], down[2 * t + c][:, :],
                                         ACT.Copy).then_inc(*z_in.more())
            act.wait_ge(*z_in.at(3))
            mean_square(z3, D, 4)

        @block.vector
        def _(dve):
            def halves(src):
                return src[:, :].rearrange("p (c w) -> p c w", w=T)

            cursor = {"half": 0}

            def split_ahead(at):
                for h in range(cursor["half"], split_limit(at)):
                    if is_half(h):
                        dve.wait_ge(*hi_done.at(split_index(h)))
                        nc.vector.tensor_tensor(lo_half(h), raw_half(h), hi_half(h).bitcast(F32),
                                                ALU.subtract).then_inc(*lo_done.more())
                cursor["half"] = max(cursor["half"], split_limit(at))

            def reach(key):
                split_ahead(AT[(stage.kind, key)])

            def low(dst, src, hi):
                return nc.vector.tensor_tensor(dst, src, hi.bitcast(F32), ALU.subtract)

            def gains(name, dst, n0):
                for i in range(DC // 2):
                    reach((name, i))
                    dve.wait_ge(*x_gained.at(n0 + i))
                    src = gain_tmp[:, i, :].rearrange("p (c w) -> p c w", w=T)
                    hi, lo = (part[:, 2 * i:2 * i + 2, :] for part in dst)
                    nc.vector.tensor_copy(hi, src).then_inc(*dve_step.more())
                    dve.wait_ge(*dve_step.last())
                    low(lo, src, hi).then_inc(*read((name, i)))

            bn = nst[:, 24:48].rearrange("p (t h s) -> p t h s", t=2, h=2)

            def statistics(half):
                for t in range(2):
                    ins = nc.vector.bn_stats(bn[:, t, half, :], z3[:, t, half * 512:half * 512 + 512])
                return ins

            def normalise(n):
                statistics(1).then_inc(*dve_step.more())
                dve.wait_ge(*dve_step.last())
                nc.vector.memset(nst[:, 63:64], 0.0)
                for t in range(2):
                    ins = nc.vector.bn_aggr(nst[:, 48 + 2 * t:50 + 2 * t], bn[:, t, :, :])
                ins.then_inc(*var_ready.more())
                dve.wait_ge(*std_ready.at(n))
                nc.vector.reciprocal(nst[:, 54:56], nst[:, 52:54]).then_inc(*dve_step.more())
                dve.wait_ge(*dve_step.last())
                for t in range(2):
                    nc.vector.tensor_scalar(z3[:, t, :], z3[:, t, :], nst[:, 48 + 2 * t:49 + 2 * t],
                                                nst[:, 54 + t:55 + t], ALU.subtract, ALU.mult).then_inc(*xhat_ready.more())

            def residual_norm(name, k, n):
                dve.wait_ge(*x_ready.at(k))
                for cb in range(4):
                    reach((name, cb))
                    dve.wait_ge(*when_full((name, cb)))
                    src = bank_of((name, cb))
                    at = slice(cb * T, cb * T + T)
                    nc.vector.scalar_tensor_tensor(z3[:, :, at], x3[:, :, at], ALPHA, halves(src),
                                                           ALU.mult, ALU.add).then_inc(*read((name, cb)))
                    if cb == 1:
                        dve.wait_ge(*when_read((name, cb)))
                        statistics(0)
                dve.wait_ge(*when_read((name, 3)))
                normalise(n)

            def residual_norm_down(k, n):
                dve.wait_ge(*x_ready.at(k))
                for c in range(2):
                    at = slice(c * 512, c * 512 + 512)
                    for t in range(2):
                        dve.wait_ge(*down_full.at(2 * t + c))
                        ins = nc.vector.scalar_tensor_tensor(z3[:, t, at], x3[:, t, at], ALPHA, down[2 * t + c][:, :],
                                                             ALU.mult, ALU.add)
                    ins.then_inc(*dve_step.more())
                    dve.wait_ge(*dve_step.last())
                    if c == 0:
                        statistics(0)
                normalise(n)

            def rope(n, rot, x_raw, cosine, sine, dst, sc_a, sc_b):
                reach(rot)
                dve.wait_ge(*when_full(rot))
                src = bank_of(rot)
                if n > 0:
                    dve.wait_ge(*rope_ready.at(n - 1))
                nc.vector.tensor_tensor(sc_a, x_raw, cosine, ALU.mult)
                nc.vector.tensor_tensor(sc_b, src[:, :], sine, ALU.mult).then_inc(*read(rot))
                dve.wait_ge(*when_read(rot))
                nc.vector.tensor_tensor(dst, sc_a, sc_b, ALU.add).then_inc(*rope_ready.more())

            def maxima(j):
                name, i = ORDER[stage.kind][j]
                number = NUM[stage.kind][0]
                reach(("scores", j))
                if name in ("na", "mla", "dil"):
                    need_exp_buffer(dve, j)
                for g in range(parts_of(name)):
                    n = number[(j, g)]
                    src = sc[n % 2]
                    e = e_ring[:, (j % 3) * 1152:(j % 3) * 1152 + 1152]
                    if name == "dil":
                        nc.vector.tensor_scalar(dbias[:, g % 2, :], distm[:, g, :], -float(SLOPES[g, i]), None,
                                                       ALU.mult).then_inc(*dve_step.more())
                        dve.wait_ge(*dve_step.last())
                    dve.wait_ge(*sc_full.at(n))
                    if name == "na":
                        for t in range(2):
                            j0 = 2 * (1 - t)
                            ins = nc.vector.scalar_tensor_tensor(
                                e[:, t * T:t * T + T], src[:, t * T:t * T + T], SCALE[name],
                                bias_tab[:, i, j0:j0 + 4, :].rearrange("p j k -> p (j k)"), ALU.mult, ALU.add)
                    elif name == "mla":
                        ins = nc.vector.scalar_tensor_tensor(e[:, 0:384], src[:, 0:384], SCALE[name],
                                                             const[:, CONST["causal"]:CONST["causal"] + 384],
                                                             ALU.mult, ALU.add)
                    elif name == "dil":
                        ins = nc.vector.scalar_tensor_tensor(e[:, g * 384:g * 384 + 384], src[:, 0:384], SCALE[name],
                                                             dbias[:, g % 2, :], ALU.mult, ALU.add)
                    if name in ("na", "mla", "dil"):
                        ins.then_inc(*sc_read.more())
                if name in ("na", "mla", "dil"):
                    dve.wait_ge(*sc_read.last())
                for t in range(2):
                    lo, hi = spans(name)[t]
                    view = exp_views(j, t) if name in ("na", "mla", "dil") else src[:, lo:hi]
                    ins = nc.vector.tensor_reduce(st("mx", j, t, t + 1), view, AX.XY if name == "dil" else AX.X,
                                                  ALU.max)
                ins.then_inc(*dve_step.more())
                dve.wait_ge(*dve_step.last())
                k = -1.0 if name in ("na", "mla", "dil") else -SCALE[name]
                nc.vector.tensor_scalar(st("nm", j), st("mx", j), k, None, ALU.mult).then_inc(*nmax.more())

            def normed(j):
                name, i = ORDER[stage.kind][j]
                dve.wait_ge(*exp_done.at(j))
                nc.vector.reciprocal(st("rec", j), st("sum", j)).then_inc(*dve_step.more())
                dve.wait_ge(*dve_step.last())
                if name == "da" and i % 2 == 0:
                    return
                if name == "da":
                    nc.vector.tensor_scalar(st("rec", j), st("rec", j), nst[:, 60:61], None, ALU.mult).then_inc(*dve_step.more())
                    dve.wait_ge(*dve_step.last())
                    for t in range(2):
                        ins = nc.vector.tensor_scalar(exp_views(j, t), exp_views(j, t), st("rec", j, t, t + 1), None,
                                                      ALU.mult)
                    ins.then_inc(*dve_step.more())
                    dve.wait_ge(*dve_step.last())
                    for t in range(2):
                        ins = nc.vector.scalar_tensor_tensor(exp_views(j, t), exp_views(j - 1, t),
                                                             st("rec", j - 1, t, t + 1), exp_views(j, t),
                                                             ALU.mult, ALU.add)
                else:
                    for t in range(2):
                        ins = nc.vector.tensor_scalar(exp_views(j, t), exp_views(j, t), st("rec", j, t, t + 1), None,
                                                      ALU.mult)
                ins.then_inc(*p_ready.more())

            def filler(key):
                kind, i = key
                if kind == "hc":
                    dve.wait_ge(*when_read(("gc", i)))
                    dve.wait_ge(*when_full(key))
                    src = bank_of(key)
                    nc.vector.tensor_tensor(cin[:, 2 * i:2 * i + 2, :], gc[:, 2 * i:2 * i + 2, :], halves(src),
                                                    ALU.mult).then_inc(*read(key))

            def attn_out(j):
                name, i = ORDER[stage.kind][j]
                if j not in NUM[stage.kind][2] or name in ("da", "dil"):
                    return
                reach(("values", j))
                dve.wait_ge(*out_hi.at(sum(ORDER[stage.kind][k][0] not in ("da", "dil") for k in NUM[stage.kind][2]
                                           if k < j)))
                dst, src = out_place(name, i)
                low(dst[1], src, dst[0]).then_inc(*po_read.more())

            def attention(name, fillers, extra={}):
                js = set_jobs(name)
                for step in range(len(js) + 2):
                    if step < len(js):
                        maxima(js[step])
                    if 1 <= step <= len(js):
                        normed(js[step - 1])
                    for key in fillers[step]:
                        reach(key)
                        filler(key)
                    if step >= 2:
                        attn_out(js[step - 2])
                    if step in extra:
                        extra[step]()

            def gated_conv(c):
                if c == 0:
                    dve.wait_ge(*x_ready.at(-1))
                    dve.wait_ge(*when_read(("hc", 1)))
                    dve.wait_ge(*when_read(("gb", 0)))
                    dve.wait_ge(*when_read(("gb", 1)))
                src, dst = cin[:, c, :], conv_tmp[:, c, :]
                w = [colp("sc_w", 3 * c + k) for k in range(3)]
                nc.vector.tensor_scalar(dst, src, w[1], None, ALU.mult).then_inc(*dve_step.more())
                dve.wait_ge(*dve_step.last())
                nc.vector.scalar_tensor_tensor(dst[:, 1:T], src[:, 0:T - 1], w[0], dst[:, 1:T],
                                               ALU.mult, ALU.add).then_inc(*dve_step.more())
                dve.wait_ge(*dve_step.last())
                nc.vector.scalar_tensor_tensor(dst[:, 0:T - 1], src[:, 1:T], w[2], dst[:, 0:T - 1],
                                               ALU.mult, ALU.add).then_inc(*dve_step.more())
                dve.wait_ge(*dve_step.last())
                nc.vector.tensor_tensor(dst, dst, gb[:, c, :], ALU.mult).then_inc(*yc_ready.more())

            def yc_split():
                dve.wait_ge(*yc_hi_ready.at(0))
                low(YC[1], conv_tmp, YC[0]).then_inc(*yc_lo_ready.more())

            def ya_norm():
                dve.wait_ge(*when_read(("ss", 0)))
                dve.wait_ge(*when_read(("ss", 1)))
                nc.vector.reciprocal(ya_rstd, ya_rstd).then_inc(*dve_step.more())
                dve.wait_ge(*dve_step.last())
                nc.vector.scalar_tensor_tensor(yT[:, 8 * T:12 * T], yT[:, 8 * T:12 * T], nst[:, 61:62],
                                               z_tok[:, 4 * T:8 * T], ALU.mult, ALU.mult).then_inc(*ya_ready.more())

            def ya_split():
                dve.wait_ge(*ya_hi_ready.at(0))
                low(YA[1], yT3[:, 8:12, :], YA[0]).then_inc(*ya_lo_ready.more())

            def merge():
                for cb in range(4):
                    for br in range(3):
                        reach(("branch", cb, br))
                        dve.wait_ge(*when_full(("branch", cb, br)))
                        src = bank_of(("branch", cb, br))
                        gate = big3[:, 8 * br + 2 * cb:8 * br + 2 * cb + 2, :]
                        acc, tmp = (merge_tmp[:, k, :].rearrange("p (c w) -> p c w", w=T)
                                    for k in (cb % 2, 2 + br % 2))
                        if br == 0:
                            nc.vector.tensor_tensor(acc, gate, halves(src), ALU.mult).then_inc(*read(("branch", cb, br)))
                            continue
                        nc.vector.tensor_tensor(tmp, gate, halves(src), ALU.mult).then_inc(*read(("branch", cb, br)))
                        dve.wait_ge(*when_read(("branch", cb, br)))
                        nc.vector.tensor_tensor(acc, acc, tmp, ALU.add).then_inc(*merge_step.more())
                        dve.wait_ge(*merge_step.last())
                    at = slice(2 * cb, 2 * cb + 2)
                    nc.vector.tensor_copy(MG[0][:, at, :], acc).then_inc(*merge_step.more())
                    dve.wait_ge(*merge_step.last())
                    low(MG[1][:, at, :], acc, MG[0][:, at, :]).then_inc(*merged_ready.more())
                    dve.wait_ge(*merged_ready.at(cb))

            def ffn(gates_too, packed, w):
                def outer_taps(i, k, which):
                    reach((which, i))
                    dve.wait_ge(*conv_init.at(2 * i + k if gates_too else i))
                    src = bank_of((which, i))
                    for turn in range(2):
                        for c in range(2):
                            ch = (k * FC if gates_too else 0) + 2 * i + c
                            s, d = src[:, c * T:c * T + T], cbuf(i % 2, k)[:, c * T:c * T + T]
                            if gates_too:
                                shift, tap = turn + 1, 1 - turn
                                s, d = s[:, 0:T - shift], d[:, shift:T]
                            else:
                                s, d, tap = ((s[:, 0:T - 1], d[:, 1:T], 0), (s[:, 1:T], d[:, 0:T - 1], 2))[turn]
                            ins = nc.vector.scalar_tensor_tensor(d, s, colp(w, 3 * ch + tap, packed), d,
                                                                 ALU.mult, ALU.add)
                        if turn == 0:
                            ins.then_inc(*dve_step.more())
                            dve.wait_ge(*dve_step.last())
                    ins.then_inc(*read((which, i)))

                def product(i):
                    prod = sbuf(i)
                    dve.wait_ge(*silu_done.at(i))
                    if gates_too:
                        dve.wait_ge(*when_read(("up", i)))
                        nc.vector.tensor_tensor(prod, prod, cbuf(i % 2, 1), ALU.mult).then_inc(*dve_step.more())
                        dve.wait_ge(*dve_step.last())
                    else:
                        dve.wait_ge(*when_full(("up", i)))
                        src = bank_of(("up", i))
                        nc.vector.tensor_tensor(prod, prod, src[:, :], ALU.mult).then_inc(*read(("up", i)))
                        dve.wait_ge(*when_read(("up", i)))
                    prod = prod.rearrange("p (c w) -> p c w", w=T)
                    hi, lo = (part[:, 2 * (i % 2):2 * (i % 2) + 2, :] for part in YA)
                    if i >= 2:
                        user, n = LAST_USE[(stage.kind, DOWN_HALF[(stage.kind, i - 2)])]
                        dve.wait_ge(*user.at(n))
                    nc.vector.tensor_copy(hi, prod).then_inc(*dve_step.more())
                    dve.wait_ge(*dve_step.last())
                    low(lo, prod, hi).then_inc(*act_ready.more())

                for i in range(FPAIR + 1):
                    if i < FPAIR:
                        outer_taps(i, 0, "gt")
                    if i == FPAIR and not gates_too:
                        reach(("up", i - 1))
                    if i >= 1:
                        product(i - 1)
                    if i < FPAIR and gates_too:
                        outer_taps(i, 1, "up")

            def inverse_std(n, n0):
                dve.wait_ge(*std_ready.at(n))
                nc.vector.reciprocal(nst[:, n0 + 16:n0 + 18], nst[:, n0 + 8:n0 + 10]).then_inc(*dve_step.more())
                dve.wait_ge(*dve_step.last())

            def add_normed(n, n0, gain_rows, done):
                inverse_std(n, n0)
                dve.wait_ge(*rows_in.at(gain_rows))
                for t in range(2):
                    ins = nc.vector.scalar_tensor_tensor(z3[:, t, :], z3[:, t, :], nst[:, n0 + 16 + t:n0 + 17 + t],
                                                         rows[:, 0:D], ALU.mult, ALU.mult)
                ins.then_inc(*dve_step.more())
                dve.wait_ge(*dve_step.last())
                nc.vector.tensor_tensor(x_tok[:, :], x_tok[:, :], z_tok[:, :], ALU.add).then_inc(*done.more())

            stage.enter("pro")
            dve.wait_ge(*const_in.at(0))
            dve.wait_ge(*xin.at(1))
            statistics(0)
            normalise(0)
            for i in (1, 3):
                dve.wait_ge(*when_full(("memT", i)))
                nc.vector.tensor_copy(memT3[:, 2 * i:2 * i + 2, :],
                                      halves(bank_of(("memT", i)))).then_inc(*read(("memT", i)))
            for h in range(SPLIT):
                dve.wait_ge(*hi_done.at(h))
                low(lo_half(h), raw_half(h), hi_half(h)).then_inc(*lo_done.more())
            gains("xT0", XT, 0)

            with dve.Fori(0, DEPTH) as l:
                stage.enter("layer", l)
                cursor["half"] = SPLIT
                dve.wait_ge(*cols_in.at(0))
                lam = col[:, COL1["lam"]:COL1["lam"] + 256].rearrange("p (a b w) -> p a b w", a=2, b=2)
                prod = e_ring[:, 0:128].rearrange("p (a w) -> p a w", a=2)
                nc.vector.tensor_tensor(prod, lam[:, :, 0, :], lam[:, :, 1, :], ALU.mult).then_inc(*dve_step.more())
                dve.wait_ge(*dve_step.last())
                nc.vector.tensor_reduce(nst[:, 56:58], prod, AX.X, ALU.add).then_inc(*lam_sum.more())
                nc.vector.tensor_tensor(nst[:, 61:62], colp("subln"), colp("one_minus"), ALU.mult)
                for n in range(4):
                    dst = (qa, ka)[n // 2][:, 2 * (n % 2):2 * (n % 2) + 2, :].rearrange("p c w -> p (c w)")
                    x_raw = raw[:, 2 * n:2 * n + 2, :].rearrange("p c w -> p (c w)")
                    rope(n, ("rot", n), x_raw, cos2, sin2, dst, scratch[:, 0, :], scratch[:, 1, :])
                dve.wait_ge(*lam_exp.at(0))
                nc.vector.tensor_tensor(nst[:, 62:63], nst[:, 59:60], nst[:, 58:59], ALU.subtract).then_inc(*dve_step.more())
                dve.wait_ge(*dve_step.last())
                nc.vector.tensor_tensor(nst[:, 60:61], nst[:, 62:63], colp("lam_init"), ALU.subtract).then_inc(*dve_step.more())
                dve.wait_ge(*dve_step.last())
                attention("da", da_fillers, {5: lambda: gated_conv(0), 6: lambda: gated_conv(1),
                                             7: lambda: gated_conv(2), 8: lambda: gated_conv(3), 9: yc_split})
                dve.wait_ge(*bias_ready.at(0))
                attention("na", na_fillers, {5: ya_norm, 6: ya_split})
                merge()
                for k in range(2):
                    dve.wait_ge(*mem_hi.at(k))
                    low(MT[1][:, 4 * k:4 * k + 4, :], memT3[:, 4 * k:4 * k + 4, :],
                        MT[0][:, 4 * k:4 * k + 4, :]).then_inc(*mem_lo.more())
                residual_norm("mix", -1, 0)
                gains("ln0", XT, 0)
                attention("xa", xa_fillers)
                residual_norm("xo", 0, 1)
                gains("ln1", XT, 4)
                ffn(False, COL1, "ffn_w")
                split_ahead(in_phase() - 1)
                residual_norm_down(1, 2)
                gains("ln2", XT, 8)
                split_ahead(in_phase())

            stage.enter("post")
            cursor["half"] = SPLIT
            dve.wait_ge(*x_ready.at(-1))
            inverse_std(0, 0)
            for t in range(2):
                nc.vector.tensor_scalar(z3[:, t, :], x3[:, t, :], nst[:, 16 + t:17 + t], None, ALU.mult).then_inc(*xhat_ready.more())
            inverse_std(1, 2)
            for t in range(2):
                nc.vector.tensor_scalar(mem2[:, t, :], mem2[:, t, :], nst[:, 18 + t:19 + t], None, ALU.mult).then_inc(*xhat_ready.more())
            dve.wait_ge(*cols_in.at(0))
            gains("premix", XT, 0)
            reach(("c", 1))
            dve.wait_ge(*pos_in.at(0))
            ang, trn, red = turns[64:96, :], half_sine[64:96, :], angle[64:96, :]
            nc.vector.tensor_copy(ang, pos_int[64:96, :]).then_inc(*dve_step.more())
            dve.wait_ge(*dve_step.last())
            nc.vector.tensor_scalar(ang, ang, const[64:96, CONST["inv"]:CONST["inv"] + 1], None, ALU.mult).then_inc(*dve_step.more())
            dve.wait_ge(*dve_step.last())
            nc.vector.tensor_scalar(trn, ang, 1.0 / (2 * np.pi), ROUND, ALU.mult, ALU.add).then_inc(*dve_step.more())
            dve.wait_ge(*dve_step.last())
            nc.vector.tensor_scalar(trn, trn, ROUND, None, ALU.subtract).then_inc(*dve_step.more())
            dve.wait_ge(*dve_step.last())
            nc.vector.scalar_tensor_tensor(red, trn, -TWO_PI[0], ang, ALU.mult, ALU.add).then_inc(*dve_step.more())
            dve.wait_ge(*dve_step.last())
            nc.vector.scalar_tensor_tensor(red, trn, -TWO_PI[1], red, ALU.mult, ALU.add).then_inc(*dve_step.more())
            dve.wait_ge(*dve_step.last())
            nc.vector.scalar_tensor_tensor(red, trn, -TWO_PI[2], red, ALU.mult, ALU.add).then_inc(*dve_step.more())
            dve.wait_ge(*dve_step.last())
            nc.vector.tensor_scalar(red, red, PI_BELOW, -PI_BELOW, ALU.min, ALU.max).then_inc(*angle_ready.more())
            reach(("c", 2))
            for n, (lo, w) in enumerate(((0, 384), (384, 256))):
                inverse_std(2 + n, 4 + 2 * n)
                for t in range(2):
                    ins = nc.vector.tensor_scalar(cz[:, t, lo:lo + w], cz[:, t, lo:lo + w],
                                                  nst[:, 20 + 2 * n + t:21 + 2 * n + t], None, ALU.mult)
            ins.then_inc(*xhat_ready.more())
            gains("mem2T", MT, 4)
            for i in range(3):
                reach(("cT", i))
                dve.wait_ge(*cT_hi.at(i))
                src = bank_of(("cT", i))
                for c in range(2 if i < 2 else 1):
                    k = 2 * i + c
                    g = colp("q_norm", k, COL2) if k < 3 else colp("kv_norm", k - 3, COL2)
                    ins = nc.vector.scalar_tensor_tensor(XO[1][:, k, :], src[:, c * T:c * T + T], g,
                                                         XO[0][:, k, :].bitcast(F32), ALU.mult, ALU.subtract)
                ins.then_inc(*read(("cT", i)))
            dve.wait_ge(*sin_ready.at(0))
            nc.vector.tensor_tensor(turns[64:96, :], half_sine[64:96, :], half_sine[64:96, :], ALU.mult).then_inc(*dve_step.more())
            dve.wait_ge(*dve_step.last())
            for c in range(2):
                ins = nc.vector.tensor_scalar(cos2[64:96, c * T:c * T + T], turns[64:96, :], -2.0, 1.0, ALU.mult, ALU.add)
            ins.then_inc(*dve_step.more())
            dve.wait_ge(*dve_step.last())
            for n in range(4):
                part = qm[64:96, 2 * n:2 * n + 2, :].rearrange("p c w -> p (c w)")
                src_key = ("rot2", n)
                reach(src_key)
                dve.wait_ge(*when_full(src_key))
                src = bank_of(src_key)
                if n > 0:
                    dve.wait_ge(*rope_ready.at(n - 1))
                nc.vector.tensor_tensor(scratch[64:96, 0, :], part, cos2[64:96, :], ALU.mult)
                nc.vector.tensor_tensor(scratch[64:96, 1, :], src[64:96, :], sin2[64:96, :], ALU.mult).then_inc(*read(src_key))
                dve.wait_ge(*when_read(src_key))
                nc.vector.tensor_tensor(part, scratch[64:96, 0, :], scratch[64:96, 1, :], ALU.add).then_inc(*rope_ready.more())
            reach(("rot2", 4))
            dve.wait_ge(*when_full(("rot2", 4)))
            src = bank_of(("rot2", 4))
            dve.wait_ge(*rope_ready.at(3))
            nc.vector.tensor_tensor(scratch[64:96, 0, 0:T], kraw[64:96, :], cos2[64:96, 0:T], ALU.mult)
            nc.vector.tensor_tensor(scratch[64:96, 1, 0:T], src[64:96, 0:T], sin2[64:96, 0:T], ALU.mult).then_inc(*read(("rot2", 4)))
            dve.wait_ge(*when_read(("rot2", 4)))
            nc.vector.tensor_tensor(km[64:96, :, :], scratch[64:96, 0:1, 0:T].to_broadcast([32, 8, T]),
                                        scratch[64:96, 1:2, 0:T].to_broadcast([32, 8, T]), ALU.add).then_inc(*rope_ready.more())
            attention("mla", mla_fillers)
            dve.wait_ge(*dil_in.at(0))
            attention("dil", dil_fillers)
            attention("mem", mem_fillers, {1: ya_split})
            merge()
            for cb in range(4):
                reach(("wo", cb))
                dve.wait_ge(*when_read(("wo", cb)))
            add_normed(4, 0, 0, z_ready)
            inverse_std(5, 2)
            for t in range(2):
                nc.vector.tensor_scalar(z3[:, t, :], x3[:, t, :], nst[:, 18 + t:19 + t], None, ALU.mult).then_inc(*xhat_ready.more())
            gains("preffn", XT, 8)
            ffn(True, COL2, "conv_w")
            split_ahead(in_phase())
            add_normed(6, 4, 1, out_ready)

        @block.gpsimd
        def _(pool):
            def load_rows(k, first=True):
                src = bass.AP(a["ln_rows"].tensor, k * (2 * D), [[0, P], [1, 2 * D]])
                pool.dma_start(rows[:, :], src).then_inc(*rows_in.more())

            def next_x(xhat, rows_n, n):
                pool.wait_ge(*rows_in.at(rows_n))
                pool.wait_ge(*xhat_ready.at(xhat))
                for t in range(2):
                    ins = nc.gpsimd.tensor_tensor(x3[:, t, :], z3[:, t, :], rows[:, 0:D], ALU.mult)
                ins.then_inc(*pool_step.more())
                pool.wait_ge(*pool_step.last())
                for t in range(2):
                    ins = nc.gpsimd.tensor_tensor(x3[:, t, :], x3[:, t, :], rows[:, D:2 * D], ALU.add)
                ins.then_inc(*x_ready.more())
                pool.wait_ge(*x_ready.at(n))

            stage.enter("pro")
            load_rows(0)
            for l in range(DEPTH):
                for h in range(RPB_H):
                    for s in range(2):
                        src = bass.AP(a["rpb"].tensor,
                                      ((l * RPB_H + h) * RPB_R + NJ - 1 - s) * RPB_C + RPB_C // 2,
                                      [[RPB_C, NJ], [-1, 64], [1, 64]])
                        dst = a["bias_scratch"][l, 64 * s:64 * s + 64, h * NJ * 64:(h + 1) * NJ * 64]
                        pool.dma_start(dst.rearrange("p (j k) -> j p k", j=NJ), src).then_inc(*bias_in.more())
            pool.wait_ge(*const_in.at(0))
            next_x(1, 0, 0)
            pool.wait_ge(*bias_in.at(2 * DEPTH * RPB_H - 1))

            with pool.Fori(0, DEPTH) as l:
                stage.enter("layer", l)
                need_last_phase(pool)
                pool.dma_start(col[:, :], a["cols"][l]).then_inc(*cols_in.more())
                pool.dma_start(area[:, 36 * T:48 * T], a["bias_scratch"][l]).then_inc(*bias_in.more())
                pool.wait_ge(*bias_in.at(0))
                table = area[:, 36 * T:48 * T].rearrange("p (a k) -> p a k", k=64)
                mask = const[:, CONST["na_mask"]:CONST["na_mask"] + 64].unsqueeze(1).to_broadcast([P, 8 * NJ, 64])
                nc.gpsimd.tensor_tensor(table, table, mask, ALU.add).then_inc(*bias_ready.more())
                for k in range(3):
                    if k == 0:
                        pool.wait_ge(*sc_read.at(READS[("layer", 15, 0)]))
                    load_rows(1 + k + 3 * l)
                    next_x(2 * k + 1, k, k)

            stage.enter("post")
            need_last_phase(pool)
            pool.dma_start(mem2, a["mem_2"].rearrange("b (t p) d -> p (b t) d", p=P)).then_inc(*mem2_in.more())
            pool.dma_start(col[:, :], a["cols"][DEPTH]).then_inc(*cols_in.more())
            pos = bass.AP(a["positions_2"].tensor, 0, [[0, 32], [1, T]])
            pool.dma_start(pos_int[64:96, :], pos).then_inc(*pos_in.more())
            pool.wait_ge(*nmax.at(7))
            pool.dma_start(z_tok[:, 0:3 * 384], a["distm"]).then_inc(*dil_in.more())
            pool.wait_ge(*nmax.at(11))
            load_rows(7)
            pool.wait_ge(*z_ready.at(0))
            load_rows(8)

        @block.sync
        def _(sp):
            def load_half(row, h):
                sp.dma_start(raw_half(h), a["stream"][row]).then_inc(*landed[h % RAW].more())

            stage.enter("pro")
            sp.dma_start(const[:, :], a["const"]).then_inc(*const_in.more())
            sp.dma_start(z3, a["x"].rearrange("b (t p) d -> p (b t) d", p=P)).then_inc(*xin.more())
            sp.dma_start(mem_tok, a["mem"].rearrange("b (t p) d -> p (b t) d", p=P)).then_inc(*xin.more())
            for h in range(RAW):
                load_half(h, h)

            def stream(total, first):
                for h in range(RAW, total):
                    if is_half(h):
                        if is_half(h - RAW):
                            sp.wait_ge(*lo_done.at(split_index(h - RAW)))
                        load_half(first + h, h)

            with sp.Fori(0, DEPTH) as l:
                stage.enter("layer", l)
                stream(PERIOD + RAW, l * PERIOD)
            stage.enter("post")
            stream(HALVES_2, DEPTH * PERIOD)
            sp.wait_ge(*out_ready.at(0))
            sp.dma_start(out.rearrange("b (t p) d -> p (b t) d", p=P), x3).then_inc(*out_done.more())
            sp.wait_ge(*out_done.at(0))

    counted = {k: tuple(v) for k, v in stage.seen.items()}
    assert counted == COUNTS, counted
    return stage


def tiles_of(w):
    k, n = w.shape
    if n % TILE_N:
        w = np.concatenate([w, np.zeros((k, TILE_N - n % TILE_N), w.dtype)], 1)
    return w.reshape(k // P, P, -1, TILE_N).transpose(2, 0, 1, 3).reshape(-1, P, TILE_N)


def halves_of(tiles, halves):
    t = np.concatenate(tiles)
    t = np.concatenate([t, np.zeros((halves * HALF_TILES - len(t), P, TILE_N), t.dtype)])
    return t.reshape(halves, HALF_TILES, P, TILE_N).transpose(0, 2, 1, 3).reshape(halves, P, HALF_N)


def stream_of(i):
    out = []
    for l in range(DEPTH):
        w = i["w_in"][l]
        cuts = {n: w[:, 512 * k:512 * k + 512]
                for k, n in enumerate(("qa", "ka", "va", "qn", "kn", "vn", "gb", "gc", "hc"))}
        t = [tiles_of(cuts[n]) for n in ("qa", "ka", "va", "qn", "gc", "hc", "gb", "kn", "vn")]
        t.append(tiles_of(w[:, 4608:]))
        t += branch_tiles(i["w_branch"][l])
        kv = i["xa_kv"][l]
        t += [tiles_of(i["w_mix_out"][l]), tiles_of(kv[:, :D]), tiles_of(i["xa_q"][l]), tiles_of(kv[:, D:]),
              tiles_of(i["xa_o"][l])]
        t += ffn_tiles(i["ffn_w_in"][l], i["ffn_w_out"][l], True)
        out.append(halves_of(t, PERIOD))
    w = i["w_in_2"][0]
    uq = i["w_uq_2"][0].reshape(384, 4, 192)
    uq = np.concatenate([uq, np.zeros((384, 4, 64), uq.dtype)], 2).reshape(384, 1024)
    ukv = i["w_ukv_2"][0].reshape(256, 8, 128)
    gates = tiles_of(w[:, 5792:])
    dq, dk, dv = (tiles_of(w[:, 672 + 1536 * k:672 + 1536 * (k + 1)]) for k in range(3))
    dv = dv.reshape(3, 2, DC, P, TILE_N).transpose(1, 0, 2, 3, 4).reshape(-1, P, TILE_N)
    t = [tiles_of(w[:, 0:672]), tiles_of(w[:, 5280:5792]), tiles_of(uq),
         tiles_of(ukv[:, :, :64].reshape(256, 512)), tiles_of(ukv[:, :, 64:].reshape(256, 512)),
         tiles_of(i["w_mem_kv_2"][0]), gates[:4 * DC], dq, dk, dv, gates[4 * DC:]]
    t += branch_tiles(np.stack([i["w_br_mla_2"][0], i["w_br_dil_2"][0], i["w_br_mem_2"][0]]))
    t.append(tiles_of(i["w_o_2"][0]))
    t += ffn_tiles(i["w_ffn_up_2"][0], i["w_ffn_down_2"][0], False)
    out.append(halves_of(t, HALVES_2))
    return np.concatenate(out)


def branch_tiles(w):
    parts = [tiles_of(x).reshape(4, 4, P, TILE_N) for x in w]
    return [parts[br][cb] for cb in range(4) for br in range(3)]


def ffn_tiles(w_in, w_out, gate_last):
    a, b = tiles_of(w_in[:, :FF]), tiles_of(w_in[:, FF:])
    gate, value = (b, a) if gate_last else (a, b)
    gate, value = gate.reshape(FPAIR, DC, P, TILE_N), value.reshape(FPAIR, DC, P, TILE_N)
    down = w_out.reshape(FC, P, D // TILE_N, TILE_N).transpose(0, 2, 1, 3).reshape(FPAIR, -1, P, TILE_N)
    out = []
    for k in range(FPAIR):
        out += [gate[k], value[k]] + ([down[k - 1]] if k else [])
    return out + [down[FPAIR - 1]]


def chunked(v):
    return v.reshape(-1, P).T


def cols_of(i):
    pages = np.zeros((DEPTH + 1, P, COL_N), np.float32)

    def put(page, at, name, value):
        pages[page, :, at[name]:at[name] + value.shape[1]] = value

    def taps(w):
        return w.reshape(3, -1, P).transpose(2, 1, 0).reshape(P, -1)

    for l in range(DEPTH):
        lam_init = 0.8 - 0.6 * float(np.exp(-0.3 * l))
        put(l, COL1, "ln_g", chunked(i["ln_g"][l].reshape(-1)))
        put(l, COL1, "ln_b", chunked(i["ln_b"][l].reshape(-1)))
        put(l, COL1, "subln", chunked(i["subln_g"][l]))
        put(l, COL1, "one_minus", np.full((P, 1), 1.0 - lam_init, np.float32))
        put(l, COL1, "lam_init", np.full((P, 1), lam_init, np.float32))
        put(l, COL1, "sc_w", taps(i["sc_conv_w"][l]))
        put(l, COL1, "ffn_w", taps(i["ffn_conv_w"][l]))
        put(l, COL1, "ffn_b", chunked(i["ffn_conv_b"][l]))
        lam = np.concatenate([i["lam_q1"][l], i["lam_k1"][l], i["lam_q2"][l], i["lam_k2"][l]])
        put(l, COL1, "lam", np.broadcast_to(lam, (P, 256)))
    for name, key in (("g_mem", "g_mem_2"), ("g_pre_mix", "g_pre_mix_2"), ("q_norm", "mla_q_norm_2"),
                      ("kv_norm", "mla_kv_norm_2"), ("b_gate", "b_gate_2"), ("g_pre_ffn", "g_pre_ffn_2"),
                      ("conv_b", "conv_b_2")):
        put(DEPTH, COL2, name, chunked(i[key][0]))
    put(DEPTH, COL2, "conv_w", taps(i["conv_w_2"][0]))
    return pages


def const_of(i):
    c = np.zeros((P, CONST_N), np.float32)

    def put(name, value):
        c[:value.shape[0], CONST[name]:CONST[name] + value.shape[1]] = value

    put("ident", np.eye(P))
    half = 32
    rot = np.zeros((P, P))
    for m in range(0, P, 64):
        for d in range(half):
            rot[m + d + half, m + d] = -1
            rot[m + d, m + d + half] = 1
    put("rot1", rot)
    inv = np.float32(10000.0) ** (-np.arange(half, dtype=np.float32) * np.float32(2.0) / np.float32(64))
    ang = (np.arange(T, dtype=np.float32)[None, :] * inv.astype(np.float32)[:, None]).astype(np.float32)
    put("cos", np.tile(np.cos(ang.astype(np.float64)), (4, 2)))
    put("sin", np.tile(np.sin(ang.astype(np.float64)), (4, 2)))
    put("ones", np.ones((P, P)))
    q, k = np.arange(P)[:, None] % 64, np.arange(64)[None, :]
    start = np.clip(q - 8, 0, 48)
    put("na_mask", np.where((k >= start) & (k < start + 16), 0.0, NEG))
    qi, ki = np.arange(P)[:, None], np.arange(P)[None, :]
    diag = np.where(ki <= qi, 0.0, NEG)
    put("causal", np.concatenate([diag, np.zeros((P, P)), diag], 1))
    rot = np.zeros((P, 96))
    for d in range(16):
        rot[64 + d + 16, 64 + d] = -1
        rot[64 + d, 64 + d + 16] = 1
    put("rot2", rot)
    inv2 = np.float32(10000.0) ** (-np.arange(16, dtype=np.float32) / np.float32(16))
    put("inv", np.tile(inv2, 8)[:, None])
    put("eps_ln", np.full((P, 1), EPS_LN))
    put("eps_rms", np.full((P, 1), EPS_RMS))
    put("emb_g", chunked(i["emb_ln_g"]))
    put("emb_b", chunked(i["emb_ln_b"]))
    return c


def distances():
    out = []
    for window, d in ((128, 1), (512, 4), (2048, 16)):
        for q0, n in ((0, P), (P, T)):
            dist = (q0 + np.arange(P))[:, None] - np.arange(n)[None, :]
            ok = (dist >= 0) & (dist % d == 0) & (dist <= window)
            out.append(np.where(ok, dist, 1e33))
    return np.concatenate(out, 1).astype(np.float32)


def kernel(**inputs):
    import concourse.bacc as _bacc
    from concourse.bass_utils import run_bass_kernel_spmd as _run

    i = {k: np.ascontiguousarray(v) for k, v in inputs.items()}
    zero = np.zeros(D, np.float32)
    rows = np.concatenate([i["emb_ln_g"], i["emb_ln_b"]]
                          + [x for l in range(DEPTH) for k in range(3) for x in (i["ln_g"][l, k], i["ln_b"][l, k])]
                          + [i["g_post_mix_2"][0], zero, i["g_post_ffn_2"][0], zero])
    arrays = {"x": i["x"], "mem": i["mem"], "mem_2": i["mem_2"], "positions_2": i["positions_2"],
              "rpb": i["rpb"].reshape(-1), "stream": stream_of(i), "cols": cols_of(i), "const": const_of(i),
              "distm": distances(), "ln_rows": rows}
    nc = _bacc.Bacc("TRN2", target_bir_lowering=False, num_devices=1)
    aps = {n: nc.dram_tensor(f"in_{n}", v.shape, mybir.dt.from_np(v.dtype), kind="ExternalInput").ap()
           for n, v in arrays.items()}
    aps["bias_scratch"] = nc.dram_tensor("bias_scratch", (DEPTH, P, RPB_H * NJ * 64), F32, kind="Internal").ap()
    out = nc.dram_tensor("out_x", (1, T, D), F32, kind="ExternalOutput").ap()
    build(nc, aps, out)
    r = _run(nc, [{f"in_{n}": v for n, v in arrays.items()}], core_ids=[0])
    return r.results[0]["out_x"]
```

```python
from contextlib import ExitStack

import numpy as np
import concourse.bass as bass
from concourse import mybir

F32 = mybir.dt.float32
F32R = mybir.dt.float32r
I32 = mybir.dt.int32
ACT = mybir.ActivationFunctionType
ALU = mybir.AluOpType
AX = mybir.AxisListType

P = 128
T = 256
D = 1024
DC = D // P
DEPTH = 2
FF = 2816
FC = FF // P
FPAIR = FC // 2
TILE_N = 256
HALF_TILES = 4
HALF_N = HALF_TILES * TILE_N
RAW = 5
SPLIT = 4
HALVES_1 = 178
PERIOD = 180
HALVES_2 = 169
ALPHA = (2.0 * DEPTH) ** 0.25
EPS_LN = 1e-5
EPS_RMS = 1e-6
NEG = -1e30

ROUND = 1.5 * 2.0 ** 23
TWO_PI = (6.28125, 0.0019350051879882812, 2 * 3.141592653589793 - 6.28125 - 0.0019350051879882812)
PI_BELOW = 3.1415925

RPB_H, RPB_R, RPB_C = 8, 15, 31
NJ = 6


def columns(*parts):
    at, n = {}, 0
    for name, width in parts:
        at[name] = n
        n += width
    return at, n


CONST, CONST_N = columns(("ident", P), ("inv", 1), ("eps_ln", 1), ("eps_rms", 1), ("emb_g", DC), ("emb_b", DC),
                         ("rot1", P), ("cos", 2 * T), ("sin", 2 * T), ("ones", P), ("na_mask", 64),
                         ("causal", 384), ("rot2", 96))
CONST_FIRST = CONST["rot1"]
COL1, COL1_N = columns(("ln_g", 3 * DC), ("ln_b", 3 * DC), ("subln", 1), ("one_minus", 1), ("lam_init", 1),
                       ("sc_w", 12), ("ffn_w", 3 * FC), ("ffn_b", FC), ("lam", 256))
COL2, COL2_N = columns(("g_mem", DC), ("g_pre_mix", DC), ("q_norm", 3), ("kv_norm", 2), ("b_gate", 24),
                       ("g_pre_ffn", DC), ("conv_w", 6 * FC), ("conv_b", 2 * FC))
COL_N = max(COL1_N, COL2_N)

SLOPES = np.exp2(-8.0 * np.arange(1, 13, dtype=np.float64) / 12).astype(np.float32).reshape(4, 3).T

COUNTS = {
    "general_full0": (2, 26, 27),
    "general_full1": (2, 26, 26),
    "general_full2": (2, 25, 26),
    "general_full3": (2, 25, 26),
    "weights_half_used": (0, 92, 87),
    "scores_full": (0, 20, 24),
    "probsT_full": (0, 16, 24),
    "attn_out_full": (0, 12, 12),
    "down_full": (0, 4, 4),
    "std_ready": (1, 3, 8),
    "xhat_tile1_ready": (1, 3, 4),
    "general_free0": (2, 26, 27),
    "general_free2": (2, 25, 26),
    "weights_hi_done": (4, 178, 165),
    "xT_gained": (4, 12, 12),
    "general_free1": (2, 26, 26),
    "general_free3": (2, 25, 26),
    "lam_exp": (0, 1, 0),
    "exp_done": (0, 20, 16),
    "probsT_ready": (0, 16, 24),
    "attn_out_read": (0, 12, 12),
    "ya_sq": (0, 1, 0),
    "attn_out_hi": (0, 8, 8),
    "memT_hi_ready": (0, 2, 0),
    "conv_init": (0, 11, 22),
    "silu_done": (0, 11, 11),
    "squares_done": (0, 0, 8),
    "cT_hi_ready": (0, 0, 3),
    "sin_ready": (0, 0, 1),
    "ya_hi_ready": (0, 0, 1),
    "down_product_in": (0, 0, 4),
    "dve_step": (6, 127, 116),
    "var_ready": (1, 3, 0),
    "norm_factors_ready": (1, 3, 5),
    "xhat_tile0_ready": (1, 3, 4),
    "weights_lo_done": (4, 178, 165),
    "lam_sums": (0, 1, 0),
    "rope_ready": (0, 4, 5),
    "neg_max_ready": (0, 20, 16),
    "probs_ready": (0, 16, 16),
    "yc_ready": (0, 4, 0),
    "scores_read": (0, 8, 20),
    "ya_ready": (0, 4, 0),
    "merge_step": (0, 12, 12),
    "merged_ready": (0, 4, 4),
    "memT_lo_ready": (0, 2, 0),
    "ffn_act_ready": (0, 11, 11),
    "angle_ready": (0, 0, 1),
    "ya_lo_ready": (0, 0, 1),
    "square_sums_ready": (0, 0, 1),
    "z_tile0_added": (0, 0, 1),
    "z_ready": (0, 0, 1),
    "out_tile_ready": (0, 0, 2),
    "rows_in": (1, 3, 2),
    "cols_in": (1, 1, 0),
    "pool_step": (2, 6, 0),
    "x_tile0_ready": (1, 3, 0),
    "x_ready": (1, 3, 0),
    "bias_built": (32, 0, 0),
    "bias_in": (0, 1, 0),
    "bias_ready": (0, 1, 0),
    "mem2_in": (0, 0, 1),
    "pos_in": (0, 0, 1),
    "dil_in": (0, 0, 1),
    "x_in": (1, 0, 0),
    "const_in": (1, 0, 0),
    "mem_in": (1, 0, 0),
    "weights_landed0": (1, 36, 33),
    "weights_landed1": (1, 36, 33),
    "weights_landed2": (1, 36, 33),
    "weights_landed3": (1, 35, 33),
    "weights_landed4": (1, 35, 32),
    "tables_in": (1, 0, 0),
    "out_done": (0, 0, 2),
}


class Signal:

    def __init__(self, name, sem, unit, stage):
        self.name, self.sem, self.unit, self.stage = name, sem, unit, stage
        self.pro, self.per, self.post = COUNTS.get(name, (0, 0, 0))

    def at(self, n):
        return self.sem, self.unit * (self.stage.base(self) + n + 1)

    def last(self):
        return self.at(self.stage.said[self.name] - 1)

    def more(self):
        self.stage.count(self)
        return self.sem, self.unit


class Stage:

    def __init__(self):
        self.kind, self.layer, self.said, self.seen = "pro", 0, {}, {}

    def enter(self, kind, layer=0):
        self.kind, self.layer, self.said = kind, layer, {}

    def base(self, s):
        if self.kind == "pro":
            return 0
        if self.kind == "layer":
            return s.pro + self.layer * s.per
        return s.pro + DEPTH * s.per

    def count(self, s, k=1):
        self.said[s.name] = self.said.get(s.name, 0) + k
        which = ("pro", "layer", "post").index(self.kind)
        self.seen.setdefault(s.name, [0, 0, 0])[which] += k


def jobs_of(kind):
    sets = {"layer": (("da", 8), ("na", 8), ("xa", 4)), "post": (("mla", 8), ("dil", 4), ("mem", 4))}[kind]
    return [(name, i) for name, n in sets for i in range(n)]


def parts_of(name):
    return 3 if name == "dil" else 1


def build(nc, a, out):
    stage = Stage()
    ctx = ExitStack()
    with ctx:
        def signal(name, unit=1):
            return Signal(name, ctx.enter_context(nc.semaphore(name)), unit, stage)

        sizes = (("raw", RAW * HALF_N), ("w_hi", SPLIT * HALF_N), ("w_lo", SPLIT * HALF_N), ("x", 2 * D), ("z", 2 * D),
                 ("xT_hi", 2 * D), ("xT_lo", 2 * D), ("memT", 2 * D), ("big", 24 * T), ("y", 12 * T),
                 ("exp", 3 * 1152), ("pT", 4 * 512), ("const", CONST_N), ("col", COL_N), ("area", 48 * T),
                 ("stat", 24), ("nst", 112))
        base = -(-nc.sbuf_base // 32) * 32
        top = base
        place = {}
        for name, width in sizes:
            place[name] = top
            top += -(-width // 8) * 32
        arena = ctx.enter_context(nc.sbuf_tensor("arena", [P, (top - nc.sbuf_base) // 4], F32))

        def sb(name, cols, where=None, col0=0, dt=F32):
            return nc.alloc_sbuf_tensor_at(name, [P, cols], dt, offset=place[where or name] + 4 * col0)

        raw_ring = sb("raw_weights", RAW * HALF_N, "raw")
        w_hi = sb("weights_hi", SPLIT * HALF_N, "w_hi", dt=F32R)
        w_lo = sb("weights_lo", SPLIT * HALF_N, "w_lo", dt=F32R)
        x_tok = sb("x_tok", 2 * D, "x")
        z_tok = sb("z_tok", 2 * D, "z")
        xT_hi, xT_lo = (sb(f"xT_{k}_part", 2 * D, f"xT_{k}", dt=F32R) for k in ("hi", "lo"))
        memT = sb("memory_T", 2 * D, "memT")
        big = sb("gates", 24 * T, "big")
        mT_hi, mT_lo = (sb(f"memT_{k}", 8 * T, "big", c, F32R) for k, c in (("hi", 8 * T), ("lo", 16 * T)))
        yT = sb("attn_outputs", 12 * T, "y")
        yb_hi, yb_lo = (sb(f"second_branch_{k}", 4 * T, "y", c, F32R) for k, c in (("hi", 0), ("lo", 4 * T)))
        e_ring = sb("exp_ring", 3 * 1152, "exp")
        pT = sb("probsT_ring", 4 * 512, "pT")
        const = sb("constants", CONST_N, "const")
        col = sb("param_cols", COL_N, "col")
        area = sb("attention_area", 48 * T, "area")
        ya_hi, ya_lo = (sb(f"first_branch_{k}", 4 * T, "area", c, F32R) for k, c in (("hi", 0), ("lo", 4 * T)))
        yc_hi, yc_lo = (sb(f"third_branch_{k}", 4 * T, "area", c, F32R) for k, c in (("hi", 28 * T), ("lo", 32 * T)))
        mg_hi, mg_lo = (sb(f"merged_{k}", 8 * T, "area", c, F32R) for k, c in (("hi", 8 * T), ("lo", 16 * T)))
        xo_hi, xo_lo = (sb(f"memory_out_{k}", 8 * T, "area", c, F32R) for k, c in (("hi", 24 * T), ("lo", 32 * T)))
        rows = area[:, 40 * T:48 * T]
        stat = sb("softmax_stats", 24, "stat")
        nst = sb("norm_stats", 112, "nst")

        def mat(tile, c0, n, w=T):
            return tile[:, c0:c0 + n * w].rearrange("p (c w) -> p c w", w=w)

        x3, z3 = mat(x_tok, 0, 2, D), mat(z_tok, 0, 2, D)
        memT3, big3, yT3 = mat(memT, 0, DC), mat(big, 0, 24), mat(yT, 0, 12)
        XT = mat(xT_hi, 0, DC), mat(xT_lo, 0, DC)
        MT = mat(mT_hi, 0, DC), mat(mT_lo, 0, DC)
        YB = mat(yb_hi, 0, 4), mat(yb_lo, 0, 4)
        YA = mat(ya_hi, 0, 4), mat(ya_lo, 0, 4)
        YC = mat(yc_hi, 0, 4), mat(yc_lo, 0, 4)
        MG = mat(mg_hi, 0, 8), mat(mg_lo, 0, 8)
        XO = mat(xo_hi, 0, 8), mat(xo_lo, 0, 8)
        ident = const[:, CONST["ident"]:CONST["ident"] + P]
        ones = const[:, CONST["ones"]:CONST["ones"] + P]
        cos2 = const[:, CONST["cos"]:CONST["cos"] + 2 * T]
        sin2 = const[:, CONST["sin"]:CONST["sin"] + 2 * T]
        qa, ka = mat(area, 0, 4), mat(area, 4 * T, 4)
        va = mat(area, 8 * T, 2, 512)
        qn, kn = mat(area, 12 * T, 4), mat(area, 16 * T, 4)
        vn = mat(area, 20 * T, 2, 512)
        gb, cin = mat(area, 24 * T, 4), mat(area, 28 * T, 4)
        gc = mat(area, 32 * T, 4)
        bias_tab = area[:, 36 * T:48 * T].rearrange("p (h j k) -> p h j k", h=8, j=NJ)
        conv_tmp = mat(z_tok, 0, 4)
        ya_rms = mat(z_tok, 4 * T, 4)
        raw = mat(big, 0, 8)
        scratch = mat(e_ring, 2048, 2, 512)
        xq, xk = mat(area, 0, 8), mat(area, 8 * T, 8)
        xv = mat(area, 16 * T, 2, D)
        qm = mat(z_tok, 0, 8)
        km = mat(area, 0, 8)
        vm = mat(area, 8 * T, 2, 512)
        mk, mq = mat(area, 12 * T, 4), mat(area, 16 * T, 4)
        mv = mat(area, 20 * T, 2, 512)
        dq, dk = mat(area, 24 * T, 12), mat(area, 36 * T, 12)
        dv = mat(area, 0, 2, 1536)
        mem2 = mat(area, 12 * T, 2, D)
        cz = mat(e_ring, 0, 2, 768)
        kraw = big[:, 0:T]
        angle, half_sine = big[:, 2 * T:3 * T], big[:, 3 * T:4 * T]
        turns, pos_int = big[:, 4 * T:5 * T], big[:, 5 * T:6 * T].bitcast(I32)
        junk = mat(yT, 0, 2, D)
        distm = z_tok[:, 0:3 * 384].rearrange("p (g w) -> p g w", g=3)
        dbias = z_tok[:, 3 * 384:5 * 384].rearrange("p (b w) -> p b w", b=2)
        merge_tmp = mat(z_tok, 0, 4, 512)
        gain_tmp = mat(pT, 0, 4, 512)
        mem_tok = mat(area, 0, 2, D)
        block_sums = nst[:, 64:72].rearrange("p (t b) -> p t b", t=2)

        def colp(name, i=0, packed=COL1):
            return col[:, packed[name] + i:packed[name] + i + 1]

        def cconst(name, i=0):
            return const[:, CONST[name] + i:CONST[name] + i + 1]

        ps = [ctx.enter_context(nc.psum_tensor(f"general{b}", [P, 512], F32)) for b in range(4)]
        sc = [ctx.enter_context(nc.psum_tensor(f"scores{b}", [P, 512], F32)) for b in range(2)]
        tp = ctx.enter_context(nc.psum_tensor("probs_transposed", [P, 512], F32))
        po = ctx.enter_context(nc.psum_tensor("attention_out", [P, 512], F32))
        down = [sc[0], sc[1], tp, po]

        const_in = signal("const_in", 16)
        xin = signal("x_in", 16)
        memin = signal("mem_in", 16)
        tables_in = signal("tables_in", 16)
        bias_built = signal("bias_built", 16)
        landed = [signal(f"weights_landed{s}", 16) for s in range(RAW)]
        hi_done = signal("weights_hi_done")
        lo_done = signal("weights_lo_done")
        half_used = signal("weights_half_used")
        x_gained = signal("xT_gained")
        cT_hi = signal("cT_hi_ready")
        out_hi = signal("attn_out_hi")
        mem_hi = signal("memT_hi_ready")
        mem_lo = signal("memT_lo_ready")
        ya_hi_ready = signal("ya_hi_ready")
        ya_lo_ready = signal("ya_lo_ready")
        down_full = signal("down_full")
        z_in = signal("down_product_in")
        cols_in = signal("cols_in", 16)
        rows_in = signal("rows_in", 16)
        bias_in = signal("bias_in", 16)
        bias_ready = signal("bias_ready")
        full = [signal(f"general_full{b}") for b in range(4)]
        free = [signal(f"general_free{b}") for b in range(4)]
        sc_full = signal("scores_full")
        sc_read = signal("scores_read")
        tp_full = signal("probsT_full")
        pT_ready = signal("probsT_ready")
        po_full = signal("attn_out_full")
        po_read = signal("attn_out_read")
        nmax = signal("neg_max_ready")
        exp_done = signal("exp_done")
        p_ready = signal("probs_ready")
        dve_step = signal("dve_step")
        pool_step = signal("pool_step")
        squares_done = signal("squares_done")
        square_sums = signal("square_sums_ready")
        var_ready = signal("var_ready")
        std_ready = signal("std_ready")
        norm_factors = signal("norm_factors_ready")
        xhat0 = signal("xhat_tile0_ready")
        xhat1 = signal("xhat_tile1_ready")
        x_tile0 = signal("x_tile0_ready")
        x_ready = signal("x_ready")
        rope_ready = signal("rope_ready")
        ya_sq = signal("ya_sq")
        ya_ready = signal("ya_ready")
        yc_ready = signal("yc_ready")
        merged_ready = signal("merged_ready")
        merge_step = signal("merge_step")
        conv_init = signal("conv_init")
        silu_done = signal("silu_done")
        act_ready = signal("ffn_act_ready")
        z_ready = signal("z_ready")
        lam_sum = signal("lam_sums")
        lam_exp = signal("lam_exp")
        angle_ready = signal("angle_ready")
        sin_ready = signal("sin_ready")
        dil_in = signal("dil_in", 16)
        pos_in = signal("pos_in", 16)
        mem2_in = signal("mem2_in", 16)
        z_tile0 = signal("z_tile0_added")
        out_ready = signal("out_tile_ready")
        out_done = signal("out_done", 16)

        FILLS, LAST_USE, AT, DOWN_HALF = {}, {}, {}, {}
        ORDER = {"layer": jobs_of("layer"), "post": jobs_of("post")}

        def fill_of(key):
            return FILLS[(stage.kind, key)]

        def need_last_phase(eng):
            for b in range(4):
                eng.wait_ge(*free[b].at(-1))


        def in_phase():
            return {"layer": HALVES_1, "post": HALVES_2}[stage.kind]

        def is_half(h):
            return stage.kind == "post" or not HALVES_1 <= h < PERIOD

        def split_index(h):
            return h - SPLIT - (PERIOD - HALVES_1 if stage.kind == "layer" and h >= PERIOD else 0)

        def when_landed(h):
            skipped = stage.kind == "layer" and h >= PERIOD and h % RAW in [k % RAW for k in range(HALVES_1, PERIOD)]
            return landed[h % RAW].at(h // RAW - 1 - skipped)

        def raw_half(h):
            return raw_ring[:, (h % RAW) * HALF_N:(h % RAW + 1) * HALF_N]

        def hi_half(h):
            return w_hi[:, (h % SPLIT) * HALF_N:(h % SPLIT + 1) * HALF_N]

        def lo_half(h):
            return w_lo[:, (h % SPLIT) * HALF_N:(h % SPLIT + 1) * HALF_N]

        def split_limit(at):
            return 0 if stage.kind == "pro" else min(at + SPLIT, in_phase())

        def cbuf(i, k):
            return e_ring[:, (2 * i + k) * 512:(2 * i + k) * 512 + 512]

        def sbuf(i):
            return e_ring[:, 2048 + (i % 2) * 512:2048 + (i % 2) * 512 + 512]

        def need_exp_buffer(eng, j):
            k = j - 3
            if k < 0:
                return
            name, i = ORDER[stage.kind][k]
            if k not in NUM[stage.kind][3]:
                eng.wait_ge(*p_ready.at(NUM[stage.kind][3][k + 1]))
            else:
                eng.wait_ge(*tp_full.at(NUM[stage.kind][1][(k, parts_of(name) - 1)]))

        def bank_of(key):
            return ps[fill_of(key)[0]]

        def when_full(key):
            b, n = fill_of(key)
            return full[b].at(n)

        def when_read(key):
            b, n = fill_of(key)
            return free[b].at(n)

        def read(key):
            return free[fill_of(key)[0]].more()

        def numbering(kind):
            scores, transposes, outs, probs, owner = {}, {}, {}, {}, []
            for j, (name, i) in enumerate(ORDER[kind]):
                for g in range(parts_of(name)):
                    scores[(j, g)] = len(scores)
                    owner.append(j)
                if name != "da" or i % 2 == 1:
                    probs[j] = len(probs)
                    for g in range(parts_of(name)):
                        transposes[(j, g)] = len(transposes)
                if name not in ("da", "na", "mla") or i % 2 == 1:
                    outs[j] = len(outs)
            return scores, transposes, outs, probs, owner

        NUM = {k: numbering(k) for k in ORDER}
        READS = {}
        for kind in ORDER:
            n = 0
            for j, (name, i) in enumerate(ORDER[kind]):
                for g in range(parts_of(name)):
                    if name in ("na", "mla", "dil"):
                        READS[(kind, j, g)] = n
                        n += 1

        def spans(name):
            return ((0, 128), (128, 384)) if name in ("mla", "dil") else ((0, 256), (256, 512))

        def exp_views(j, t):
            name, _ = ORDER[stage.kind][j]
            lo, hi = spans(name)[t]
            e = e_ring[:, (j % 3) * 1152:(j % 3) * 1152 + 1152]
            if name == "dil":
                return e.rearrange("p (g w) -> p g w", g=3)[:, :, lo:hi]
            return e[:, lo:hi]

        def st(kind, j, t0=0, t1=2):
            o = {"mx": 0, "nm": 6, "sum": 12, "rec": 18}[kind] + 2 * (j % 3)
            return stat[:, o + t0:o + t1]

        def set_jobs(name):
            return [j for j, (s, _) in enumerate(ORDER[stage.kind]) if s == name]

        def step_slots(fillers, n):
            slots = [[] for _ in range(n)]
            each, extra = divmod(len(fillers), n - 2)
            k = 0
            for i in range(n - 2):
                take = each + (i < extra)
                slots[1 + i] = fillers[k:k + take]
                k += take
            return slots

        def blocks(name, n0, n1):
            return [(name, i) for i in range(n0, n1)]

        da_fillers = step_slots(blocks("gc", 0, 2) + blocks("hc", 0, 2) + blocks("gb", 0, 2) + blocks("kn", 0, 2)
                                + blocks("vn", 0, 2), 10)
        na_fillers = [[]] + [blocks("gate", k, k + n) for k, n in ((0, 1), (1, 2), (3, 2), (5, 2), (7, 2), (9, 1),
                                                                   (10, 1), (11, 1))] + [[]]
        xa_fillers = step_slots(blocks("xv", 0, 4), 6)
        mla_fillers = step_slots(blocks("mv", 1, 2) + blocks("gate", 0, 4) + blocks("dq", 0, 3), 10)
        dil_fillers = [[("dv", 0)], [("dv", 2), ("dv", 4)], [("dv", 1), ("dv", 3)], [("dv", 5), ("gate", 4)],
                       blocks("gate", 5, 7), [("gate", 7)]]
        mem_fillers = step_slots(blocks("gate", 8, 12), 6)

        SCALE = {"da": 0.125, "na": 0.125, "xa": 1.0 / 16, "mla": 96.0 ** -0.5, "dil": 128.0 ** -0.5,
                 "mem": 128.0 ** -0.5}

        def out_place(name, i):
            if name == "xa":
                at, parts, src = slice(2 * i, 2 * i + 2), XO, po[:, :].rearrange("p (c w) -> p c w", w=T)
            elif name == "mem":
                at, parts, src = i, YC, po[:, 0:T]
            else:
                at, parts, src = i // 2, YB, po[:, 0:T]
            return [part[:, at, :] for part in parts], src

        block = ctx.enter_context(nc.Block())

        @block.tensor
        def _(pe):
            state = {"tile": 0, "bank": 0, "uses": [0] * 4}

            def start_phase(kind, l=0):
                stage.enter(kind, l)
                state["tile"], state["bank"], state["uses"] = 0, 0, [0] * 4

            def open_bank(key):
                b = state["bank"] % 4
                state["bank"] += 1
                n = state["uses"][b]
                state["uses"][b] += 1
                FILLS[(stage.kind, key)] = (b, n)
                if n > 0 or stage.kind != "pro":
                    pe.wait_ge(*free[b].at(n - 1))
                return b

            def half_at(g):
                h = g // HALF_TILES
                if g % HALF_TILES == 0:
                    pe.wait_ge(*lo_done.at(split_index(h)))
                c = (h % SPLIT) * HALF_N + g % HALF_TILES * TILE_N
                return w_hi[:, c:c + TILE_N], w_lo[:, c:c + TILE_N]

            def linear(key, act, kcs, feature_major, m=P, before=None):
                b = open_bank(key)
                g0 = state["tile"]
                state["tile"] += kcs
                AT[(stage.kind, key)] = (g0 + kcs - 1) // HALF_TILES
                for kc in range(kcs):
                    if before:
                        before(kc)
                    g = g0 + kc
                    w = half_at(g)
                    x = [part[:, kc, :] for part in act]
                    for half in range(2):
                        for n, (wk, xk_) in enumerate(((0, 0), (0, 1), (1, 0))):
                            first = kc == 0 and half == 0 and n == 0
                            last = kc == kcs - 1 and half == 1 and n == 2
                            if feature_major:
                                ins = nc.tensor.matmul(ps[b][0:m, half * T:half * T + T],
                                                       w[wk][:, half * m:half * m + m], x[xk_], start=first, stop=last,
                                                       skip_group_check=True)
                            else:
                                ins = nc.tensor.matmul(ps[b][:, half * T:half * T + T],
                                                       x[wk][:, half * P:half * P + P], w[xk_], start=first, stop=last,
                                                       skip_group_check=True)
                    if kc == kcs - 1:
                        ins.then_inc(*full[b].more())
                        if g % HALF_TILES == HALF_TILES - 1:
                            LAST_USE[(stage.kind, g // HALF_TILES)] = (full[b], FILLS[(stage.kind, key)][1])
                    elif g % HALF_TILES == HALF_TILES - 1:
                        LAST_USE[(stage.kind, g // HALF_TILES)] = (half_used, stage.said.get(half_used.name, 0))
                        ins.then_inc(*half_used.more())

            def down_product(i):
                pe.wait_ge(*act_ready.at(i))
                act = [part[:, 2 * (i % 2):2 * (i % 2) + 2, :] for part in YA]
                g = state["tile"]
                state["tile"] += 2 * HALF_TILES
                DOWN_HALF[(stage.kind, i)] = (g + HALF_TILES) // HALF_TILES
                last = i == FPAIR - 1
                blocks_of_pair = [(kc, t, c) for kc in range(2) for t in range(2) for c in range(2)]
                if last:
                    half_at(g)
                    half_at(g + HALF_TILES)
                    blocks_of_pair.sort(key=lambda b: b[1:])
                for kc, t, c in blocks_of_pair:
                    h = g // HALF_TILES + kc
                    if not last and (t, c) == (0, 0):
                        half_at(h * HALF_TILES)
                    w = hi_half(h), lo_half(h)
                    for n, (xk_, wk) in enumerate(((0, 0), (0, 1), (1, 0))):
                        ins = nc.tensor.matmul(down[2 * t + c][:, :], act[xk_][:, kc, t * P:t * P + P],
                                               w[wk][:, c * 512:c * 512 + 512], start=(i + kc + n == 0),
                                               stop=(last and kc == 1 and n == 2), skip_group_check=True)
                    if last and kc == 1:
                        ins.then_inc(*down_full.more())
                    elif not last and (t, c) == (1, 1):
                        LAST_USE[(stage.kind, h)] = (half_used, stage.said.get(half_used.name, 0))
                        ins.then_inc(*half_used.more())
                if last:
                    for kc in range(2):
                        LAST_USE[(stage.kind, g // HALF_TILES + kc)] = (down_full, 3)

            def transposes(key, src, n0):
                b = open_bank(key)
                for c in range(2):
                    for t in range(2):
                        ins = nc.tensor.transpose(ps[b][:, c * T + t * P:c * T + t * P + P],
                                                  src[:, t, (n0 + c) * P:(n0 + c) * P + P], ident)
                ins.then_inc(*full[b].more())
                AT[(stage.kind, key)] = state["tile"] // HALF_TILES

            def to_feature(name, src):
                for i in range(DC // 2):
                    transposes((name, i), src, 2 * i)

            def job(j):
                return ORDER[stage.kind][j]

            def mark(event, j):
                AT[(stage.kind, (event, j))] = state["tile"] // HALF_TILES

            def scores(j):
                name, i = job(j)
                mark("scores", j)
                number = NUM[stage.kind][0]
                for g in range(parts_of(name)):
                    n = number[(j, g)]
                    if n >= 2:
                        jj = NUM[stage.kind][4][n - 2]
                        gg = n - 2 - number[(jj, 0)]
                        if job(jj)[0] in ("na", "mla", "dil"):
                            pe.wait_ge(*sc_read.at(READS[(stage.kind, jj, gg)]))
                        else:
                            pe.wait_ge(*exp_done.at(jj))
                    dst = sc[n % 2]
                    for t in range(2):
                        lo, hi = spans(name)[t]
                        q0 = t * P
                        if name in ("da", "na"):
                            r0 = 64 * (i % 2)
                            q, k = (qa, ka) if name == "da" else (qn, kn)
                            pairs = [(q[r0:r0 + 64, i // 2, q0:q0 + P], k[r0:r0 + 64, i // 2, :])]
                        elif name == "xa":
                            pairs = [(xq[:, 2 * i + c, q0:q0 + P], xk[:, 2 * i + c, :]) for c in range(2)]
                        elif name == "mla":
                            pairs = [(qm[0:96, i, q0:q0 + P], km[0:96, i, 0:hi - lo])]
                        elif name == "dil":
                            pairs = [(dq[:, 4 * g + i, q0:q0 + P], dk[:, 4 * g + i, 0:hi - lo])]
                        else:
                            pairs = [(mq[:, i, q0:q0 + P], mk[:, i, :])]
                        for c, (q, k) in enumerate(pairs):
                            ins = nc.tensor.matmul(dst[:, lo:hi], q, k, start=(c == 0), stop=(c == len(pairs) - 1))
                    ins.then_inc(*sc_full.more())

            def turn(j):
                name, i = job(j)
                if j not in NUM[stage.kind][3]:
                    return
                mark("turn", j)
                pe.wait_ge(*p_ready.at(NUM[stage.kind][3][j]))
                for g in range(parts_of(name)):
                    n = NUM[stage.kind][1][(j, g)]
                    if n > 0:
                        pe.wait_ge(*pT_ready.at(n - 1))
                    for t in range(2):
                        e = exp_views(j, t)
                        if name == "dil":
                            e = e[:, g, :]
                        for kt in range(2 if spans(name)[t][1] - spans(name)[t][0] == 256 else 1):
                            ins = nc.tensor.transpose(tp[:, kt * T + t * P:kt * T + t * P + P],
                                                      e[:, kt * P:kt * P + P], ident)
                    ins.then_inc(*tp_full.more())

            def values(j):
                name, i = job(j)
                if j not in NUM[stage.kind][3]:
                    return
                parts = parts_of(name)
                mark("values", j)
                pe.wait_ge(*pT_ready.at(NUM[stage.kind][1][(j, parts - 1)]))
                if name == "dil" and i % 2 == 0:
                    for g in range(parts):
                        pe.wait_ge(*when_read(("dv", 2 * g + i // 2)))
                pair = name in ("na", "mla")
                if not (pair and i % 2 == 1):
                    n = NUM[stage.kind][2][j + 1 if pair else j]
                    if n > 0:
                        pe.wait_ge(*po_read.at(n - 1))
                for c in range(2 if name == "xa" else 1):
                    first = True
                    for g in range(parts):
                        slot = NUM[stage.kind][1][(j, g)] % 4
                        for kt in range(2):
                            p = pT[:, slot * 512 + kt * T:slot * 512 + kt * T + T]
                            lo = P if kt == 1 and name in ("mla", "dil") else 0
                            if name == "da":
                                v, r0, m = va[:, kt, (i // 2) * P:(i // 2) * P + P], 0, P
                            elif name == "na":
                                v, r0, m = vn[:, kt, i * 64:i * 64 + 64], 64 * (i % 2), 64
                            elif name == "mla":
                                v, r0, m = vm[:, kt, i * 64:i * 64 + 64], 64 * (i % 2), 64
                            elif name == "xa":
                                v, r0, m = xv[:, kt, (2 * i + c) * P:(2 * i + c) * P + P], 0, P
                            elif name == "dil":
                                v, r0, m = dv[:, kt, (4 * g + i) * P:(4 * g + i) * P + P], 0, P
                            else:
                                v, r0, m = mv[:, kt, i * P:i * P + P], 0, P
                            ins = nc.tensor.matmul(po[r0:r0 + m, c * T + lo:c * T + T], v, p[:, lo:T],
                                                   start=first, stop=(g == parts - 1 and kt == 1))
                            first = False
                if j in NUM[stage.kind][2]:
                    ins.then_inc(*po_full.more())

            def filler(key):
                kind = key[0]
                if kind in ("xv", "mv"):
                    linear(key, MT, DC, False)
                elif kind == "mk":
                    linear(key, MT, DC, True)
                else:
                    linear(key, XT, DC, kind not in ("vn", "dv"))

            def ya_squares():
                pe.wait_ge(*ya_sq.at(0))
                for i in range(2):
                    b = open_bank(("ss", i))
                    AT[(stage.kind, ("ss", i))] = state["tile"] // HALF_TILES
                    nc.tensor.matmul(ps[b][:, :], ones, conv_tmp[:, 2 * i:2 * i + 2, :], start=True,
                                     stop=True).then_inc(*full[b].more())

            def attention(name, fillers, extra={}):
                js = set_jobs(name)
                for step in range(len(js) + 2):
                    if step < len(js):
                        scores(js[step])
                    for key in fillers[step]:
                        filler(key)
                    if step >= 2:
                        values(js[step - 2])
                    if 1 <= step <= len(js):
                        turn(js[step - 1])
                    if step in extra:
                        extra[step]()

            def as_ready(name):
                return lambda kc: pe.wait_ge(*when_read((name, kc // 2))) if kc % 2 == 0 else None

            def branches(parts):
                for cb in range(4):
                    for br, y in enumerate(parts):
                        linear(("branch", cb, br), y, 4, True)

            def project(name, n):
                for cb in range(4):
                    linear((name, cb), MG, DC, False,
                           before=lambda kc: pe.wait_ge(*merged_ready.at(kc // 2)) if cb == 0 and kc % 2 == 0 else None)

            def ffn(source):
                for i in range(FPAIR):
                    linear(("gt", i), XT, DC, True, before=as_ready(source) if i == 0 else None)
                    linear(("up", i), XT, DC, True)
                    if i:
                        down_product(i - 1)
                down_product(FPAIR - 1)

            start_phase("pro")
            pe.wait_ge(*const_in.at(0))
            pe.wait_ge(*memin.at(0))
            to_feature("memT", mem_tok)
            for tile in (xhat0, xhat1):
                pe.wait_ge(*tile.at(0))
            to_feature("xT0", z3)

            with pe.Fori(0, DEPTH) as l:
                start_phase("layer", l)
                for name in ("qa", "ka"):
                    for i in range(2):
                        linear((name, i), XT, DC, True,
                               before=lambda kc: pe.wait_ge(*free[kc // 2].at(-1)) if (name, i) == ("qa", 0) else None)
                for i in range(2):
                    linear(("va", i), XT, DC, False)
                pe.wait_ge(*tables_in.at(-1))
                for n, (name, i) in enumerate((("qa", 0), ("qa", 1), ("ka", 0), ("ka", 1))):
                    pe.wait_ge(*when_read((name, i)))
                    b = open_bank(("rot", n))
                    AT[(stage.kind, ("rot", n))] = state["tile"] // HALF_TILES
                    nc.tensor.matmul(ps[b][:, :], const[:, CONST["rot1"]:CONST["rot1"] + P],
                                         raw[:, 2 * n:2 * n + 2, :], start=True, stop=True).then_inc(*full[b].more())
                for i in range(2):
                    linear(("qn", i), XT, DC, True)
                pe.wait_ge(*rope_ready.at(3))
                pe.wait_ge(*when_read(("va", 1)))
                attention("da", da_fillers)
                for key in (("qn", 0), ("qn", 1), ("kn", 0), ("kn", 1), ("vn", 0), ("vn", 1)):
                    pe.wait_ge(*when_read(key))
                attention("na", na_fillers, {1: ya_squares})
                for signal_, n in ((yc_ready, 3), (po_read, NUM["layer"][2][15]), (ya_ready, 3)):
                    pe.wait_ge(*signal_.at(n))
                branches((YA, YB, YC))
                project("mix", 0)
                pe.wait_ge(*mem_lo.at(1))
                for i in range(4):
                    linear(("xk", i), MT, DC, True)
                for tile in (xhat0, xhat1):
                    pe.wait_ge(*tile.at(0))
                to_feature("ln0", z3)
                for i in range(4):
                    linear(("xq", i), XT, DC, True, before=as_ready("ln0") if i == 0 else None)
                pe.wait_ge(*when_read(("xk", 3)))
                for i in range(4):
                    pe.wait_ge(*when_read(("xq", i)))
                attention("xa", xa_fillers)
                pe.wait_ge(*po_read.at(NUM["layer"][2][19]))
                for cb in range(4):
                    linear(("xo", cb), XO, DC, False)
                for tile in (xhat0, xhat1):
                    pe.wait_ge(*tile.at(1))
                to_feature("ln1", z3)
                ffn("ln1")
                for tile in (xhat0, xhat1):
                    pe.wait_ge(*tile.at(2))
                state["bank"] = 0
                to_feature("ln2", z3)

            start_phase("post")
            for tile in (xhat0, xhat1):
                pe.wait_ge(*tile.at(0))
            to_feature("premix", z3)
            for i in range(3):
                linear(("c", i), XT, DC, False, before=as_ready("premix") if i == 0 else None)
            for tile in (xhat0, xhat1):
                pe.wait_ge(*tile.at(1))
            to_feature("mem2T", mem2)
            for i in range(2):
                filler(("mq", i))
            for tile in (xhat0, xhat1):
                pe.wait_ge(*tile.at(2))
            for i in range(3):
                b = open_bank(("cT", i))
                for c in range(2):
                    lo, w = ((2 * i + c) * P, P) if 2 * i + c < 5 else (576, 96)
                    for t in range(2):
                        ins = nc.tensor.transpose(ps[b][0:w, c * T + t * P:c * T + t * P + P], cz[:, t, lo:lo + w],
                                                  ident)
                ins.then_inc(*full[b].more())
                AT[(stage.kind, ("cT", i))] = state["tile"] // HALF_TILES
            for i in range(4):
                pe.wait_ge(*when_read(("mem2T", i)))
            filler(("mk", 0))
            for i in range(3):
                pe.wait_ge(*when_read(("cT", i)))
            for i in range(4):
                linear(("uq", i), XO, 3, True, m=96)
            for i in range(2):
                linear(("uk", i), [part[:, 3:5, :] for part in XO], 2, True)
            for i in range(2):
                linear(("uv", i), [part[:, 3:5, :] for part in XO], 2, False)
            for i in range(5):
                b = open_bank(("rot2", i))
                AT[(stage.kind, ("rot2", i))] = state["tile"] // HALF_TILES
                if i < 4:
                    pe.wait_ge(*when_read(("uq", i)))
                    src = qm[64:96, 2 * i:2 * i + 2, :]
                else:
                    src = kraw[64:96, :]
                nc.tensor.matmul(ps[b][0:96, 0:512 if i < 4 else T], const[64:96, CONST["rot2"]:CONST["rot2"] + 96],
                                     src, start=True, stop=True).then_inc(*full[b].more())
            for key in (("mk", 1), ("mv", 0)):
                filler(key)
            pe.wait_ge(*rope_ready.at(4))
            for key in (("uk", 0), ("uk", 1), ("uv", 0), ("uv", 1)):
                pe.wait_ge(*when_read(key))
            attention("mla", mla_fillers)
            for name, i in blocks("dq", 3, 6) + blocks("dk", 0, 6):
                linear((name, i), XT, DC, True)
            for key in blocks("dq", 0, 6) + blocks("dk", 0, 6):
                pe.wait_ge(*when_read(key))
            attention("dil", dil_fillers)
            for key in (("mk", 0), ("mk", 1), ("mv", 0), ("mv", 1), ("mq", 0), ("mq", 1)):
                pe.wait_ge(*when_read(key))
            attention("mem", mem_fillers)
            for signal_, n in ((po_read, NUM["post"][2][15]), (ya_lo_ready, 0)):
                pe.wait_ge(*signal_.at(n))
            branches((YB, YA, YC))
            project("wo", 0)
            for tile in (xhat0, xhat1):
                pe.wait_ge(*tile.at(3))
            to_feature("preffn", z3)
            ffn("preffn")

        @block.scalar
        def _(act):
            cursor = {"half": 0}

            def split_to(limit):
                for h in range(cursor["half"], limit):
                    if is_half(h):
                        act.wait_ge(*when_landed(h))
                        if is_half(h - SPLIT):
                            user, n = LAST_USE[(stage.kind, h - SPLIT)]
                            act.wait_ge(*user.at(n))
                        nc.scalar.activation(hi_half(h), raw_half(h), ACT.Copy).then_inc(*hi_done.more())
                cursor["half"] = max(cursor["half"], limit)

            def reach(key):
                split_to(split_limit(AT[(stage.kind, key)]))

            def evacuate(key, dst, func=ACT.Copy, **kw):
                reach(key)
                act.wait_ge(*when_full(key))
                src = bank_of(key)
                nc.scalar.activation(dst, src[:, :].rearrange("p (c w) -> p c w", w=T), func, **kw).then_inc(*read(key))

            def gains(name, gain, bias, between=None):
                for i in range(DC // 2):
                    reach((name, i))
                    act.wait_ge(*when_full((name, i)))
                    src = bank_of((name, i))
                    for c in range(2):
                        part, o = src[:, c * T:c * T + T], gain_tmp[:, i, c * T:c * T + T]
                        if bias is None:
                            ins = nc.scalar.activation(o, part, ACT.Copy, scale=gain(2 * i + c))
                        else:
                            ins = nc.scalar.activation(o, part, ACT.Identity, bias=bias(2 * i + c),
                                                       scale=gain(2 * i + c))
                    ins.then_inc(*x_gained.more())
                    if between:
                        between(i)

            def exps(j):
                name, i = ORDER[stage.kind][j]
                reach(("scores", j))
                act.wait_ge(*nmax.at(j))
                scale = SCALE[name]
                from_psum = name in ("da", "xa", "mem")
                if from_psum:
                    need_exp_buffer(act, j)
                for t in range(2):
                    e = exp_views(j, t)
                    lo, hi = spans(name)[t]
                    src = sc[NUM[stage.kind][0][(j, 0)] % 2][:, lo:hi] if from_psum else e
                    ins = nc.scalar.activation(e, src, ACT.Exp, bias=st("nm", j, t, t + 1),
                                               scale=scale if from_psum else 1.0, accum_out=st("sum", j, t, t + 1))
                ins.then_inc(*exp_done.more())

            def probs_out(j):
                name, i = ORDER[stage.kind][j]
                if j not in NUM[stage.kind][3]:
                    return
                reach(("turn", j))
                for g in range(parts_of(name)):
                    n = NUM[stage.kind][1][(j, g)]
                    act.wait_ge(*tp_full.at(n))
                    if n >= 4:
                        jj = [k for k, v in NUM[stage.kind][1].items() if v == n - 4][0][0]
                        outs = NUM[stage.kind][2]
                        if jj in outs:
                            act.wait_ge(*po_full.at(outs[jj]))
                        else:
                            act.wait_ge(*po_full.at(outs[jj + 1]))
                    slot = n % 4
                    if name in ("mla", "dil"):
                        nc.scalar.activation(pT[:, slot * 512:slot * 512 + T], tp[:, 0:T], ACT.Copy)
                        ins = nc.scalar.activation(pT[:, slot * 512 + 384:slot * 512 + 512], tp[:, 384:512], ACT.Copy)
                    else:
                        ins = nc.scalar.activation(pT[:, slot * 512:slot * 512 + 512], tp[:, :], ACT.Copy)
                    ins.then_inc(*pT_ready.more())

            def attn_out(j):
                name, i = ORDER[stage.kind][j]
                if j not in NUM[stage.kind][2]:
                    return
                reach(("values", j))
                act.wait_ge(*po_full.at(NUM[stage.kind][2][j]))
                if name in ("da", "dil"):
                    c = 8 + (i // 2 if name == "da" else i)
                    nc.scalar.activation(yT3[:, c, :], po[:, 0:T], ACT.Copy).then_inc(*po_read.more())
                else:
                    dst, src = out_place(name, i)
                    nc.scalar.activation(dst[0], src, ACT.Copy).then_inc(*out_hi.more())

            def filler(key):
                kind, i = key
                if kind == "gate":
                    reach(key)
                    act.wait_ge(*when_full(key))
                    src = bank_of(key)
                    if stage.kind == "layer":
                        nc.scalar.activation(big3[:, 2 * i:2 * i + 2, :],
                                             src[:, :].rearrange("p (c w) -> p c w", w=T),
                                             ACT.Sigmoid).then_inc(*read(key))
                    else:
                        for c in range(2):
                            ins = nc.scalar.activation(big3[:, 2 * i + c, :], src[:, c * T:c * T + T], ACT.Sigmoid,
                                                       bias=colp("b_gate", 2 * i + c, COL2), scale=1.0)
                        ins.then_inc(*read(key))
                elif kind in ("gc", "gb", "kn", "mk", "mq", "dq"):
                    dst = {"gc": gc, "gb": gb, "kn": kn, "mk": mk, "mq": mq, "dq": dq}[kind]
                    evacuate(key, dst[:, 2 * i:2 * i + 2, :])
                elif kind in ("vn", "xv", "mv", "dv"):
                    dst = {"vn": vn, "xv": xv, "mv": mv, "dv": dv}[kind]
                    evacuate(key, dst[:, :, i * T:i * T + T])

            def attention(name, fillers, extra={}):
                js = set_jobs(name)
                for step in range(len(js) + 2):
                    if step < len(js):
                        exps(js[step])
                    for key in fillers[step]:
                        filler(key)
                    if step >= 2:
                        attn_out(js[step - 2])
                    if 1 <= step <= len(js):
                        probs_out(js[step - 1])
                    if step in extra:
                        extra[step]()

            def ya_squares():
                act.wait_ge(*po_read.at(NUM["layer"][2][7]))
                act.wait_ge(*yc_ready.at(3))
                nc.scalar.activation(conv_tmp, yT3[:, 8:12, :], ACT.Square).then_inc(*ya_sq.more())

            def ya_roots():
                for i in range(2):
                    reach(("ss", i))
                    act.wait_ge(*when_full(("ss", i)))
                    src = bank_of(("ss", i))
                    nc.scalar.activation(ya_rms[:, 2 * i:2 * i + 2, :],
                                         src[:, :].rearrange("p (c w) -> p c w", w=T), ACT.Sqrt,
                                         bias=cconst("eps_ln"), scale=1.0 / P).then_inc(*read(("ss", i)))

            def ya_split():
                act.wait_ge(*po_read.at(NUM["post"][2][11]))
                nc.scalar.activation(YA[0], yT3[:, 8:12, :], ACT.Copy).then_inc(*ya_hi_ready.more())

            def layer_norm(n):
                act.wait_ge(*var_ready.at(n))
                nc.scalar.activation(nst[:, 52:54], nst[:, 49:52:2], ACT.Sqrt, bias=cconst("eps_ln"),
                                     scale=1.0).then_inc(*std_ready.more())
                act.wait_ge(*norm_factors.at(n))
                nc.scalar.activation(z3[:, 1, :], z3[:, 1, :], ACT.Identity, bias=nst[:, 23:24],
                                     scale=nst[:, 55:56]).then_inc(*xhat1.more())

            def ffn(gates_too, packed, w, b):
                def first_tap(i, k, which):
                    reach((which, i))
                    act.wait_ge(*when_full((which, i)))
                    src = bank_of((which, i))
                    if i >= 2:
                        act.wait_ge(*act_ready.at(i - 2))
                    for c in range(2):
                        ch = (k * FC if gates_too else 0) + 2 * i + c
                        tap = 2 if gates_too else 1
                        ins = nc.scalar.activation(cbuf(i % 2, k)[:, c * T:c * T + T], src[:, c * T:c * T + T],
                                                   ACT.Identity, bias=colp(b, ch, packed),
                                                   scale=colp(w, 3 * ch + tap, packed))
                    ins.then_inc(*conv_init.more())

                for i in range(FPAIR + 1):
                    if i < FPAIR:
                        first_tap(i, 0, "gt")
                    if i >= 1:
                        act.wait_ge(*when_read(("gt", i - 1)))
                        nc.scalar.activation(sbuf(i - 1), cbuf((i - 1) % 2, 0), ACT.Silu).then_inc(*silu_done.more())
                    if i < FPAIR and gates_too:
                        first_tap(i, 1, "up")

            stage.enter("pro")
            act.wait_ge(*const_in.at(0))
            layer_norm(0)
            for i in (0, 2):
                act.wait_ge(*when_full(("memT", i)))
                src = bank_of(("memT", i))
                nc.scalar.activation(memT3[:, 2 * i:2 * i + 2, :], src[:, :].rearrange("p (c w) -> p c w", w=T),
                                     ACT.Copy).then_inc(*read(("memT", i)))

            def first_split(h):
                act.wait_ge(*landed[h].at(0))
                nc.scalar.activation(hi_half(h), raw_half(h), ACT.Copy).then_inc(*hi_done.more())

            first_split(0)
            gains("xT0", lambda c: cconst("emb_g", c), lambda c: cconst("emb_b", c),
                  lambda i: first_split(i) if i else None)

            with act.Fori(0, DEPTH) as l:
                stage.enter("layer", l)
                cursor["half"] = SPLIT
                need_last_phase(act)
                for n, (name, i) in enumerate((("qa", 0), ("qa", 1), ("ka", 0), ("ka", 1))):
                    evacuate((name, i), raw[:, 2 * n:2 * n + 2, :])
                for i in range(2):
                    evacuate(("va", i), va[:, :, i * T:i * T + T])
                reach(("rot", 3))
                act.wait_ge(*lam_sum.at(0))
                nc.scalar.activation(nst[:, 58:60], nst[:, 56:58], ACT.Exp).then_inc(*lam_exp.more())
                for i in range(2):
                    evacuate(("qn", i), qn[:, 2 * i:2 * i + 2, :])
                attention("da", da_fillers)
                attention("na", na_fillers, {0: ya_squares, 2: ya_roots})
                reach(("branch", 3, 2))
                act.wait_ge(*when_read(("branch", 3, 2)))
                for k in range(2):
                    nc.scalar.activation(MT[0][:, 4 * k:4 * k + 4, :], memT3[:, 4 * k:4 * k + 4, :],
                                         ACT.Copy).then_inc(*mem_hi.more())
                reach(("mix", 3))
                layer_norm(0)
                for i in range(4):
                    evacuate(("xk", i), xk[:, 2 * i:2 * i + 2, :])
                gains("ln0", lambda c: colp("ln_g", c), lambda c: colp("ln_b", c))
                for i in range(4):
                    evacuate(("xq", i), xq[:, 2 * i:2 * i + 2, :])
                attention("xa", xa_fillers)
                reach(("xo", 3))
                layer_norm(1)
                gains("ln1", lambda c: colp("ln_g", DC + c), lambda c: colp("ln_b", DC + c))
                ffn(False, COL1, "ffn_w", "ffn_b")
                split_to(in_phase())
                layer_norm(2)
                split_to(PERIOD + 1)
                gains("ln2", lambda c: colp("ln_g", 2 * DC + c), lambda c: colp("ln_b", 2 * DC + c),
                      lambda i: split_to(PERIOD + 1 + i))

            stage.enter("post")
            cursor["half"] = SPLIT

            def mean_square(src, width, n0, first=None, both=None):
                for t in range(2):
                    if first:
                        producer, n = (first, both)[t]
                        act.wait_ge(*producer.at(n))
                    ins = nc.scalar.activation(junk[:, t, 0:width], src[:, t, 0:width], ACT.Square,
                                               accum_out=nst[:, n0 + t:n0 + t + 1])
                ins.then_inc(*squares_done.more())
                act.wait_ge(*squares_done.last())
                nc.scalar.activation(nst[:, n0 + 8:n0 + 10], nst[:, n0:n0 + 2], ACT.Sqrt,
                                         bias=cconst("eps_rms"), scale=1.0 / width).then_inc(*std_ready.more())

            def load_sqrt():
                nc.scalar.activation(nst[:, 62:63], cconst("eps_rms"), ACT.Sqrt)

            def scale_tile1(n, dst, src, factor):
                act.wait_ge(*norm_factors.at(n))
                nc.scalar.activation(dst, src, ACT.Copy, scale=factor).then_inc(*xhat1.more())

            mean_square(x3, D, 0, (x_tile0, -1), (x_ready, -1))
            scale_tile1(0, z3[:, 1, :], x3[:, 1, :], nst[:, 17:18])
            act.wait_ge(*cols_in.at(-1))
            gains("premix", lambda c: colp("g_pre_mix", c, COL2), None)
            act.wait_ge(*mem2_in.at(0))
            mean_square(mem2, D, 2)
            scale_tile1(1, mem2[:, 1, :], mem2[:, 1, :], nst[:, 19:20])
            for i in range(3):
                evacuate(("c", i), cz[:, :, i * T:i * T + T])
            gains("mem2T", lambda c: colp("g_mem", c, COL2), None)
            act.wait_ge(*when_read(("c", 2)))
            for lo, w, n0 in ((0, 384, 4), (384, 256, 6)):
                mean_square(cz[:, :, lo:lo + w], w, n0)
            act.wait_ge(*norm_factors.at(3))
            for lo, w, at in ((0, 384, 21), (384, 256, 23)):
                ins = nc.scalar.activation(cz[:, 1, lo:lo + w], cz[:, 1, lo:lo + w], ACT.Copy, scale=nst[:, at:at + 1])
            ins.then_inc(*xhat1.more())
            for i in range(2):
                filler(("mq", i))
            for i in range(3):
                reach(("cT", i))
                act.wait_ge(*when_full(("cT", i)))
                src = bank_of(("cT", i))
                for c in range(2):
                    k = 2 * i + c
                    if k < 5:
                        g = colp("q_norm", k, COL2) if k < 3 else colp("kv_norm", k - 3, COL2)
                        ins = nc.scalar.activation(XO[0][:, k, :], src[:, c * T:c * T + T], ACT.Copy, scale=g)
                    else:
                        ins = nc.scalar.activation(kraw[64:96, :], src[64:96, c * T:c * T + T], ACT.Copy)
                ins.then_inc(*cT_hi.more())
            filler(("mk", 0))
            act.wait_ge(*angle_ready.at(0))
            nc.scalar.activation(sin2[64:96, 0:T], angle[64:96, :], ACT.Sin)
            nc.scalar.activation(sin2[64:96, T:2 * T], angle[64:96, :], ACT.Sin)
            nc.scalar.activation(half_sine[64:96, :], angle[64:96, :], ACT.Sin, scale=0.5).then_inc(*sin_ready.more())
            for i in range(4):
                reach(("uq", i))
                act.wait_ge(*when_full(("uq", i)))
                src = bank_of(("uq", i))
                nc.scalar.activation(qm[0:96, 2 * i:2 * i + 2, :], src[0:96, :].rearrange("p (c w) -> p c w", w=T),
                                     ACT.Copy).then_inc(*read(("uq", i)))
            for i in range(2):
                reach(("uk", i))
                act.wait_ge(*when_full(("uk", i)))
                src = bank_of(("uk", i))
                for par in range(2):
                    ins = nc.scalar.activation(km[0:64, 4 * i + par:4 * i + par + 3:2, :],
                                               src[64 * par:64 * par + 64, :].rearrange("p (c w) -> p c w", w=T),
                                               ACT.Copy)
                ins.then_inc(*read(("uk", i)))
            for i in range(2):
                evacuate(("uv", i), vm[:, :, i * T:i * T + T])
            for key in (("mk", 1), ("mv", 0)):
                filler(key)
            attention("mla", mla_fillers)
            for name, i in blocks("dq", 3, 6) + blocks("dk", 0, 6):
                evacuate((name, i), (dq if name == "dq" else dk)[:, 2 * i:2 * i + 2, :])
            attention("dil", dil_fillers)
            attention("mem", mem_fillers, {0: ya_split})
            for cb in range(4):
                evacuate(("wo", cb), z3[:, :, cb * T:cb * T + T])
                if cb == 2:
                    load_sqrt()
                act.wait_ge(*when_read(("wo", cb)))
                for t in range(2):
                    ins = nc.scalar.activation(junk[:, t, cb * T:cb * T + T], z3[:, t, cb * T:cb * T + T], ACT.Square,
                                               accum_out=block_sums[:, t, cb:cb + 1])
            ins.then_inc(*squares_done.more())
            act.wait_ge(*square_sums.at(0))
            nc.scalar.activation(nst[:, 8:10], nst[:, 0:2], ACT.Sqrt, bias=cconst("eps_rms"),
                                 scale=1.0 / D).then_inc(*std_ready.more())
            reach(("preffn", 0))
            mean_square(x3, D, 2, (z_tile0, 0), (z_ready, 0))
            scale_tile1(4, z3[:, 1, :], x3[:, 1, :], nst[:, 19:20])
            gains("preffn", lambda c: colp("g_pre_ffn", c, COL2), None)
            ffn(True, COL2, "conv_w", "conv_b")
            split_to(in_phase())
            load_sqrt()
            for t in range(2):
                for c in range(2):
                    act.wait_ge(*down_full.at(2 * t + c))
                    nc.scalar.activation(z3[:, t, c * 512:c * 512 + 512], down[2 * t + c][:, :],
                                         ACT.Copy).then_inc(*z_in.more())
                act.wait_ge(*z_in.at(2 * t + 1))
                nc.scalar.activation(junk[:, t, :], z3[:, t, :], ACT.Square,
                                     accum_out=nst[:, 4 + t:5 + t]).then_inc(*squares_done.more())
                act.wait_ge(*squares_done.last())
                nc.scalar.activation(nst[:, 12 + t:13 + t], nst[:, 4 + t:5 + t], ACT.Sqrt, bias=cconst("eps_rms"),
                                     scale=1.0 / D).then_inc(*std_ready.more())

        @block.vector
        def _(dve):
            def halves(src):
                return src[:, :].rearrange("p (c w) -> p c w", w=T)

            cursor = {"half": 0}

            def split_to(limit):
                for h in range(cursor["half"], limit):
                    if is_half(h):
                        dve.wait_ge(*hi_done.at(split_index(h)))
                        nc.vector.tensor_tensor(lo_half(h), raw_half(h), hi_half(h).bitcast(F32),
                                                ALU.subtract).then_inc(*lo_done.more())
                cursor["half"] = max(cursor["half"], limit)

            def reach(key):
                split_to(split_limit(AT[(stage.kind, key)]))

            def low(dst, src, hi):
                return nc.vector.tensor_tensor(dst, src, hi.bitcast(F32), ALU.subtract)

            def gains(name, dst, n0, between=None):
                for i in range(DC // 2):
                    reach((name, i))
                    dve.wait_ge(*x_gained.at(n0 + i))
                    src = gain_tmp[:, i, :].rearrange("p (c w) -> p c w", w=T)
                    hi, lo = (part[:, 2 * i:2 * i + 2, :] for part in dst)
                    nc.vector.tensor_copy(hi, src).then_inc(*dve_step.more())
                    dve.wait_ge(*dve_step.last())
                    low(lo, src, hi).then_inc(*read((name, i)))
                    if between:
                        between(i)

            bn = nst[:, 64:112].rearrange("p (t b s) -> p t b s", t=2, b=4)

            def statistics(t, cb):
                return nc.vector.bn_stats(bn[:, t, cb, :], z3[:, t, cb * T:cb * T + T])

            def normalise(n):
                dve.wait_ge(*dve_step.last())
                nc.vector.memset(nst[:, 63:64], 0.0)
                for t in range(2):
                    ins = nc.vector.bn_aggr(nst[:, 48 + 2 * t:50 + 2 * t], bn[:, t, :, :])
                ins.then_inc(*var_ready.more())
                dve.wait_ge(*std_ready.at(n))
                nc.vector.reciprocal(nst[:, 54:56], nst[:, 52:54]).then_inc(*dve_step.more())
                dve.wait_ge(*dve_step.last())
                nc.vector.scalar_tensor_tensor(nst[:, 23:24], nst[:, 50:51], -1.0, nst[:, 55:56],
                                               ALU.mult, ALU.mult).then_inc(*norm_factors.more())
                nc.vector.tensor_scalar(z3[:, 0, :], z3[:, 0, :], nst[:, 48:49], nst[:, 54:55],
                                        ALU.subtract, ALU.mult).then_inc(*xhat0.more())

            def residual_norm(name, k, n):
                dve.wait_ge(*x_ready.at(k))
                for cb in range(4):
                    reach((name, cb))
                    dve.wait_ge(*when_full((name, cb)))
                    src = bank_of((name, cb))
                    at = slice(cb * T, cb * T + T)
                    nc.vector.scalar_tensor_tensor(z3[:, :, at], x3[:, :, at], ALPHA, halves(src),
                                                           ALU.mult, ALU.add).then_inc(*read((name, cb)))
                    dve.wait_ge(*when_read((name, cb)))
                    for t in range(2):
                        ins = statistics(t, cb)
                ins.then_inc(*dve_step.more())
                normalise(n)

            def residual_norm_down(k, n):
                dve.wait_ge(*x_ready.at(k))
                for t in range(2):
                    for c in range(2):
                        at = slice(c * 512, c * 512 + 512)
                        dve.wait_ge(*down_full.at(2 * t + c))
                        nc.vector.scalar_tensor_tensor(z3[:, t, at], x3[:, t, at], ALPHA, down[2 * t + c][:, :],
                                                       ALU.mult, ALU.add).then_inc(*dve_step.more())
                        dve.wait_ge(*dve_step.last())
                        for cb in (2 * c, 2 * c + 1):
                            ins = statistics(t, cb)
                ins.then_inc(*dve_step.more())
                normalise(n)

            def rope(n, rot, x_raw, cosine, sine, dst, sc_a, sc_b):
                reach(rot)
                dve.wait_ge(*when_full(rot))
                src = bank_of(rot)
                if n > 0:
                    dve.wait_ge(*rope_ready.at(n - 1))
                nc.vector.tensor_tensor(sc_a, x_raw, cosine, ALU.mult)
                nc.vector.tensor_tensor(sc_b, src[:, :], sine, ALU.mult).then_inc(*read(rot))
                dve.wait_ge(*when_read(rot))
                nc.vector.tensor_tensor(dst, sc_a, sc_b, ALU.add).then_inc(*rope_ready.more())

            def maxima(j):
                name, i = ORDER[stage.kind][j]
                number = NUM[stage.kind][0]
                reach(("scores", j))
                if name in ("na", "mla", "dil"):
                    need_exp_buffer(dve, j)
                for g in range(parts_of(name)):
                    n = number[(j, g)]
                    src = sc[n % 2]
                    e = e_ring[:, (j % 3) * 1152:(j % 3) * 1152 + 1152]
                    if name == "dil":
                        nc.vector.tensor_scalar(dbias[:, g % 2, :], distm[:, g, :], -float(SLOPES[g, i]), None,
                                                       ALU.mult).then_inc(*dve_step.more())
                        dve.wait_ge(*dve_step.last())
                    dve.wait_ge(*sc_full.at(n))
                    if name == "na":
                        for t in range(2):
                            j0 = 2 * (1 - t)
                            ins = nc.vector.scalar_tensor_tensor(
                                e[:, t * T:t * T + T], src[:, t * T:t * T + T], SCALE[name],
                                bias_tab[:, i, j0:j0 + 4, :].rearrange("p j k -> p (j k)"), ALU.mult, ALU.add)
                    elif name == "mla":
                        ins = nc.vector.scalar_tensor_tensor(e[:, 0:384], src[:, 0:384], SCALE[name],
                                                             const[:, CONST["causal"]:CONST["causal"] + 384],
                                                             ALU.mult, ALU.add)
                    elif name == "dil":
                        ins = nc.vector.scalar_tensor_tensor(e[:, g * 384:g * 384 + 384], src[:, 0:384], SCALE[name],
                                                             dbias[:, g % 2, :], ALU.mult, ALU.add)
                    if name in ("na", "mla", "dil"):
                        ins.then_inc(*sc_read.more())
                if name in ("na", "mla", "dil"):
                    dve.wait_ge(*sc_read.last())
                for t in range(2):
                    lo, hi = spans(name)[t]
                    view = exp_views(j, t) if name in ("na", "mla", "dil") else src[:, lo:hi]
                    ins = nc.vector.tensor_reduce(st("mx", j, t, t + 1), view, AX.XY if name == "dil" else AX.X,
                                                  ALU.max)
                ins.then_inc(*dve_step.more())
                dve.wait_ge(*dve_step.last())
                k = -1.0 if name in ("na", "mla", "dil") else -SCALE[name]
                nc.vector.tensor_scalar(st("nm", j), st("mx", j), k, None, ALU.mult).then_inc(*nmax.more())

            def normed(j):
                name, i = ORDER[stage.kind][j]
                dve.wait_ge(*exp_done.at(j))
                nc.vector.reciprocal(st("rec", j), st("sum", j)).then_inc(*dve_step.more())
                dve.wait_ge(*dve_step.last())
                if name == "da" and i % 2 == 0:
                    return
                if name == "da":
                    nc.vector.tensor_scalar(st("rec", j), st("rec", j), nst[:, 60:61], None,
                                            ALU.mult).then_inc(*dve_step.more())
                    dve.wait_ge(*dve_step.last())
                    for t in range(2):
                        ins = nc.vector.tensor_scalar(exp_views(j, t), exp_views(j, t), st("rec", j, t, t + 1), None,
                                                      ALU.mult)
                    ins.then_inc(*dve_step.more())
                    dve.wait_ge(*dve_step.last())
                    for t in range(2):
                        ins = nc.vector.scalar_tensor_tensor(exp_views(j, t), exp_views(j - 1, t),
                                                             st("rec", j - 1, t, t + 1), exp_views(j, t),
                                                             ALU.mult, ALU.add)
                else:
                    for t in range(2):
                        ins = nc.vector.tensor_scalar(exp_views(j, t), exp_views(j, t), st("rec", j, t, t + 1), None,
                                                      ALU.mult)
                ins.then_inc(*p_ready.more())

            def filler(key):
                kind, i = key
                if kind == "hc":
                    dve.wait_ge(*when_read(("gc", i)))
                    dve.wait_ge(*when_full(key))
                    src = bank_of(key)
                    nc.vector.tensor_tensor(cin[:, 2 * i:2 * i + 2, :], gc[:, 2 * i:2 * i + 2, :], halves(src),
                                                    ALU.mult).then_inc(*read(key))

            def attn_out(j):
                name, i = ORDER[stage.kind][j]
                if j not in NUM[stage.kind][2] or name in ("da", "dil"):
                    return
                reach(("values", j))
                dve.wait_ge(*out_hi.at(sum(ORDER[stage.kind][k][0] not in ("da", "dil") for k in NUM[stage.kind][2]
                                           if k < j)))
                dst, src = out_place(name, i)
                low(dst[1], src, dst[0]).then_inc(*po_read.more())

            def attention(name, fillers, extra={}):
                js = set_jobs(name)
                for step in range(len(js) + 2):
                    if 1 <= step <= len(js):
                        normed(js[step - 1])
                    if step < len(js):
                        maxima(js[step])
                    for key in fillers[step]:
                        reach(key)
                        filler(key)
                    if step >= 2:
                        attn_out(js[step - 2])
                    if step in extra:
                        extra[step]()

            def gated_conv(chunks):
                for c in chunks:
                    if c == 0:
                        dve.wait_ge(*x_ready.at(-1))
                        dve.wait_ge(*when_read(("hc", 1)))
                    if c % 2 == 0:
                        dve.wait_ge(*when_read(("gb", c // 2)))
                    src, dst = cin[:, c, :], conv_tmp[:, c, :]
                    w = [colp("sc_w", 3 * c + k) for k in range(3)]
                    nc.vector.tensor_scalar(dst, src, w[1], None, ALU.mult).then_inc(*dve_step.more())
                    dve.wait_ge(*dve_step.last())
                    nc.vector.scalar_tensor_tensor(dst[:, 1:T], src[:, 0:T - 1], w[0], dst[:, 1:T],
                                                   ALU.mult, ALU.add).then_inc(*dve_step.more())
                    dve.wait_ge(*dve_step.last())
                    nc.vector.scalar_tensor_tensor(dst[:, 0:T - 1], src[:, 1:T], w[2], dst[:, 0:T - 1],
                                                   ALU.mult, ALU.add).then_inc(*dve_step.more())
                    dve.wait_ge(*dve_step.last())
                    nc.vector.tensor_tensor(dst, dst, gb[:, c, :], ALU.mult).then_inc(*dve_step.more())
                    dve.wait_ge(*dve_step.last())
                    nc.vector.tensor_copy(YC[0][:, c, :], dst).then_inc(*dve_step.more())
                    dve.wait_ge(*dve_step.last())
                    low(YC[1][:, c, :], dst, YC[0][:, c, :]).then_inc(*yc_ready.more())

            def ya_norm(c):
                y = yT3[:, 8 + c, :]
                dve.wait_ge(*when_read(("ss", c // 2)))
                nc.vector.reciprocal(ya_rms[:, c, :], ya_rms[:, c, :]).then_inc(*dve_step.more())
                dve.wait_ge(*dve_step.last())
                nc.vector.scalar_tensor_tensor(y, y, nst[:, 61:62], ya_rms[:, c, :],
                                               ALU.mult, ALU.mult).then_inc(*dve_step.more())
                dve.wait_ge(*dve_step.last())
                nc.vector.tensor_copy(YA[0][:, c, :], y).then_inc(*dve_step.more())
                dve.wait_ge(*dve_step.last())
                low(YA[1][:, c, :], y, YA[0][:, c, :]).then_inc(*ya_ready.more())

            def ya_split():
                dve.wait_ge(*ya_hi_ready.at(0))
                low(YA[1], yT3[:, 8:12, :], YA[0]).then_inc(*ya_lo_ready.more())

            def merge():
                for cb in range(4):
                    for br in range(3):
                        reach(("branch", cb, br))
                        dve.wait_ge(*when_full(("branch", cb, br)))
                        src = bank_of(("branch", cb, br))
                        gate = big3[:, 8 * br + 2 * cb:8 * br + 2 * cb + 2, :]
                        acc, tmp = (merge_tmp[:, k, :].rearrange("p (c w) -> p c w", w=T)
                                    for k in (cb % 2, 2 + br % 2))
                        if br == 0:
                            nc.vector.tensor_tensor(acc, gate, halves(src),
                                                    ALU.mult).then_inc(*read(("branch", cb, br)))
                            continue
                        nc.vector.tensor_tensor(tmp, gate, halves(src), ALU.mult).then_inc(*read(("branch", cb, br)))
                        dve.wait_ge(*when_read(("branch", cb, br)))
                        nc.vector.tensor_tensor(acc, acc, tmp, ALU.add).then_inc(*merge_step.more())
                        dve.wait_ge(*merge_step.last())
                    at = slice(2 * cb, 2 * cb + 2)
                    nc.vector.tensor_copy(MG[0][:, at, :], acc).then_inc(*merge_step.more())
                    dve.wait_ge(*merge_step.last())
                    low(MG[1][:, at, :], acc, MG[0][:, at, :]).then_inc(*merged_ready.more())
                    dve.wait_ge(*merged_ready.at(cb))

            def ffn(gates_too, packed, w):
                def outer_taps(i, k, which):
                    reach((which, i))
                    dve.wait_ge(*conv_init.at(2 * i + k if gates_too else i))
                    src = bank_of((which, i))
                    for turn in range(2):
                        for c in range(2):
                            ch = (k * FC if gates_too else 0) + 2 * i + c
                            s, d = src[:, c * T:c * T + T], cbuf(i % 2, k)[:, c * T:c * T + T]
                            if gates_too:
                                shift, tap = turn + 1, 1 - turn
                                s, d = s[:, 0:T - shift], d[:, shift:T]
                            else:
                                s, d, tap = ((s[:, 0:T - 1], d[:, 1:T], 0), (s[:, 1:T], d[:, 0:T - 1], 2))[turn]
                            ins = nc.vector.scalar_tensor_tensor(d, s, colp(w, 3 * ch + tap, packed), d,
                                                                 ALU.mult, ALU.add)
                        if turn == 0:
                            ins.then_inc(*dve_step.more())
                            dve.wait_ge(*dve_step.last())
                    ins.then_inc(*read((which, i)))

                def product(i):
                    prod = sbuf(i)
                    dve.wait_ge(*silu_done.at(i))
                    if gates_too:
                        dve.wait_ge(*when_read(("up", i)))
                        nc.vector.tensor_tensor(prod, prod, cbuf(i % 2, 1), ALU.mult).then_inc(*dve_step.more())
                        dve.wait_ge(*dve_step.last())
                    else:
                        dve.wait_ge(*when_full(("up", i)))
                        src = bank_of(("up", i))
                        nc.vector.tensor_tensor(prod, prod, src[:, :], ALU.mult).then_inc(*read(("up", i)))
                        dve.wait_ge(*when_read(("up", i)))
                    prod = prod.rearrange("p (c w) -> p c w", w=T)
                    hi, lo = (part[:, 2 * (i % 2):2 * (i % 2) + 2, :] for part in YA)
                    if i >= 2:
                        user, n = LAST_USE[(stage.kind, DOWN_HALF[(stage.kind, i - 2)])]
                        dve.wait_ge(*user.at(n))
                    nc.vector.tensor_copy(hi, prod).then_inc(*dve_step.more())
                    dve.wait_ge(*dve_step.last())
                    low(lo, prod, hi).then_inc(*act_ready.more())

                for i in range(FPAIR + 1):
                    if i < FPAIR:
                        outer_taps(i, 0, "gt")
                    if i == FPAIR and not gates_too:
                        reach(("up", i - 1))
                    if i >= 1:
                        product(i - 1)
                    if i < FPAIR and gates_too:
                        outer_taps(i, 1, "up")

            def inverse_std(n, n0):
                dve.wait_ge(*std_ready.at(n))
                nc.vector.reciprocal(nst[:, n0 + 16:n0 + 18], nst[:, n0 + 8:n0 + 10]).then_inc(*norm_factors.more())
                dve.wait_ge(*norm_factors.last())

            def add_normed(t, factor, gain_rows, done):
                dve.wait_ge(*rows_in.at(gain_rows))
                nc.vector.scalar_tensor_tensor(z3[:, t, :], z3[:, t, :], factor, rows[:, 0:D],
                                               ALU.mult, ALU.mult).then_inc(*dve_step.more())
                dve.wait_ge(*dve_step.last())
                nc.vector.tensor_tensor(x3[:, t, :], x3[:, t, :], z3[:, t, :], ALU.add).then_inc(*done.more())

            stage.enter("pro")
            dve.wait_ge(*xin.at(0))
            for t in range(2):
                for cb in range(4):
                    ins = statistics(t, cb)
            ins.then_inc(*dve_step.more())
            normalise(0)
            for i in (1, 3):
                dve.wait_ge(*when_full(("memT", i)))
                nc.vector.tensor_copy(memT3[:, 2 * i:2 * i + 2, :],
                                      halves(bank_of(("memT", i)))).then_inc(*read(("memT", i)))

            def first_split(h):
                dve.wait_ge(*hi_done.at(h))
                low(lo_half(h), raw_half(h), hi_half(h)).then_inc(*lo_done.more())

            first_split(0)
            gains("xT0", XT, 0, lambda i: first_split(i) if i else None)

            with dve.Fori(0, DEPTH) as l:
                stage.enter("layer", l)
                cursor["half"] = SPLIT
                dve.wait_ge(*cols_in.at(-1))
                dve.wait_ge(*tables_in.at(-1))
                lam = col[:, COL1["lam"]:COL1["lam"] + 256].rearrange("p (a b w) -> p a b w", a=2, b=2)
                prod = e_ring[:, 0:128].rearrange("p (a w) -> p a w", a=2)
                nc.vector.tensor_tensor(prod, lam[:, :, 0, :], lam[:, :, 1, :], ALU.mult).then_inc(*dve_step.more())
                dve.wait_ge(*dve_step.last())
                nc.vector.tensor_reduce(nst[:, 56:58], prod, AX.X, ALU.add).then_inc(*lam_sum.more())
                nc.vector.tensor_tensor(nst[:, 61:62], colp("subln"), colp("one_minus"), ALU.mult)
                for n in range(4):
                    dst = (qa, ka)[n // 2][:, 2 * (n % 2):2 * (n % 2) + 2, :].rearrange("p c w -> p (c w)")
                    x_raw = raw[:, 2 * n:2 * n + 2, :].rearrange("p c w -> p (c w)")
                    rope(n, ("rot", n), x_raw, cos2, sin2, dst, scratch[:, 0, :], scratch[:, 1, :])
                dve.wait_ge(*lam_exp.at(0))
                nc.vector.tensor_tensor(nst[:, 62:63], nst[:, 59:60], nst[:, 58:59],
                                        ALU.subtract).then_inc(*dve_step.more())
                dve.wait_ge(*dve_step.last())
                nc.vector.tensor_tensor(nst[:, 60:61], nst[:, 62:63], colp("lam_init"),
                                        ALU.subtract).then_inc(*dve_step.more())
                dve.wait_ge(*dve_step.last())
                attention("da", da_fillers, {4: lambda: gated_conv((0,)), 6: lambda: gated_conv((1, 2)),
                                             8: lambda: gated_conv((3,))})
                dve.wait_ge(*bias_ready.at(0))
                attention("na", na_fillers, {2: lambda: ya_norm(0), 3: lambda: ya_norm(1),
                                             4: lambda: ya_norm(2), 5: lambda: ya_norm(3)})
                merge()
                for k in range(2):
                    dve.wait_ge(*mem_hi.at(k))
                    low(MT[1][:, 4 * k:4 * k + 4, :], memT3[:, 4 * k:4 * k + 4, :],
                        MT[0][:, 4 * k:4 * k + 4, :]).then_inc(*mem_lo.more())
                residual_norm("mix", -1, 0)
                gains("ln0", XT, 0)
                attention("xa", xa_fillers)
                residual_norm("xo", 0, 1)
                gains("ln1", XT, 4)
                ffn(False, COL1, "ffn_w")
                split_to(in_phase())
                residual_norm_down(1, 2)
                split_to(PERIOD + 1)
                gains("ln2", XT, 8, lambda i: split_to(PERIOD + 1 + i))

            stage.enter("post")
            cursor["half"] = SPLIT
            dve.wait_ge(*x_ready.at(-1))
            inverse_std(0, 0)
            nc.vector.tensor_scalar(z3[:, 0, :], x3[:, 0, :], nst[:, 16:17], None, ALU.mult).then_inc(*xhat0.more())
            dve.wait_ge(*cols_in.at(-1))
            gains("premix", XT, 0)
            inverse_std(1, 2)
            nc.vector.tensor_scalar(mem2[:, 0, :], mem2[:, 0, :], nst[:, 18:19], None, ALU.mult).then_inc(*xhat0.more())
            reach(("c", 1))
            dve.wait_ge(*pos_in.at(0))
            ang, trn, red = turns[64:96, :], half_sine[64:96, :], angle[64:96, :]
            nc.vector.tensor_copy(ang, pos_int[64:96, :]).then_inc(*dve_step.more())
            dve.wait_ge(*dve_step.last())
            nc.vector.tensor_scalar(ang, ang, const[64:96, CONST["inv"]:CONST["inv"] + 1], None,
                                    ALU.mult).then_inc(*dve_step.more())
            dve.wait_ge(*dve_step.last())
            nc.vector.tensor_scalar(trn, ang, 1.0 / (2 * np.pi), ROUND, ALU.mult, ALU.add).then_inc(*dve_step.more())
            dve.wait_ge(*dve_step.last())
            nc.vector.tensor_scalar(trn, trn, ROUND, None, ALU.subtract).then_inc(*dve_step.more())
            dve.wait_ge(*dve_step.last())
            nc.vector.scalar_tensor_tensor(red, trn, -TWO_PI[0], ang, ALU.mult, ALU.add).then_inc(*dve_step.more())
            dve.wait_ge(*dve_step.last())
            nc.vector.scalar_tensor_tensor(red, trn, -TWO_PI[1], red, ALU.mult, ALU.add).then_inc(*dve_step.more())
            dve.wait_ge(*dve_step.last())
            nc.vector.scalar_tensor_tensor(red, trn, -TWO_PI[2], red, ALU.mult, ALU.add).then_inc(*dve_step.more())
            dve.wait_ge(*dve_step.last())
            nc.vector.tensor_scalar(red, red, PI_BELOW, -PI_BELOW, ALU.min, ALU.max).then_inc(*angle_ready.more())
            reach(("c", 2))
            gains("mem2T", MT, 4)
            for n, (lo, w) in enumerate(((0, 384), (384, 256))):
                inverse_std(2 + n, 4 + 2 * n)
                ins = nc.vector.tensor_scalar(cz[:, 0, lo:lo + w], cz[:, 0, lo:lo + w],
                                              nst[:, 20 + 2 * n:21 + 2 * n], None, ALU.mult)
            ins.then_inc(*xhat0.more())
            for i in range(3):
                reach(("cT", i))
                dve.wait_ge(*cT_hi.at(i))
                src = bank_of(("cT", i))
                for c in range(2 if i < 2 else 1):
                    k = 2 * i + c
                    g = colp("q_norm", k, COL2) if k < 3 else colp("kv_norm", k - 3, COL2)
                    ins = nc.vector.scalar_tensor_tensor(XO[1][:, k, :], src[:, c * T:c * T + T], g,
                                                         XO[0][:, k, :].bitcast(F32), ALU.mult, ALU.subtract)
                ins.then_inc(*read(("cT", i)))
            dve.wait_ge(*sin_ready.at(0))
            nc.vector.tensor_tensor(turns[64:96, :], half_sine[64:96, :], half_sine[64:96, :],
                                    ALU.mult).then_inc(*dve_step.more())
            dve.wait_ge(*dve_step.last())
            for c in range(2):
                ins = nc.vector.tensor_scalar(cos2[64:96, c * T:c * T + T], turns[64:96, :], -2.0, 1.0,
                                              ALU.mult, ALU.add)
            ins.then_inc(*dve_step.more())
            dve.wait_ge(*dve_step.last())
            for n in range(4):
                part = qm[64:96, 2 * n:2 * n + 2, :].rearrange("p c w -> p (c w)")
                src_key = ("rot2", n)
                reach(src_key)
                dve.wait_ge(*when_full(src_key))
                src = bank_of(src_key)
                if n > 0:
                    dve.wait_ge(*rope_ready.at(n - 1))
                nc.vector.tensor_tensor(scratch[64:96, 0, :], part, cos2[64:96, :], ALU.mult)
                nc.vector.tensor_tensor(scratch[64:96, 1, :], src[64:96, :], sin2[64:96, :],
                                        ALU.mult).then_inc(*read(src_key))
                dve.wait_ge(*when_read(src_key))
                nc.vector.tensor_tensor(part, scratch[64:96, 0, :], scratch[64:96, 1, :],
                                        ALU.add).then_inc(*rope_ready.more())
            reach(("rot2", 4))
            dve.wait_ge(*when_full(("rot2", 4)))
            src = bank_of(("rot2", 4))
            dve.wait_ge(*rope_ready.at(3))
            nc.vector.tensor_tensor(scratch[64:96, 0, 0:T], kraw[64:96, :], cos2[64:96, 0:T], ALU.mult)
            nc.vector.tensor_tensor(scratch[64:96, 1, 0:T], src[64:96, 0:T], sin2[64:96, 0:T],
                                    ALU.mult).then_inc(*read(("rot2", 4)))
            dve.wait_ge(*when_read(("rot2", 4)))
            nc.vector.tensor_tensor(km[64:96, :, :], scratch[64:96, 0:1, 0:T].to_broadcast([32, 8, T]),
                                        scratch[64:96, 1:2, 0:T].to_broadcast([32, 8, T]), ALU.add).then_inc(*rope_ready.more())
            attention("mla", mla_fillers)
            dve.wait_ge(*dil_in.at(0))
            attention("dil", dil_fillers)
            attention("mem", mem_fillers, {1: ya_split})
            merge()
            for cb in range(4):
                reach(("wo", cb))
                dve.wait_ge(*when_read(("wo", cb)))
            dve.wait_ge(*squares_done.at(4))
            nc.vector.tensor_reduce(nst[:, 0:2], block_sums, AX.X, ALU.add).then_inc(*square_sums.more())
            dve.wait_ge(*std_ready.at(4))
            nc.vector.reciprocal(nst[:, 16:18], nst[:, 8:10]).then_inc(*dve_step.more())
            dve.wait_ge(*dve_step.last())
            add_normed(0, nst[:, 16:17], 0, z_tile0)
            add_normed(1, nst[:, 17:18], 0, z_ready)
            dve.wait_ge(*z_tile0.at(0))
            inverse_std(5, 2)
            nc.vector.tensor_scalar(z3[:, 0, :], x3[:, 0, :], nst[:, 18:19], None, ALU.mult).then_inc(*xhat0.more())
            gains("preffn", XT, 8)
            ffn(True, COL2, "conv_w")
            split_to(in_phase())
            for t in range(2):
                dve.wait_ge(*std_ready.at(6 + t))
                nc.vector.reciprocal(nst[:, 20 + t:21 + t], nst[:, 12 + t:13 + t]).then_inc(*dve_step.more())
                dve.wait_ge(*dve_step.last())
                add_normed(t, nst[:, 20 + t:21 + t], 1, out_ready)

        @block.gpsimd
        def _(pool):
            def load_rows(k, first=True):
                src = bass.AP(a["ln_rows"].tensor, k * (2 * D), [[0, P], [1, 2 * D]])
                pool.dma_start(rows[:, :], src).then_inc(*rows_in.more())

            def next_x(norm, rows_n, n):
                pool.wait_ge(*rows_in.at(rows_n))
                for t in range(2):
                    pool.wait_ge(*(xhat0, xhat1)[t].at(norm))
                    nc.gpsimd.tensor_tensor(x3[:, t, :], z3[:, t, :], rows[:, 0:D],
                                            ALU.mult).then_inc(*pool_step.more())
                    pool.wait_ge(*pool_step.last())
                    nc.gpsimd.tensor_tensor(x3[:, t, :], x3[:, t, :], rows[:, D:2 * D],
                                            ALU.add).then_inc(*(x_tile0, x_ready)[t].more())
                pool.wait_ge(*x_ready.at(n))

            stage.enter("pro")
            load_rows(0)
            pool.dma_start(col[:, :], a["cols"][0]).then_inc(*cols_in.more())
            next_x(0, 0, 0)
            for l in range(DEPTH):
                for h in range(RPB_H):
                    for s in range(2):
                        src = bass.AP(a["rpb"].tensor,
                                      ((l * RPB_H + h) * RPB_R + NJ - 1 - s) * RPB_C + RPB_C // 2,
                                      [[RPB_C, NJ], [-1, 64], [1, 64]])
                        dst = a["bias_scratch"][l, 64 * s:64 * s + 64, h * NJ * 64:(h + 1) * NJ * 64]
                        pool.dma_start(dst.rearrange("p (j k) -> j p k", j=NJ), src).then_inc(*bias_built.more())

            with pool.Fori(0, DEPTH) as l:
                stage.enter("layer", l)
                need_last_phase(pool)
                pool.wait_ge(*bias_built.at(-1))
                pool.dma_start(area[:, 36 * T:48 * T], a["bias_scratch"][l]).then_inc(*bias_in.more())
                pool.wait_ge(*bias_in.at(0))
                table = area[:, 36 * T:48 * T].rearrange("p (a k) -> p a k", k=64)
                pool.wait_ge(*tables_in.at(-1))
                mask = const[:, CONST["na_mask"]:CONST["na_mask"] + 64].unsqueeze(1).to_broadcast([P, 8 * NJ, 64])
                nc.gpsimd.tensor_tensor(table, table, mask, ALU.add).then_inc(*bias_ready.more())
                for k in range(3):
                    if k == 0:
                        pool.wait_ge(*sc_read.at(READS[("layer", 15, 0)]))
                    load_rows(1 + k + 3 * l)
                    next_x(k, k, k)
                pool.wait_ge(*x_gained.at(11))
                pool.dma_start(col[:, :], a["cols"][l + 1]).then_inc(*cols_in.more())

            stage.enter("post")
            need_last_phase(pool)
            pool.dma_start(mem2, a["mem_2"].rearrange("b (t p) d -> p (b t) d", p=P)).then_inc(*mem2_in.more())
            pos = bass.AP(a["positions_2"].tensor, 0, [[0, 32], [1, T]])
            pool.dma_start(pos_int[64:96, :], pos).then_inc(*pos_in.more())
            pool.wait_ge(*nmax.at(7))
            pool.dma_start(z_tok[:, 0:3 * 384], a["distm"]).then_inc(*dil_in.more())
            pool.wait_ge(*nmax.at(11))
            load_rows(7)
            pool.wait_ge(*z_ready.at(0))
            load_rows(8)

        @block.sync
        def _(sp):
            def load_half(row, h):
                sp.dma_start(raw_half(h), a["stream"][row]).then_inc(*landed[h % RAW].more())

            stage.enter("pro")
            sp.dma_start(z3, a["x"].rearrange("b (t p) d -> p (b t) d", p=P)).then_inc(*xin.more())
            sp.dma_start(const[:, 0:CONST_FIRST], a["const"][:, 0:CONST_FIRST]).then_inc(*const_in.more())
            sp.dma_start(mem_tok, a["mem"].rearrange("b (t p) d -> p (b t) d", p=P)).then_inc(*memin.more())
            for h in range(RAW):
                load_half(h, h)
            sp.dma_start(const[:, CONST_FIRST:CONST_N], a["const"][:, CONST_FIRST:CONST_N]).then_inc(*tables_in.more())

            def stream(total, first):
                for h in range(RAW, total):
                    if is_half(h):
                        if is_half(h - RAW):
                            sp.wait_ge(*lo_done.at(split_index(h - RAW)))
                        load_half(first + h, h)

            with sp.Fori(0, DEPTH) as l:
                stage.enter("layer", l)
                stream(PERIOD + RAW, l * PERIOD)
            stage.enter("post")
            stream(HALVES_2, DEPTH * PERIOD)
            for t in range(2):
                sp.wait_ge(*out_ready.at(t))
                sp.dma_start(out[0, t * P:t * P + P, :], x3[:, t, :]).then_inc(*out_done.more())
            sp.wait_ge(*out_done.at(1))

    counted = {k: tuple(v) for k, v in stage.seen.items()}
    assert counted == COUNTS, counted
    return stage


def tiles_of(w):
    k, n = w.shape
    if n % TILE_N:
        w = np.concatenate([w, np.zeros((k, TILE_N - n % TILE_N), w.dtype)], 1)
    return w.reshape(k // P, P, -1, TILE_N).transpose(2, 0, 1, 3).reshape(-1, P, TILE_N)


def halves_of(tiles, halves):
    t = np.concatenate(tiles)
    t = np.concatenate([t, np.zeros((halves * HALF_TILES - len(t), P, TILE_N), t.dtype)])
    return t.reshape(halves, HALF_TILES, P, TILE_N).transpose(0, 2, 1, 3).reshape(halves, P, HALF_N)


def stream_of(i):
    out = []
    for l in range(DEPTH):
        w = i["w_in"][l]
        cuts = {n: w[:, 512 * k:512 * k + 512]
                for k, n in enumerate(("qa", "ka", "va", "qn", "kn", "vn", "gb", "gc", "hc"))}
        t = [tiles_of(cuts[n]) for n in ("qa", "ka", "va", "qn", "gc", "hc", "gb", "kn", "vn")]
        t.append(tiles_of(w[:, 4608:]))
        t += branch_tiles(i["w_branch"][l])
        kv = i["xa_kv"][l]
        t += [tiles_of(i["w_mix_out"][l]), tiles_of(kv[:, :D]), tiles_of(i["xa_q"][l]), tiles_of(kv[:, D:]),
              tiles_of(i["xa_o"][l])]
        t += ffn_tiles(i["ffn_w_in"][l], i["ffn_w_out"][l], True)
        out.append(halves_of(t, PERIOD))
    w = i["w_in_2"][0]
    uq = i["w_uq_2"][0].reshape(384, 4, 192)
    uq = np.concatenate([uq, np.zeros((384, 4, 64), uq.dtype)], 2).reshape(384, 1024)
    ukv = i["w_ukv_2"][0].reshape(256, 8, 128)
    gates = tiles_of(w[:, 5792:])
    dq, dk, dv = (tiles_of(w[:, 672 + 1536 * k:672 + 1536 * (k + 1)]) for k in range(3))
    dv = dv.reshape(3, 2, DC, P, TILE_N).transpose(1, 0, 2, 3, 4).reshape(-1, P, TILE_N)
    mem_kv = tiles_of(i["w_mem_kv_2"][0])
    t = [tiles_of(w[:, 0:672]), tiles_of(w[:, 5280:5792]), mem_kv[:DC], tiles_of(uq),
         tiles_of(ukv[:, :, :64].reshape(256, 512)), tiles_of(ukv[:, :, 64:].reshape(256, 512)),
         mem_kv[DC:], gates[:4 * DC], dq, dk, dv, gates[4 * DC:]]
    t += branch_tiles(np.stack([i["w_br_mla_2"][0], i["w_br_dil_2"][0], i["w_br_mem_2"][0]]))
    t.append(tiles_of(i["w_o_2"][0]))
    t += ffn_tiles(i["w_ffn_up_2"][0], i["w_ffn_down_2"][0], False)
    out.append(halves_of(t, HALVES_2))
    return np.concatenate(out)


def branch_tiles(w):
    parts = [tiles_of(x).reshape(4, 4, P, TILE_N) for x in w]
    return [parts[br][cb] for cb in range(4) for br in range(3)]


def ffn_tiles(w_in, w_out, gate_last):
    a, b = tiles_of(w_in[:, :FF]), tiles_of(w_in[:, FF:])
    gate, value = (b, a) if gate_last else (a, b)
    gate, value = gate.reshape(FPAIR, DC, P, TILE_N), value.reshape(FPAIR, DC, P, TILE_N)
    down = w_out.reshape(FC, P, D // TILE_N, TILE_N).transpose(0, 2, 1, 3).reshape(FPAIR, -1, P, TILE_N)
    out = []
    for k in range(FPAIR):
        out += [gate[k], value[k]] + ([down[k - 1]] if k else [])
    return out + [down[FPAIR - 1]]


def chunked(v):
    return v.reshape(-1, P).T


def cols_of(i):
    pages = np.zeros((DEPTH + 1, P, COL_N), np.float32)

    def put(page, at, name, value):
        pages[page, :, at[name]:at[name] + value.shape[1]] = value

    def taps(w):
        return w.reshape(3, -1, P).transpose(2, 1, 0).reshape(P, -1)

    for l in range(DEPTH):
        lam_init = 0.8 - 0.6 * float(np.exp(-0.3 * l))
        put(l, COL1, "ln_g", chunked(i["ln_g"][l].reshape(-1)))
        put(l, COL1, "ln_b", chunked(i["ln_b"][l].reshape(-1)))
        put(l, COL1, "subln", chunked(i["subln_g"][l]))
        put(l, COL1, "one_minus", np.full((P, 1), 1.0 - lam_init, np.float32))
        put(l, COL1, "lam_init", np.full((P, 1), lam_init, np.float32))
        put(l, COL1, "sc_w", taps(i["sc_conv_w"][l]))
        put(l, COL1, "ffn_w", taps(i["ffn_conv_w"][l]))
        put(l, COL1, "ffn_b", chunked(i["ffn_conv_b"][l]))
        lam = np.concatenate([i["lam_q1"][l], i["lam_k1"][l], i["lam_q2"][l], i["lam_k2"][l]])
        put(l, COL1, "lam", np.broadcast_to(lam, (P, 256)))
    for name, key in (("g_mem", "g_mem_2"), ("g_pre_mix", "g_pre_mix_2"), ("q_norm", "mla_q_norm_2"),
                      ("kv_norm", "mla_kv_norm_2"), ("b_gate", "b_gate_2"), ("g_pre_ffn", "g_pre_ffn_2"),
                      ("conv_b", "conv_b_2")):
        put(DEPTH, COL2, name, chunked(i[key][0]))
    put(DEPTH, COL2, "conv_w", taps(i["conv_w_2"][0]))
    return pages


def const_of(i):
    c = np.zeros((P, CONST_N), np.float32)

    def put(name, value):
        c[:value.shape[0], CONST[name]:CONST[name] + value.shape[1]] = value

    put("ident", np.eye(P))
    half = 32
    rot = np.zeros((P, P))
    for m in range(0, P, 64):
        for d in range(half):
            rot[m + d + half, m + d] = -1
            rot[m + d, m + d + half] = 1
    put("rot1", rot)
    inv = np.float32(10000.0) ** (-np.arange(half, dtype=np.float32) * np.float32(2.0) / np.float32(64))
    ang = (np.arange(T, dtype=np.float32)[None, :] * inv.astype(np.float32)[:, None]).astype(np.float32)
    put("cos", np.tile(np.cos(ang.astype(np.float64)), (4, 2)))
    put("sin", np.tile(np.sin(ang.astype(np.float64)), (4, 2)))
    put("ones", np.ones((P, P)))
    q, k = np.arange(P)[:, None] % 64, np.arange(64)[None, :]
    start = np.clip(q - 8, 0, 48)
    put("na_mask", np.where((k >= start) & (k < start + 16), 0.0, NEG))
    qi, ki = np.arange(P)[:, None], np.arange(P)[None, :]
    diag = np.where(ki <= qi, 0.0, NEG)
    put("causal", np.concatenate([diag, np.zeros((P, P)), diag], 1))
    rot = np.zeros((P, 96))
    for d in range(16):
        rot[64 + d + 16, 64 + d] = -1
        rot[64 + d, 64 + d + 16] = 1
    put("rot2", rot)
    inv2 = np.float32(10000.0) ** (-np.arange(16, dtype=np.float32) / np.float32(16))
    put("inv", np.tile(inv2, 8)[:, None])
    put("eps_ln", np.full((P, 1), EPS_LN))
    put("eps_rms", np.full((P, 1), EPS_RMS))
    put("emb_g", chunked(i["emb_ln_g"]))
    put("emb_b", chunked(i["emb_ln_b"]))
    return c


def distances():
    out = []
    for window, d in ((128, 1), (512, 4), (2048, 16)):
        for q0, n in ((0, P), (P, T)):
            dist = (q0 + np.arange(P))[:, None] - np.arange(n)[None, :]
            ok = (dist >= 0) & (dist % d == 0) & (dist <= window)
            out.append(np.where(ok, dist, 1e33))
    return np.concatenate(out, 1).astype(np.float32)


def kernel(**inputs):
    import concourse.bacc as _bacc
    from concourse.bass_utils import run_bass_kernel_spmd as _run

    i = {k: np.ascontiguousarray(v) for k, v in inputs.items()}
    zero = np.zeros(D, np.float32)
    rows = np.concatenate([i["emb_ln_g"], i["emb_ln_b"]]
                          + [x for l in range(DEPTH) for k in range(3) for x in (i["ln_g"][l, k], i["ln_b"][l, k])]
                          + [i["g_post_mix_2"][0], zero, i["g_post_ffn_2"][0], zero])
    arrays = {"x": i["x"], "mem": i["mem"], "mem_2": i["mem_2"], "positions_2": i["positions_2"],
              "rpb": i["rpb"].reshape(-1), "stream": stream_of(i), "cols": cols_of(i), "const": const_of(i),
              "distm": distances(), "ln_rows": rows}
    nc = _bacc.Bacc("TRN2", target_bir_lowering=False, num_devices=1)
    aps = {n: nc.dram_tensor(f"in_{n}", v.shape, mybir.dt.from_np(v.dtype), kind="ExternalInput").ap()
           for n, v in arrays.items()}
    aps["bias_scratch"] = nc.dram_tensor("bias_scratch", (DEPTH, P, RPB_H * NJ * 64), F32, kind="Internal").ap()
    out = nc.dram_tensor("out_x", (1, T, D), F32, kind="ExternalOutput").ap()
    build(nc, aps, out)
    r = _run(nc, [{f"in_{n}": v for n, v in arrays.items()}], core_ids=[0])
    return r.results[0]["out_x"]
```
